# Optimizing a Trainium2 kernel written in Bass

```python
import jax, jax.numpy as jnp
from jax import lax
import numpy as np

D_MODEL = 1024
BATCH = 1
SEQ = 512
DEPTH = 1

RW_HEADS = 16
RW_HEAD_DIM = 64
RW_WIDTH = RW_HEADS * RW_HEAD_DIM
LORA_DECAY = 64
LORA_AAA = 64
LORA_VRES = 32
LORA_GATE = 160
CONV_WIDTH = 1024
CONV_K = 3
MEM_LEN = 256
MEM_HEADS = 4
MEM_HEAD_DIM = D_MODEL // MEM_HEADS
N_GROUPS = 4
EXPERTS_PER_GROUP = 4
N_EXPERTS = N_GROUPS * EXPERTS_PER_GROUP
TOP_K_IN_GROUP = 2
D_EXPERT = 512

RMS_EPS = 1e-6
LNX_EPS = 64e-5
L2_EPS = 1e-12

RW_COLS = 3 * RW_WIDTH + LORA_DECAY + LORA_AAA + LORA_GATE
CONV_COLS = 3 * CONV_WIDTH
GATE_COLS = 2 * D_MODEL
IN_COLS = RW_COLS + CONV_COLS + GATE_COLS

kernel_name = "hybrid_rwkv7_shortconv_memxattn_hmoe"

def rms_norm(x, g):
    xf = x.astype(jnp.float32)
    y = xf * lax.rsqrt(jnp.mean(xf * xf, axis=-1, keepdims=True) + RMS_EPS)
    return (y * g.astype(jnp.float32)).astype(x.dtype)

def token_shift(z):
    return jnp.pad(z, ((0, 0), (1, 0), (0, 0)))[:, :-1]

def shift_mix(z, mu):
    return z + (token_shift(z) - z) * mu

def wkv7_scan(r, w, k, v, a, b):
    bsz, _, h, n = r.shape
    seqs = tuple(jnp.moveaxis(t, 1, 0) for t in (r, w, k, v, a, b))

    def step(S, inp):
        r_t, w_t, k_t, v_t, a_t, b_t = inp
        sa = jnp.einsum('bhvk,bhk->bhv', S, a_t)
        S = (S * w_t[:, :, None, :] + sa[..., None] * b_t[:, :, None, :]
             + v_t[..., None] * k_t[:, :, None, :])
        y = jnp.einsum('bhvk,bhk->bhv', S, r_t)
        return S, y

    S0 = jnp.zeros((bsz, h, n, n), jnp.float32)
    _, ys = lax.scan(step, S0, seqs)
    return jnp.moveaxis(ys, 0, 1)

def causal_dwconv(u, w):
    seq = u.shape[1]
    up = jnp.pad(u, ((0, 0), (CONV_K - 1, 0), (0, 0)))
    y = w[0] * up[:, 0:seq]
    for j in range(1, CONV_K):
        y = y + w[j] * up[:, j:j + seq]
    return y

def mem_cross_attn(h, mem, gq, gkv, wq, wkv, wo):
    bsz, seq, _ = h.shape
    hn = rms_norm(h, gq)
    mn = rms_norm(mem, gkv)
    q = (hn @ wq).reshape(bsz, seq, MEM_HEADS, MEM_HEAD_DIM)
    k, v = jnp.split(mn @ wkv, 2, axis=-1)
    k = k.reshape(bsz, -1, MEM_HEADS, MEM_HEAD_DIM)
    v = v.reshape(bsz, -1, MEM_HEADS, MEM_HEAD_DIM)
    s = jnp.einsum('bqhd,bmhd->bhqm', q, k).astype(jnp.float32) * (MEM_HEAD_DIM ** -0.5)
    p = jax.nn.softmax(s, axis=-1).astype(v.dtype)
    o = jnp.einsum('bhqm,bmhd->bqhd', p, v).reshape(bsz, seq, MEM_HEADS * MEM_HEAD_DIM)
    return o @ wo

def hier_moe(h, rg, rgb, re, reb, wg, wu, wd):
    bsz, seq, d = h.shape
    n = h.reshape(bsz * seq, d)
    gp = jax.nn.softmax((n @ rg + rgb).astype(jnp.float32), axis=-1)
    g_w, g_i = lax.top_k(gp, 1)
    el = (n @ re + reb).astype(jnp.float32).reshape(-1, N_GROUPS, EXPERTS_PER_GROUP)
    el_sel = jnp.sum(el * jax.nn.one_hot(g_i[:, 0], N_GROUPS, dtype=jnp.float32)[:, :, None], axis=1)
    ep = jax.nn.softmax(el_sel, axis=-1)
    e_p, e_i = lax.top_k(ep, TOP_K_IN_GROUP)
    e_p = e_p / jnp.sum(e_p, axis=-1, keepdims=True)
    comb_w = g_w * e_p
    e_glob = g_i * EXPERTS_PER_GROUP + e_i
    combine = jnp.einsum('nk,nke->ne', comb_w,
                         jax.nn.one_hot(e_glob, N_EXPERTS, dtype=jnp.float32)).astype(n.dtype)
    out = jnp.zeros_like(n)
    for e in range(N_EXPERTS):
        he = jax.nn.silu(n @ wg[e]) * (n @ wu[e])
        out = out + combine[:, e:e + 1] * (he @ wd[e])
    return out.reshape(bsz, seq, d)

def setup_inputs(seed: int = 0) -> dict:
    key = jax.random.key(seed)
    ks = iter(jax.random.split(key, 64))
    L, D = DEPTH, D_MODEL

    def nrm(shape, scale):
        return jax.random.normal(next(ks), shape, jnp.float32) * scale

    def uni(shape, lo, hi):
        return jax.random.uniform(next(ks), shape, jnp.float32, lo, hi)

    def gain(shape):
        return 1.0 + nrm(shape, 0.02)

    return {
        "x": nrm((BATCH, SEQ, D), 1.0),
        "mem": nrm((BATCH, MEM_LEN, D), 1.0),
        "norm_mix": gain((L, D)),
        "w_in": nrm((L, D, IN_COLS), D ** -0.5),
        "mu_in": uni((L, RW_COLS), 0.0, 1.0),
        "w_vres_in": nrm((L - 1, D, LORA_VRES), D ** -0.5),
        "mu_vres": uni((L - 1, LORA_VRES), 0.0, 1.0),
        "w0": uni((L, RW_WIDTH), -6.0, -1.0),
        "w_decay_up": nrm((L, LORA_DECAY, RW_WIDTH), 0.1 * LORA_DECAY ** -0.5),
        "a0": nrm((L, RW_WIDTH), 0.5),
        "w_aaa_up": nrm((L, LORA_AAA, RW_WIDTH), LORA_AAA ** -0.5),
        "w_gate_up": nrm((L, LORA_GATE, RW_WIDTH), LORA_GATE ** -0.5),
        "v0": nrm((L - 1, RW_WIDTH), 0.5),
        "w_vres_up": nrm((L - 1, LORA_VRES, RW_WIDTH), LORA_VRES ** -0.5),
        "k_k": 0.85 + nrm((L, RW_WIDTH), 0.05),
        "k_a": 1.0 + nrm((L, RW_WIDTH), 0.05),
        "r_k": nrm((L, RW_HEADS, RW_HEAD_DIM), 0.1),
        "lnx_g": gain((L, RW_WIDTH)),
        "lnx_b": nrm((L, RW_WIDTH), 0.02),
        "conv_w": nrm((L, CONV_K, CONV_WIDTH), CONV_K ** -0.5),
        "gate_b": nrm((L, GATE_COLS), 0.1),
        "w_br_a": nrm((L, RW_WIDTH, D), RW_WIDTH ** -0.5),
        "w_br_b": nrm((L, CONV_WIDTH, D), CONV_WIDTH ** -0.5),
        "w_mix_out": nrm((L, D, D), D ** -0.5),
        "norm_memq": gain((L, D)),
        "norm_memkv": gain((L, D)),
        "wq_mem": nrm((L, D, MEM_HEADS * MEM_HEAD_DIM), D ** -0.5),
        "wkv_mem": nrm((L, D, 2 * MEM_HEADS * MEM_HEAD_DIM), D ** -0.5),
        "wo_mem": nrm((L, MEM_HEADS * MEM_HEAD_DIM, D), (MEM_HEADS * MEM_HEAD_DIM) ** -0.5),
        "norm_ffn": gain((L, D)),
        "router_g": nrm((L, D, N_GROUPS), D ** -0.5),
        "router_g_b": nrm((L, N_GROUPS), 0.01),
        "router_e": nrm((L, D, N_EXPERTS), D ** -0.5),
        "router_e_b": nrm((L, N_EXPERTS), 0.01),
        "w_e_gate": nrm((L, N_EXPERTS, D, D_EXPERT), D ** -0.5),
        "w_e_up": nrm((L, N_EXPERTS, D, D_EXPERT), D ** -0.5),
        "w_e_down": nrm((L, N_EXPERTS, D_EXPERT, D), D_EXPERT ** -0.5),
        "norm_f": gain((D,)),
    }

def reference(x, mem, norm_mix, w_in, mu_in, w_vres_in, mu_vres, w0, w_decay_up, a0,
              w_aaa_up, w_gate_up, v0, w_vres_up, k_k, k_a, r_k, lnx_g, lnx_b, conv_w,
              gate_b, w_br_a, w_br_b, w_mix_out, norm_memq, norm_memkv, wq_mem, wkv_mem,
              wo_mem, norm_ffn, router_g, router_g_b, router_e, router_e_b, w_e_gate,
              w_e_up, w_e_down, norm_f):
    bsz, seq, _ = x.shape
    f32 = jnp.float32

    def heads(z):
        return z.reshape(bsz, seq, RW_HEADS, RW_HEAD_DIM).astype(f32)

    v_first = None
    for l in range(DEPTH):
        xn = rms_norm(x, norm_mix[l])
        w_proj = w_in[l] if l == 0 else jnp.concatenate([w_in[l], w_vres_in[l - 1]], axis=1)
        p = xn @ w_proj
        rw = shift_mix(p[..., :RW_COLS], mu_in[l])
        conv_cols = p[..., RW_COLS:RW_COLS + CONV_COLS]
        gate_cols = p[..., RW_COLS + CONV_COLS:IN_COLS]

        o = 0
        r = rw[..., o:o + RW_WIDTH]; o += RW_WIDTH
        k = rw[..., o:o + RW_WIDTH]; o += RW_WIDTH
        v = rw[..., o:o + RW_WIDTH]; o += RW_WIDTH
        wd = rw[..., o:o + LORA_DECAY]; o += LORA_DECAY
        ad = rw[..., o:o + LORA_AAA]; o += LORA_AAA
        gd = rw[..., o:o + LORA_GATE]

        wlog = -jax.nn.softplus(-(w0[l] + jnp.tanh(wd) @ w_decay_up[l]).astype(f32)) - 0.5
        decay = jnp.exp(-jnp.exp(wlog))
        aa = jax.nn.sigmoid(a0[l] + ad @ w_aaa_up[l])
        og = jax.nn.sigmoid(gd) @ w_gate_up[l]
        if l == 0:
            v_first = v
        else:
            vd = shift_mix(p[..., IN_COLS:], mu_vres[l - 1])
            v = v + (v_first - v) * jax.nn.sigmoid(v0[l - 1] + vd @ w_vres_up[l - 1])
        kk = heads(k * k_k[l])
        kk = kk / jnp.maximum(jnp.sqrt(jnp.sum(kk * kk, axis=-1, keepdims=True)), L2_EPS)
        k = k * (1.0 + (aa - 1.0) * k_a[l])
        rh, kh, vh = heads(r), heads(k), heads(v)
        y = wkv7_scan(rh, heads(decay), kh, vh, -kk, kk * heads(aa))
        y_mu = jnp.mean(y, axis=-1, keepdims=True)
        y_var = jnp.mean(jnp.square(y - y_mu), axis=-1, keepdims=True)
        y = ((y - y_mu) * lax.rsqrt(y_var + LNX_EPS)).reshape(bsz, seq, RW_WIDTH)
        y = y * lnx_g[l] + lnx_b[l]
        bonus = jnp.sum(rh * kh * r_k[l], axis=-1, keepdims=True) * vh
        y_a = ((y + bonus.reshape(bsz, seq, RW_WIDTH)) * og).astype(x.dtype)

        cx = conv_cols[..., :CONV_WIDTH]
        cb = conv_cols[..., CONV_WIDTH:2 * CONV_WIDTH]
        cc = conv_cols[..., 2 * CONV_WIDTH:]
        y_b = cb * causal_dwconv(cc * cx, conv_w[l])

        gts = gate_cols + gate_b[l]
        g_a = jax.nn.sigmoid(gts[..., :D_MODEL])
        g_b = jax.nn.sigmoid(gts[..., D_MODEL:])
        merged = g_a * (y_a @ w_br_a[l]) + g_b * (y_b @ w_br_b[l])
        x = x + merged @ w_mix_out[l]

        x = x + mem_cross_attn(x, mem, norm_memq[l], norm_memkv[l], wq_mem[l], wkv_mem[l], wo_mem[l])

        hn = rms_norm(x, norm_ffn[l])
        x = x + hier_moe(hn, router_g[l], router_g_b[l], router_e[l], router_e_b[l],
                         w_e_gate[l], w_e_up[l], w_e_down[l])

    return rms_norm(x, norm_f)


_drawn_inputs = setup_inputs


def setup_inputs(seed=0):
    import zlib

    import numpy as np

    out = dict(_drawn_inputs(seed))
    spreads = {}
    factors = {'w_decay_up': 8.0,
     'k_k': 3.216,
     'k_a': 3.298,
     'lnx_g': 4.204,
     'lnx_b': 8.0,
     'norm_memq': 8.0,
     'norm_memkv': 5.418,
     'router_g_b': 27.264,
     'router_e_b': 64.0,
     'norm_f': 7.374,
     'norm_ffn': 8.0}
    for name, (base, spread) in spreads.items():
        noise = np.random.default_rng([zlib.crc32(name.encode()), seed]).standard_normal(out[name].shape)
        drawn = base * np.exp(spread * noise) if base else spread * noise
        out[name] = __import__('jax').numpy.asarray(drawn.astype(out[name].dtype))
    for name, factor in factors.items():
        out[name] = (out[name] * factor).astype(out[name].dtype)
    return out
```

```python
import concourse.bass as bass
from concourse import mybir
from contextlib import ExitStack

F32 = mybir.dt.float32
I32 = mybir.dt.int32
ALU = mybir.AluOpType
ACT = mybir.ActivationFunctionType
AX = mybir.AxisListType

P = 128
D = 1024
T = 512
KT = D // P
TT = T // P
HEADS, HD = 16, 64
PAIRS = HEADS // 2
C = 32
NCH = T // C
MEM = 256
MH, MHD = 4, 256
NG, EPG = 4, 4
NE = NG * EPG
DE = 512
SLOTS = P
RMS_EPS, LNX_EPS = 1e-6, 64e-5
EXP_M_HALF = 0.6065306597126334

RW_COLS = 3 * D + 64 + 64 + 160
CONV0 = RW_COLS
GATE0 = RW_COLS + 3 * D


class Steps:

    def __init__(self, eng, sem):
        self.eng, self.sem, self.n, self.i, self.per = eng, sem, 0, None, 0

    def value(self):
        return self.n if self.i is None else self.i * self.per + self.n

    def __call__(self, ins):
        ins.then_inc(self.sem, 1)
        self.n += 1
        self.eng.wait_ge(self.sem, self.value())

    def last(self, ins):
        ins.then_inc(self.sem, 1)
        self.n += 1

    def wait(self):
        self.eng.wait_ge(self.sem, self.value())

    def enter(self, i, per):
        self.i, self.per, self.base = i, per, self.n

    def leave(self, turns):
        assert self.n - self.base == self.per, (self.n - self.base, self.per)
        self.n, self.i = self.base + turns * self.per, None


def build_trunk(nc, x, mem, norm_mix, w_in, mu_in, w0, w_decay_up, a0, w_aaa_up, w_gate_up, k_k, k_a, r_k,
                lnx_g, lnx_b, conv_w, gate_b, w_br_a, w_br_b, w_mix_out, norm_memq, norm_memkv, wq_mem,
                wkv_mem, wo_mem, norm_ffn, router_g, router_g_b, router_e, router_e_b, w_e_gate, w_e_up,
                w_e_down, norm_f, out):
    whole = ExitStack()

    def dram(name, shape, dt=F32):
        return nc.dram_tensor(name, shape, dt).ap()

    x_scr = dram("x_scr", [P, KT, T])
    og_scr = dram("og_scr", [P, KT, T])
    ya_scr = dram("ya_scr", [P, KT, T])
    bonus_scr = dram("bonus_scr", [P, KT, T])
    yb_scr = dram("yb_scr", [P, KT, T])
    gates_scr = dram("gates_scr", [P, 2 * KT, T])
    m_scr = dram("m_scr", [PAIRS * NCH, 2, C, C])
    t_scr = dram("t_scr", [PAIRS * NCH, 2, C, C])
    hn_scr = dram("hn_scr", [T, D])
    tok_scr = dram("tok_scr", [NE * T, 1], I32)
    y_scr = dram("y_scr", [NE * T, D])

    with whole:
        class Area:

            parts = 0
            sems = []

            @staticmethod
            def recycle():
                nc.clear_and_free_semaphores(Area.sems)
                nc.all_engine_barrier()
                Area.sems = []

            def __init__(self, stack):
                self.stack = stack
                Area.parts += 1
                self.part = Area.parts

            def sb(self, name, shape, dt=F32):
                return self.stack.enter_context(nc.sbuf_tensor(f"{name}_{self.part}", shape, dt))

            def sem(self, name):
                sem = nc.alloc_semaphore(f"{name}_{self.part}")
                Area.sems.append(sem)
                return sem

        top = Area(whole)
        bank = [whole.enter_context(nc.psum_tensor(f"bank{i}", [P, 512], F32)) for i in range(8)]
        ident = top.sb("ident", [P, P])
        mean_ones = top.sb("mean_ones", [P, P])
        head_ones = top.sb("head_ones", [P, P])
        earlier = top.sb("earlier", [P, P])
        pcol = top.sb("pcol", [P, 256])
        eps_col = top.sb("eps_col", [P, 2])
        one_minus_mu = top.sb("one_minus_mu", [P, 27])
        one_minus_ka = top.sb("one_minus_ka", [P, KT])

        rows, where = [], {}

        def param(name, ap, n, tile):
            at = sum(r[2] for r in rows if r[3] == tile)
            rows.append((name, ap, n, tile, at))
            where[name] = tile * P + at

        def flat(ap):
            return ap.rearrange("(j p) -> j p", p=P)

        param("mu", flat(mu_in[0, 0:3328]), 26, 0)
        param("norm_mix", flat(norm_mix[0, :]), 8, 0)
        param("w0", flat(w0[0, :]), 8, 0)
        param("a0", flat(a0[0, :]), 8, 0)
        param("k_k", flat(k_k[0, :]), 8, 0)
        param("k_a", flat(k_a[0, :]), 8, 0)
        param("r_k", r_k[0, :, :].rearrange("(j h) n -> j (h n)", h=2), 8, 0)
        param("lnx_g", flat(lnx_g[0, :]), 8, 0)
        param("lnx_b", flat(lnx_b[0, :]), 8, 0)
        param("conv_w", conv_w[0, :, :].rearrange("c (j p) -> (c j) p", p=P), 24, 0)
        param("norm_ffn", flat(norm_ffn[0, :]), 8, 0)
        param("gate_b", flat(gate_b[0, :]), 16, 1)
        param("norm_memq", flat(norm_memq[0, :]), 8, 1)
        param("norm_memkv", flat(norm_memkv[0, :]), 8, 1)
        where["mu_g1"] = P + 32

        def col(name, j=0, n=1):
            at = where[name]
            return pcol[:, bass.ds(at + j, n)]

        wkv = ExitStack()
        w = Area(wkv)
        rkv = w.sb("rkv", [P, 24, T])
        aa = w.sb("aa", [P, KT, T])
        w_end = w.sb("w_end", [P, NCH, PAIRS])
        xn = w.sb("xn", [P, KT, T])
        lq = w.sb("lq", [P, PAIRS, NCH, 2, C])
        sc = w.sb("sc", [P, PAIRS, NCH, 2, C])
        lq_flat = lq[:, :, :, :, :].rearrange("p j c a t -> p (j c a t)")
        sc_flat = sc[:, :, :, :, :].rearrange("p j c a t -> p (j c a t)")
        early = ExitStack()
        decay = early.enter_context(nc.sbuf_tensor("decay", [P, KT, T], F32))
        ring_stack = ExitStack()
        ring = ring_stack.enter_context(nc.sbuf_tensor("ring_rkv", [P, 2, KT, 512], F32))
        w_loaded = [w.sem("w_loaded0"), w.sem("w_loaded1")]

        def w_cols(c0, n):
            return w_in[0, :, bass.ds(c0, n)].rearrange("(k p) c -> p k c", p=P)

        with ExitStack() as s:
            a = Area(s)
            x_tok = rkv[:, 0:8, :].rearrange("p k t -> p (k t)").rearrange("p (i e) -> p i e", i=TT)
            prow = a.sb("prow", [P, 2, P])
            xT, sq, rstd = rkv[:, 8:16, :], rkv[:, 16:24, :], lq_flat[:, 0:T]
            const_step, consts, prow_clear, prow_in, x_in = map(a.sem, ("const_step", "consts", "prow_clear", "prow_in", "x_in"))
            pcol_T, x_T, x_out, sq_ok, mean_ok, dve_step, xn_ok, stored, std_ok = map(
                a.sem, ("pcol_T", "x_T", "x_out", "sq_ok", "mean_ok", "dve_step", "xn_ok", "stored", "std_ok"))
            block = s.enter_context(nc.Block())

            @block.gpsimd
            def _(pool):
                step = Steps(pool, const_step)
                step(nc.gpsimd.memset(ident[:, :], 0.0))
                step(nc.gpsimd.affine_select(out=ident[:, :], in_=ident[:, :], compare_op=ALU.not_equal, fill=1.0,
                                             base=0, pattern=[[-1, P]], channel_multiplier=1))
                step(nc.gpsimd.memset(earlier[:, :], 0.0))
                step(nc.gpsimd.affine_select(out=earlier[:, :], in_=earlier[:, :], compare_op=ALU.is_ge, fill=1.0,
                                             base=0, pattern=[[-1, P]], channel_multiplier=1))
                step(nc.gpsimd.memset(mean_ones[:, :], 1.0 / D))
                step(nc.gpsimd.memset(head_ones[:, :], 0.0))
                step(nc.gpsimd.memset(head_ones[0:HD, 0:HD], 1.0))
                nc.gpsimd.memset(head_ones[HD:P, HD:P], 1.0).then_inc(consts, 1)

            @block.sync
            def _(sp):
                sp.dma_start(x_tok[:, :, :], x[0, :, :].rearrange("(i p) d -> p i d", p=P)).then_inc(x_in, 16)
                sp.wait_ge(prow_clear, 1)
                for name, ap, n, tile, at in rows:
                    sp.dma_start(prow[at:at + n, tile, :], ap).then_inc(prow_in, 16)
                sp.dma_start(prow[32:33, 1, 0:32], mu_in[0:1, 3328:3360]).then_inc(prow_in, 16)
                for u in range(2):
                    sp.dma_start(ring[:, u, :, :], w_cols(u * 512, 512)).then_inc(w_loaded[u], 16)
                sp.wait_ge(x_out, KT)
                sp.dma_start(x_scr, xT[:, :, :]).then_inc(stored, 16)
                sp.wait_ge(stored, 16)

            @block.tensor
            def _(pe):
                pe.wait_ge(consts, 1)
                pe.wait_ge(prow_in, 16 * (len(rows) + 1))
                for i in range(2):
                    nc.tensor.transpose(bank[5][:, i * P:(i + 1) * P], prow[:, i, :], ident[:, :]).then_inc(pcol_T, 1)
                pe.wait_ge(x_in, 16)
                for k in range(KT):
                    if k >= 4:
                        pe.wait_ge(x_out, k - 3)
                        pe.wait_ge(sq_ok, k - 3)
                    for i in range(TT):
                        last = nc.tensor.transpose(bank[k % 4][:, i * P:(i + 1) * P],
                                                   x_tok[:, i, k * P:(k + 1) * P], ident[:, :])
                    last.then_inc(x_T, 1)
                for k in range(KT):
                    pe.wait_ge(sq_ok, k + 1)
                    last = nc.tensor.matmul(bank[4][:, :], mean_ones[:, :], sq[:, k, :], start=(k == 0), stop=(k == KT - 1))
                last.then_inc(mean_ok, 1)

            @block.scalar
            def _(act):
                for k in range(KT):
                    act.wait_ge(x_T, k + 1)
                    nc.scalar.activation(xT[:, k, :], bank[k % 4][:, :], ACT.Copy).then_inc(x_out, 1)
                    nc.scalar.activation(sq[:, k, :], bank[k % 4][:, :], ACT.Square).then_inc(sq_ok, 1)
                act.wait_ge(dve_step, 5)
                nc.scalar.activation(rstd[:, :], rstd[:, :], ACT.Sqrt).then_inc(std_ok, 1)

            @block.vector
            def _(dve):
                step = Steps(dve, dve_step)
                nc.vector.memset(prow[:, :, :], 0.0).then_inc(prow_clear, 1)
                nc.vector.memset(eps_col[:, 0:1], RMS_EPS)
                nc.vector.memset(eps_col[:, 1:2], LNX_EPS)
                dve.wait_ge(pcol_T, 2)
                step(nc.vector.tensor_copy(pcol[:, :], bank[5][:, 0:256]))
                step(nc.vector.tensor_scalar(one_minus_mu[:, 0:26], pcol[:, 0:26], -1.0, 1.0, ALU.mult, ALU.add))
                step(nc.vector.tensor_scalar(one_minus_mu[:, 26:27], col("mu_g1"), -1.0, 1.0, ALU.mult, ALU.add))
                step(nc.vector.tensor_scalar(one_minus_ka[:, :], col("k_a", 0, 8), -1.0, 1.0, ALU.mult, ALU.add))
                dve.wait_ge(mean_ok, 1)
                step(nc.vector.tensor_scalar(rstd[:, :], bank[4][:, :], RMS_EPS, None, ALU.add))
                dve.wait_ge(x_out, KT)
                dve.wait_ge(std_ok, 1)
                step(nc.vector.reciprocal(rstd[:, :], rstd[:, :]))
                for k in range(KT):
                    nc.vector.scalar_tensor_tensor(out=xn[:, k, :], in0=xT[:, k, :], scalar=col("norm_mix", k), in1=rstd[:, :],
                                                   op0=ALU.mult, op1=ALU.mult).then_inc(xn_ok, 1)

        with ExitStack() as s0:
            with ExitStack() as s:
                a = Area(s)
                lora = sc_flat[:, 0:3 * T].rearrange("p (k t) -> p k t", k=3)
                og = lq_flat[:, 0:KT * T].rearrange("p (k t) -> p k t", k=KT)
                up_da = lq_flat[:, 4096:4096 + D]
                up_g = lq_flat[:, 4096 + D:4096 + 3 * D].rearrange("p (k d) -> p k d", k=2)
                up_in, mm_ok, part1, shifted, lora_act, up_ok, up_out, og_out, og_st, dve_step, act_step = map(
                    a.sem, ("up_in", "mm_ok", "part1", "shifted", "lora_act", "up_ok", "up_out", "og_out", "og_st", "dve_step", "act_step"))
                block = s.enter_context(nc.Block())

                @block.sync
                def _(sp):
                    sp.dma_start(up_da[0:64, :], w_decay_up[0, :, :]).then_inc(up_in, 16)
                    sp.dma_start(up_da[64:128, :], w_aaa_up[0, :, :]).then_inc(up_in, 16)
                    sp.dma_start(up_g[:, 0, :], w_gate_up[0, 0:128, :]).then_inc(up_in, 16)
                    sp.dma_start(up_g[0:32, 1, :], w_gate_up[0, 128:160, :]).then_inc(up_in, 16)
                    with sp.Fori(0, 2) as i:
                        for u in range(2):
                            sp.wait_ge(mm_ok, i * 8 + 4 * (u + 1))
                            sp.dma_start(ring[:, u, :, :], w_cols(i * 1024 + (u + 2) * 512, 512)).then_inc(w_loaded[u], 16)
                    sp.wait_ge(mm_ok, 20)
                    sp.dma_start(ring[:, 0, :, 0:288], w_cols(3072, 288)).then_inc(w_loaded[0], 16)
                    sp.wait_ge(og_out, KT)
                    sp.dma_start(og_scr, og[:, :, :]).then_inc(og_st, 16)
                    sp.wait_ge(og_st, 16)

                @block.tensor
                def _(pe):
                    with pe.Fori(0, 3) as i:
                        for u in range(2):
                            pe.wait_ge(w_loaded[u], i * 16 + 16)
                            for q in range(4):
                                pe.wait_ge(shifted, i * 8 + 4 * u + q + 1)
                                for k in range(KT):
                                    last = nc.tensor.matmul(bank[q][:, :], ring[:, u, k, q * P:(q + 1) * P], xn[:, k, :],
                                                            start=(k == 0), stop=(k == KT - 1))
                                last.then_inc(mm_ok, 1)
                    pe.wait_ge(w_loaded[0], 64)
                    for q in range(3):
                        n = (P, P, 32)[q]
                        pe.wait_ge(shifted, 24 + q + 1)
                        for k in range(KT):
                            last = nc.tensor.matmul(bank[q][0:n, :], ring[:, 0, k, q * P:q * P + n], xn[:, k, :],
                                                    start=(k == 0), stop=(k == KT - 1))
                        last.then_inc(mm_ok, 1)
                    pe.wait_ge(up_in, 64)
                    pe.wait_ge(lora_act, 3)
                    for j in range(KT):
                        cs = slice(j * P, (j + 1) * P)
                        for q in range(3):
                            n = 3 * j + q
                            b = bank[4 + n % 4]
                            if n >= 4:
                                pe.wait_ge(up_out, n - 3)
                            if q < 2:
                                rs = slice(64 * q, 64 * q + 64)
                                nc.tensor.matmul(b[:, :], up_da[rs, cs], lora[rs, 0, :], start=True, stop=True).then_inc(up_ok, 1)
                            else:
                                nc.tensor.matmul(b[:, :], up_g[:, 0, cs], lora[:, 1, :], start=True, stop=False)
                                nc.tensor.matmul(b[:, :], up_g[0:32, 1, cs], lora[0:32, 2, :], start=False, stop=True).then_inc(up_ok, 1)

                @block.scalar
                def _(act):
                    with act.Fori(0, 6) as i:
                        for q in range(4):
                            act.wait_ge(mm_ok, i * 4 + q + 1)
                            nc.scalar.activation(rkv[:, bass.ds(i * 4 + q, 1), :], bank[q][:, :].rearrange("p (a t) -> p a t", a=1), ACT.Copy,
                                                 scale=one_minus_mu[:, bass.ds(i * 4 + q, 1)]).then_inc(part1, 1)
                    for q in range(3):
                        n = (P, P, 32)[q]
                        act.wait_ge(mm_ok, 24 + q + 1)
                        nc.scalar.activation(lora[0:n, q, :], bank[q][0:n, :], ACT.Copy,
                                             scale=one_minus_mu[0:n, 24 + q:25 + q]).then_inc(part1, 1)
                    act.wait_ge(shifted, 4 + 27)
                    nc.scalar.activation(lora[0:64, 0, :], lora[0:64, 0, :], ACT.Tanh).then_inc(lora_act, 1)
                    nc.scalar.activation(lora[:, 1, :], lora[:, 1, :], ACT.Sigmoid).then_inc(lora_act, 1)
                    nc.scalar.activation(lora[0:32, 2, :], lora[0:32, 2, :], ACT.Sigmoid).then_inc(lora_act, 1)
                    for j in range(KT):
                        act.wait_ge(up_ok, 3 * j + 1)
                        nc.scalar.activation(decay[:, j, :], bank[4 + (3 * j) % 4][:, :], ACT.Sigmoid, bias=col("w0", j)).then_inc(up_out, 1)
                        act.wait_ge(up_ok, 3 * j + 2)
                        nc.scalar.activation(aa[:, j, :], bank[4 + (3 * j + 1) % 4][:, :], ACT.Sigmoid, bias=col("a0", j)).then_inc(up_out, 1)
                        act.wait_ge(up_ok, 3 * j + 3)
                        nc.scalar.activation(og[:, j, :], bank[4 + (3 * j + 2) % 4][:, :], ACT.Copy).then_inc(up_out, 1)
                    act.wait_ge(up_out, 3 * KT)
                    nc.scalar.sem_inc(og_out, KT)

                @block.vector
                def _(dve):
                    dve.sem_inc(shifted, 4)
                    with dve.Fori(0, 6) as i:
                        for q in range(4):
                            n = i * 4 + q
                            dve.wait_ge(part1, n + 1)
                            later = rkv[:, bass.ds(n, 1), 1:T]
                            nc.vector.scalar_tensor_tensor(out=later, in0=bank[q][:, 0:T - 1].rearrange("p (a t) -> p a t", a=1),
                                                           scalar=pcol[:, bass.ds(n, 1)], in1=later,
                                                           op0=ALU.mult, op1=ALU.add).then_inc(shifted, 1)
                    for q in range(3):
                        n = (P, P, 32)[q]
                        dve.wait_ge(part1, 24 + q + 1)
                        mu = pcol[0:n, 24 + q:25 + q] if q < 2 else pcol[0:n, where["mu_g1"]:where["mu_g1"] + 1]
                        nc.vector.scalar_tensor_tensor(out=lora[0:n, q, 1:T], in0=bank[q][0:n, 0:T - 1], scalar=mu,
                                                       in1=lora[0:n, q, 1:T], op0=ALU.mult, op1=ALU.add).then_inc(shifted, 1)


            ring_stack.close()
            with ExitStack() as s:
                a = Area(s)
                not_first = a.sb("not_first", [P, T])
                causal = a.sb("causal", [P, 2, C])
                kk0, ssq, ka, w_cum, w_inv, rk, w_log, bonus, conv_y = (
                    a.sb(n, [P, T]) for n in ("kk0", "ssq", "ka", "w_cum", "w_inv", "rk", "w_log", "bonus", "conv_y"))
                sq, kb, conv_x = ssq, w_log, conv_y
                conv_u = a.sb("conv_u", [P, T + 2])
                conv_w3 = a.sb("conv_w3", [P, 3, KT, P])
                lb = a.sb("lb", [P, NCH, 2, 2, C])
                bh, kh = aa, rkv[:, 8:16, :]
                cw_in = [a.sem(f"cw_in{q}") for q in range(3)]
                (bonus_out, yb_out, cx_mm, cc_mm, cb_mm, cx_ok, u_ok, c1_ok, c2_ok, c3_ok, yb_ok, yb_free) = map(
                    a.sem, ("bonus_out", "yb_out", "cx_mm", "cc_mm", "cb_mm", "cx_ok", "u_ok", "c1_ok", "c2_ok", "c3_ok", "yb_ok", "yb_free"))
                (cs, masks_ok, lb_clear, kk0_ok, sq_ok, ka_ok, ssq_mm, ssq_ok, norm_ok, wlog_ok, winv_used, wcum_ok, winv_ok,
                 km_ok, kk_ok, rk_ok, rksum_mm, lq_ok, kb_ok, bh_ok, kh_ok, bonus_ok, wend_ok, lb_ok, sc_mm, sc_ok, spread_begun) = map(
                    a.sem, ("cs", "masks_ok", "lb_clear", "kk0_ok", "sq_ok", "ka_ok", "ssq_mm", "ssq_ok", "norm_ok", "wlog_ok",
                            "winv_used", "wcum_ok", "winv_ok", "km_ok", "kk_ok", "rk_ok", "rksum_mm", "lq_ok", "kb_ok", "bh_ok",
                            "kh_ok", "bonus_ok", "wend_ok", "lb_ok", "sc_mm", "sc_ok", "spread_begun"))
                block = s.enter_context(nc.Block())

                def tile(arr, j):
                    return arr[:, bass.ds(j, 1), :].rearrange("p a t -> p (a t)")

                def chunks(ap):
                    return ap.rearrange("p (c t) -> p c t", c=NCH)

                @block.sync
                def _(sp):
                    def conv_weights(j, q):
                        src = (0, 2, 1)[q] * D + CONV0
                        sp.dma_start(conv_w3[:, q, :, :], w_cols(j * P + src, P)).then_inc(cw_in[q], 16)

                    sp.sem_inc(bonus_out, 16)
                    sp.sem_inc(yb_out, 16)
                    for q in range(3):
                        conv_weights(0, q)
                    with sp.Fori(0, PAIRS - 1) as j:
                        for q, used in enumerate((cx_mm, cc_mm, cb_mm)):
                            sp.wait_ge(used, j + 1)
                            conv_weights(j + 1, q)
                        sp.wait_ge(bonus_ok, j + 2)
                        sp.dma_start(bonus_scr[:, bass.ds(j, 1), :], bonus[:, :].unsqueeze(1)).then_inc(bonus_out, 16)
                        sp.wait_ge(yb_ok, j + 1)
                        sp.dma_start(yb_scr[:, bass.ds(j, 1), :], conv_y[:, :].unsqueeze(1)).then_inc(yb_out, 16)
                    sp.wait_ge(bonus_ok, PAIRS + 1)
                    sp.dma_start(bonus_scr[:, PAIRS - 1, :], bonus[:, :]).then_inc(bonus_out, 16)
                    sp.wait_ge(yb_ok, PAIRS)
                    sp.dma_start(yb_scr[:, PAIRS - 1, :], conv_y[:, :]).then_inc(yb_out, 16)
                    sp.wait_ge(bonus_out, 16 * (PAIRS + 1))
                    sp.wait_ge(yb_out, 16 * (PAIRS + 1))

                @block.gpsimd
                def _(pool):
                    step = Steps(pool, cs)
                    step(nc.gpsimd.memset(not_first[:, :], 1.0))
                    step(nc.gpsimd.memset(chunks(not_first[:, :])[:, :, 0:1], 0.0))
                    for q in range(4):
                        qs = slice(C * q, C * q + C)
                        step(nc.gpsimd.tensor_copy(causal[qs, 0, :], earlier[qs, qs]))
                        step(nc.gpsimd.tensor_tensor(causal[qs, 1, :], earlier[qs, qs], ident[qs, qs], ALU.add))
                    nc.gpsimd.memset(lb[:, :, :, :, :], 0.0).then_inc(lb_clear, 1)
                    with pool.Fori(0, PAIRS) as j:
                        pool.wait_ge(norm_ok, 2 * j + 2)
                        nc.gpsimd.tensor_tensor(kk0[:, :], kk0[:, :], ssq[:, :], ALU.mult).then_inc(kk_ok, 1)

                @block.scalar
                def _(act):
                    with act.Fori(0, PAIRS) as j:
                        act.wait_ge(kk_ok, j + 1)
                        act.wait_ge(bh_ok, j + 1)
                        act.wait_ge(lb_clear, 2)
                        nc.scalar.activation(kk0[:, :], tile(rkv, j + 8), ACT.Copy, scale=col("k_k", j)).then_inc(kk0_ok, 1)
                        act.wait_ge(kk0_ok, j + 1)
                        nc.scalar.activation(sq[:, :], kk0[:, :], ACT.Square).then_inc(sq_ok, 1)
                        act.wait_ge(wlog_ok, j + 1)
                        act.wait_ge(lq_ok, 3 * j + 3)
                        act.wait_ge(wend_ok, j + 1)
                        nc.scalar.activation(w_cum[:, :], w_log[:, :], ACT.Exp, scale=-EXP_M_HALF).then_inc(wcum_ok, 1)
                        nc.scalar.activation(w_inv[:, :], w_log[:, :], ACT.Exp, scale=EXP_M_HALF).then_inc(winv_ok, 1)
                        act.wait_ge(winv_ok, j + 1)
                        act.sem_inc(winv_used, 1)
                        act.wait_ge(km_ok, j + 1)
                        act.wait_ge(lb_clear, 2)
                        nc.scalar.activation(ka[:, :], tile(aa, j), ACT.Identity, scale=col("k_a", j),
                                             bias=one_minus_ka[:, bass.ds(j, 1)]).then_inc(ka_ok, 1)
                        act.wait_ge(ssq_ok, j + 2)
                        nc.scalar.activation(ssq[:, :], ssq[:, :], ACT.Ln).then_inc(norm_ok, 1)
                        act.wait_ge(norm_ok, 2 * j + 1)
                        nc.scalar.activation(ssq[:, :], ssq[:, :], ACT.Exp, scale=-0.5).then_inc(norm_ok, 1)
                        act.wait_ge(sc_mm, 2 * j + 2)
                        act.wait_ge(bh_ok, j + 2)
                        act.wait_ge(kh_ok, j + 1)
                        act.sem_inc(spread_begun, 1)
                        for h in range(2):
                            hs = slice(HD * h, HD * h + HD)
                            nc.scalar.activation(lb[hs, :, 0, h, :], chunks(bh[hs, bass.ds(j, 1), :].rearrange("p a t -> p (a t)")), ACT.Copy).then_inc(lb_ok, 1)
                            nc.scalar.activation(lb[hs, :, 1, h, :], chunks(kh[hs, bass.ds(j, 1), :].rearrange("p a t -> p (a t)")), ACT.Copy).then_inc(lb_ok, 1)
                        act.wait_ge(cx_mm, j + 1)
                        act.wait_ge(yb_out, j * 16 + 16)
                        nc.scalar.activation(conv_x[:, :], bank[4][:, :], ACT.Copy).then_inc(cx_ok, 1)
                        act.wait_ge(u_ok, j + 1)
                        nc.scalar.activation(conv_y[:, :], conv_u[:, 2:T + 2], ACT.Copy, scale=col("conv_w", j + 16)).then_inc(c1_ok, 1)

                @block.tensor
                def _(pe):
                    pe.sem_inc(sc_mm, 2)

                    def conv(j, q, done):
                        pe.wait_ge(cw_in[q], j * 16 + 16)
                        for k in range(KT):
                            last = nc.tensor.matmul(bank[4 + q][:, :], conv_w3[:, q, k, :], xn[:, k, :], start=(k == 0), stop=(k == KT - 1))
                        last.then_inc(done, 1)

                    with pe.Fori(0, PAIRS) as j:
                        pe.wait_ge(sq_ok, j + 1)
                        pe.wait_ge(ssq_ok, j + 1)
                        nc.tensor.matmul(bank[0][:, :], head_ones[:, :], sq[:, :], start=True, stop=True).then_inc(ssq_mm, 1)
                        pe.wait_ge(yb_free, j + 1)
                        conv(j, 0, cx_mm)
                        pe.wait_ge(rk_ok, j + 1)
                        pe.wait_ge(bonus_ok, j + 1)
                        nc.tensor.matmul(bank[1][:, :], head_ones[:, :], rk[:, :], start=True, stop=True).then_inc(rksum_mm, 1)
                        conv(j, 1, cc_mm)
                        conv(j, 2, cb_mm)
                        pe.wait_ge(lb_ok, 4 * j + 4)
                        pe.wait_ge(lq_ok, 3 * j + 6)
                        for g in range(2):
                            pe.wait_ge(sc_ok, 2 * j + g + 1)
                            for c in range(8):
                                last = nc.tensor.matmul(bank[2 + g][:, c * 64:(c + 1) * 64], lb[:, 8 * g + c, :, :, :].rearrange("p b h s -> p (b h s)"),
                                                        lq[:, bass.ds(j, 1), 8 * g + c, :, :].rearrange("p j a t -> p (j a t)"),
                                                        start=True, stop=True)
                            last.then_inc(sc_mm, 1)

                @block.vector
                def _(dve):
                    for n, unused in ((3, lq_ok), (1, wend_ok), (1, yb_free)):
                        dve.sem_inc(unused, n)
                    for unused in (kk_ok, bh_ok, km_ok, ssq_ok, bonus_ok, winv_used, sc_ok, sc_ok):
                        dve.sem_inc(unused, 1)
                    nc.vector.memset(conv_u[:, 0:2], 0.0).then_inc(lb_clear, 1)
                    dve.wait_ge(lb_clear, 2)
                    with dve.Fori(0, PAIRS) as j:
                        r, k, v = (tile(rkv, j + n) for n in (0, 8, 16))
                        dve.wait_ge(winv_used, j + 1)
                        dve.wait_ge(bh_ok, j + 1)
                        nc.vector.tensor_tensor_scan(w_log[:, :], not_first[:, :], tile(decay, j), 0.0, ALU.mult, ALU.add).then_inc(wlog_ok, 1)
                        dve.wait_ge(ka_ok, j + 1)
                        nc.vector.tensor_tensor(k, k, ka[:, :], ALU.mult).then_inc(km_ok, 1)
                        dve.wait_ge(ssq_mm, j + 1)
                        dve.wait_ge(kk_ok, j + 1)
                        nc.vector.tensor_scalar(ssq[:, :], bank[0][:, :], 1e-24, None, ALU.max).then_inc(ssq_ok, 1)
                        dve.wait_ge(km_ok, j + 2)
                        nc.vector.scalar_tensor_tensor(out=rk[:, :], in0=r, scalar=col("r_k", j), in1=k, op0=ALU.mult, op1=ALU.mult).then_inc(rk_ok, 1)
                        dve.wait_ge(wcum_ok, j + 1)
                        lqj = lq[:, bass.ds(j, 1), :, :, :]
                        nc.vector.tensor_tensor(lqj[:, :, :, 1, :].rearrange("p j c t -> p (j c) t"), chunks(r), chunks(w_cum[:, :]), ALU.mult).then_inc(lq_ok, 1)
                        dve.wait_ge(kk_ok, j + 2)
                        nc.vector.tensor_tensor(lqj[:, :, :, 0, 1:C].rearrange("p j c t -> p (j c) t"), chunks(kk0[:, :])[:, :, 1:C],
                                                chunks(w_cum[:, :])[:, :, 0:C - 1], ALU.mult).then_inc(lq_ok, 1)
                        nc.vector.tensor_copy(lqj[:, :, :, 0, 0:1].rearrange("p j c t -> p (j c) t"), chunks(kk0[:, :])[:, :, 0:1]).then_inc(lq_ok, 1)
                        dve.wait_ge(winv_ok, j + 1)
                        nc.vector.scalar_tensor_tensor(out=kb[:, :], in0=kk0[:, :], scalar=-1.0, in1=tile(aa, j), op0=ALU.mult, op1=ALU.mult).then_inc(kb_ok, 1)
                        dve.wait_ge(winv_ok, j + 1)
                        nc.vector.tensor_tensor(k, k, w_inv[:, :], ALU.mult).then_inc(kh_ok, 1)
                        dve.wait_ge(kb_ok, j + 1)
                        nc.vector.tensor_tensor(tile(aa, j), kb[:, :], w_inv[:, :], ALU.mult).then_inc(bh_ok, 1)
                        nc.vector.tensor_copy(w_end[:, :, bass.ds(j, 1)], chunks(w_cum[:, :])[:, :, C - 1:C]).then_inc(wend_ok, 1)
                        dve.wait_ge(rksum_mm, j + 1)
                        dve.wait_ge(bonus_out, j * 16 + 16)
                        nc.vector.tensor_tensor(bonus[:, :], bank[1][:, :], v, ALU.mult).then_inc(bonus_ok, 1)
                        dve.wait_ge(cc_mm, j + 1)
                        dve.wait_ge(cx_ok, j + 1)
                        nc.vector.tensor_tensor(conv_u[:, 2:T + 2], bank[5][:, :], conv_x[:, :], ALU.mult).then_inc(u_ok, 1)
                        for g in range(2):
                            dve.wait_ge(sc_mm, 2 * j + g + 3)
                            nc.vector.tensor_tensor(sc[:, bass.ds(j, 1), 8 * g:8 * g + 8, :, :].rearrange("p j c a t -> p (j c) (a t)"),
                                                    bank[2 + g][:, :].rearrange("p (c a) -> p c a", c=8),
                                                    causal[:, :, :].rearrange("p a t -> p (a t)").unsqueeze(1).to_broadcast([P, 8, 2 * C]),
                                                    ALU.mult).then_inc(sc_ok, 1)
                        dve.wait_ge(c1_ok, j + 1)
                        nc.vector.scalar_tensor_tensor(out=conv_y[:, :], in0=conv_u[:, 1:T + 1], scalar=col("conv_w", j + 8), in1=conv_y[:, :],
                                                       op0=ALU.mult, op1=ALU.add).then_inc(c2_ok, 1)
                        dve.wait_ge(c2_ok, j + 1)
                        nc.vector.scalar_tensor_tensor(out=conv_y[:, :], in0=conv_u[:, 0:T], scalar=col("conv_w", j), in1=conv_y[:, :],
                                                       op0=ALU.mult, op1=ALU.add).then_inc(c3_ok, 1)
                        dve.wait_ge(c3_ok, j + 1)
                        dve.wait_ge(cb_mm, j + 1)
                        nc.vector.tensor_tensor(conv_y[:, :], conv_y[:, :], bank[6][:, :], ALU.mult).then_inc(yb_ok, 1)
                        dve.wait_ge(yb_ok, j + 1)
                        dve.sem_inc(yb_free, 1)
        early.close()

        with ExitStack() as s:
            a = Area(s)
            inv = a.sb("inv", [P, 2, C, C])
            prod = a.sb("prod", [P, 2, C * C // 4])
            m_out, m_in, solve_step, solved, t_out = map(a.sem, ("m_out", "m_in", "solve_step", "solved", "t_out"))
            block = s.enter_context(nc.Block())

            @block.sync
            def _(sp):
                for h in range(2):
                    sp.dma_start(m_scr[:, h, :, :].rearrange("u s t -> s u t"),
                                 sc[C * h:C * h + C, :, :, 0, :].rearrange("s j c t -> s (j c) t")).then_inc(m_out, 16)
                sp.wait_ge(m_out, 32)
                sp.dma_start(inv[:, :, :, :], m_scr).then_inc(m_in, 16)
                sp.wait_ge(solved, 1)
                sp.dma_start(t_scr, inv[:, :, :, :]).then_inc(t_out, 16)
                sp.wait_ge(t_out, 16)

            @block.vector
            def _(dve):
                step = Steps(dve, solve_step)
                dve.wait_ge(m_in, 16)
                for n in range(1, C - 1):
                    left, later = n, C - 1 - n
                    pr = prod[:, :, 0:left * later].rearrange("p h (j t) -> p h j t", j=left)
                    step(nc.vector.tensor_tensor(pr, inv[:, :, 0:n, n:n + 1].to_broadcast([P, 2, left, later]),
                                                 inv[:, :, n:n + 1, n + 1:C].to_broadcast([P, 2, left, later]), ALU.mult))
                    step(nc.vector.tensor_tensor(inv[:, :, 0:n, n + 1:C], inv[:, :, 0:n, n + 1:C], pr, ALU.add))
                flat_inv = inv[:, :, :, :].rearrange("p h s t -> p h (s t)")
                nc.vector.tensor_scalar(flat_inv[:, :, 0:C * C:C + 1], flat_inv[:, :, 0:C * C:C + 1], 1.0, None, ALU.add).then_inc(solved, 1)

        yT = rkv[:, 0:8, :]
        with ExitStack() as s:
            a = Area(s)
            state = a.sb("state", [P, PAIRS, HD])
            lqx = [a.sb(f"lqx{u}", [P, PAIRS, 2, 2, C]) for u in range(2)]
            scx = [a.sb(f"scx{u}", [P, PAIRS, 2, 2, C]) for u in range(2)]
            lbx = [a.sb(f"lbx{u}", [P, PAIRS, P]) for u in range(2)]
            ttx = [a.sb(f"ttx{u}", [2 * C, PAIRS, 2, C]) for u in range(2)]
            uv = [a.sb(f"uv{u}", [P, PAIRS, HD]) for u in range(2)]
            qs = a.sb("qs", [2 * C, PAIRS, HD])
            gate_w = a.sb("gate_w", [P, 4, KT, P])
            gate = a.sb("gate", [P, 2, T])
            gw_in = [a.sem(f"gw_in{n}") for n in range(4)]
            gate_out = [a.sem(f"gate_out{n}") for n in range(2)]
            g_mm, gate_ok = a.sem("g_mm"), a.sem("gate_ok")
            head_is = a.sb("head_is", [P, 2])
            (clear, spread, turned, tt_in0, tt_in1, q_mm, q_ok, u_mm, u_ok, s_mm, s_added, s_ok, y_mm, y_ok) = map(
                a.sem, ("clear", "spread", "turned", "tt_in0", "tt_in1", "q_mm", "q_ok", "u_mm", "u_ok", "s_mm", "s_added", "s_ok", "y_mm", "y_ok"))
            tt_in = [tt_in0, tt_in1]
            bh, kh, v = aa, rkv[:, 8:16, :], rkv[:, 16:24, :]
            HP = PAIRS // 2
            block = s.enter_context(nc.Block())

            @block.sync
            def _(sp):
                t_of = t_scr.rearrange("(j c) h s t -> c h s j t", c=NCH)
                for n in range(4):
                    sp.dma_start(gate_w[:, n, :, :], w_cols(GATE0 + n * P, P)).then_inc(gw_in[n], 16)
                sp.wait_ge(clear, 2)
                for c in range(NCH):
                    if c >= 2:
                        sp.wait_ge(u_mm, 2 * (c - 1))
                    for h in range(2):
                        sp.dma_start(ttx[c % 2][C * h:C * h + C, :, h, :], t_of[c, h, :, :, :]).then_inc(tt_in[c % 2], 16)
                    if c >= 2:
                        n = c - 2
                        sp.wait_ge(g_mm, n + 1)
                        if n + 4 < NCH:
                            sp.dma_start(gate_w[:, n % 4, :, :], w_cols(GATE0 + (n + 4) * P, P)).then_inc(gw_in[n % 4], 16)
                        sp.wait_ge(gate_ok, n + 1)
                        sp.dma_start(gates_scr[:, n, :], gate[:, n % 2, :]).then_inc(gate_out[n % 2], 16)
                for n in range(NCH - 2, NCH):
                    sp.wait_ge(gate_ok, n + 1)
                    sp.dma_start(gates_scr[:, n, :], gate[:, n % 2, :]).then_inc(gate_out[n % 2], 16)
                for n in range(2):
                    sp.wait_ge(gate_out[n], 16 * NCH // 2)

            @block.gpsimd
            def _(pool):
                for u in range(2):
                    nc.gpsimd.memset(ttx[u][:, :, :, :], 0.0)
                    nc.gpsimd.memset(lqx[u][:, :, :, :, :], 0.0)
                    nc.gpsimd.memset(lbx[u][:, :, :], 0.0)
                nc.gpsimd.memset(state[:, :, :], 0.0).then_inc(clear, 1)

            @block.scalar
            def _(act):
                act.wait_ge(clear, 2)

                def spread_chunk(c):
                    if c >= 2:
                        act.wait_ge(y_mm, 2 * (c - 1))
                    x = c % 2
                    for h in range(2):
                        hs = slice(HD * h, HD * h + HD)
                        nc.scalar.activation(lqx[x][hs, :, :, h, :], lq[hs, :, c, :, :], ACT.Copy).then_inc(spread, 1)
                        nc.scalar.activation(scx[x][:, :, :, h, :], sc[:, :, c, :, :], ACT.Copy,
                                             scale=head_is[:, h:h + 1]).then_inc(spread, 1)

                def gate_sigmoid(n):
                    act.wait_ge(g_mm, n + 1)
                    if n >= 2:
                        act.wait_ge(gate_out[n % 2], 16 * (n // 2))
                    nc.scalar.activation(gate[:, n % 2, :], bank[6 + n % 2][:, :], ACT.Sigmoid, bias=col("gate_b", n)).then_inc(gate_ok, 1)

                spread_chunk(0)
                for c in range(NCH):
                    if c + 1 < NCH:
                        spread_chunk(c + 1)
                    for g in range(2):
                        act.wait_ge(u_mm, 2 * c + g + 1)
                        nc.scalar.activation(uv[c % 2][0:2 * C, HP * g:HP * g + HP, :],
                                             bank[2 + g][0:2 * C, 0:HP * HD].rearrange("p (j v) -> p j v", j=HP), ACT.Copy).then_inc(u_ok, 1)
                    if c >= 1:
                        gate_sigmoid(c - 1)
                gate_sigmoid(NCH - 1)

            @block.vector
            def _(dve):
                for q in range(4):
                    nc.vector.memset(head_is[C * q:C * q + C, q % 2:q % 2 + 1], 1.0)
                    last = nc.vector.memset(head_is[C * q:C * q + C, 1 - q % 2:2 - q % 2], 0.0)
                last.then_inc(clear, 1)
                dve.wait_ge(clear, 2)

                def turn_chunk(c):
                    if c >= 2:
                        dve.wait_ge(y_mm, 2 * (c - 1))
                    cs = slice(C * c, C * c + C)
                    for h in range(2):
                        for half in range(2):
                            src = slice(HD * h + C * half, HD * h + C * half + C)
                            to = slice(HD * h + C * half, HD * h + C * half + C)
                            for kind, arr in ((0, bh), (1, kh)):
                                rs = slice(2 * C * kind + C * h, 2 * C * kind + C * h + C)
                                nc.vector.transpose(lbx[c % 2][rs, :, to], arr[src, :, cs]).then_inc(turned, 1)
                            nc.vector.transpose(uv[c % 2][2 * C + C * h:2 * C + C * h + C, :, C * half:C * half + C],
                                                v[src, :, cs]).then_inc(turned, 1)

                turn_chunk(0)
                for c in range(NCH):
                    for g in range(2):
                        js = slice(HP * g, HP * g + HP)
                        dve.wait_ge(q_mm, 2 * c + g + 1)
                        if c >= 1:
                            dve.wait_ge(u_mm, 2 * c - 1 + g)
                        nc.vector.tensor_copy(qs[:, js, :], bank[g][0:2 * C, 0:HP * HD].rearrange("p (j v) -> p j v", j=HP)).then_inc(q_ok, 1)
                    if c + 1 < NCH:
                        turn_chunk(c + 1)
                    for g in range(2):
                        js = slice(HP * g, HP * g + HP)
                        dve.wait_ge(s_mm, 2 * c + g + 1)
                        nc.vector.tensor_tensor(state[:, js, :], state[:, js, :], bank[4 + g][:, 0:HP * HD].rearrange("p (j v) -> p j v", j=HP),
                                                ALU.add).then_inc(s_added, 1)
                        dve.wait_ge(s_added, 2 * c + g + 1)
                        nc.vector.tensor_tensor(state[:, js, :], state[:, js, :],
                                                w_end[:, c, js].unsqueeze(2).to_broadcast([P, HP, HD]), ALU.mult).then_inc(s_ok, 1)
                    for g in range(2):
                        dve.wait_ge(y_mm, 2 * c + g + 1)
                        for h in range(2):
                            for half in range(2):
                                nc.vector.transpose(yT[HD * h + C * half:HD * h + C * half + C, HP * g:HP * g + HP, C * c:C * c + C],
                                                    bank[g][2 * C + C * h:2 * C + C * h + C, 0:HP * HD].rearrange("p (j v) -> p j v", j=HP)[:, :, C * half:C * half + C]).then_inc(y_ok, 1)

            @block.tensor
            def _(pe):
                pe.wait_ge(clear, 2)

                def gate_part(n, ks):
                    if ks[0] == 0:
                        pe.wait_ge(gw_in[n % 4], 16 * (n // 4 + 1))
                        if n >= 2:
                            pe.wait_ge(gate_ok, n - 1)
                    for k in ks:
                        last = nc.tensor.matmul(bank[6 + n % 2][:, :], gate_w[:, n % 4, k, :], xn[:, k, :], start=(k == 0), stop=(k == KT - 1))
                    if ks[-1] == KT - 1:
                        last.then_inc(g_mm, 1)

                for c in range(NCH):
                    x = c % 2
                    pe.wait_ge(spread, 4 * (c + 1))
                    pe.wait_ge(turned, 12 * (c + 1))
                    for g in range(2):
                        if c >= 1:
                            pe.wait_ge(s_ok, 2 * (c - 1) + g + 1)
                            pe.wait_ge(y_ok, 8 * (c - 1) + 4 * g + 4)
                        for n in range(HP):
                            j = HP * g + n
                            cols = slice(HD * n, HD * n + HD)
                            nc.tensor.matmul(bank[g][:, cols], lqx[x][:, j, :, :, :].rearrange("p a h t -> p (a h t)"), state[:, j, :],
                                             start=(n == 0), stop=False, skip_group_check=True)
                            last = nc.tensor.matmul(bank[g][0:2 * C, cols], scx[x][2 * C:P, j, 0, :, :].rearrange("p h t -> p (h t)"),
                                                    uv[x][2 * C:P, j, :], start=False, stop=False, skip_group_check=True)
                        last.then_inc(q_mm, 1)
                    gate_part(c, (0,))
                    pe.wait_ge(tt_in[x], 32 * (c // 2 + 1))
                    for g in range(2):
                        pe.wait_ge(q_ok, 2 * c + g + 1)
                        if c >= 1:
                            pe.wait_ge(u_ok, 2 * (c - 1) + g + 1)
                        for n in range(HP):
                            j = HP * g + n
                            last = nc.tensor.matmul(bank[2 + g][0:2 * C, HD * n:HD * n + HD], ttx[x][:, j, :, :].rearrange("p h t -> p (h t)"),
                                                    qs[:, j, :], start=True, stop=True)
                        last.then_inc(u_mm, 1)
                    gate_part(c, (1,))
                    for g in range(2):
                        pe.wait_ge(u_ok, 2 * c + g + 1)
                        for n in range(HP):
                            j = HP * g + n
                            last = nc.tensor.matmul(bank[4 + g][:, HD * n:HD * n + HD], lbx[x][:, j, :], uv[x][:, j, :], start=True, stop=True)
                        last.then_inc(s_mm, 1)
                        for n in range(HP):
                            j = HP * g + n
                            last = nc.tensor.matmul(bank[g][2 * C:P, HD * n:HD * n + HD], scx[x][:, j, 1, :, :].rearrange("p h t -> p (h t)"),
                                                    uv[x][:, j, :], start=False, stop=True, skip_group_check=True)
                        last.then_inc(y_mm, 1)
                    gate_part(c, (2, 3, 4, 5, 6, 7))


        with ExitStack() as s:
            a = Area(s)
            y_sq, y_rstd = sc_flat[:, 0:4096], sc_flat[:, 4096:8192]
            og = lq_flat[:, 0:4096]
            bonus = rkv[:, 8:16, :].rearrange("p k t -> p (k t)")
            yf = yT.rearrange("p k t -> p (k t)")
            (og_in, mean_mm, centred, sq_ok, var_mm, rstd_ok, scaled, affine, with_bonus, gated, ya_out) = map(
                a.sem, ("og_in", "mean_mm", "centred", "sq_ok", "var_mm", "rstd_ok", "scaled", "affine", "with_bonus", "gated", "ya_out"))
            block = s.enter_context(nc.Block())

            def ts(j):
                return slice(j * T, j * T + T)

            @block.sync
            def _(sp):
                sp.dma_start(og, og_scr).then_inc(og_in, 16)
                sp.dma_start(bonus, bonus_scr).then_inc(og_in, 16)
                sp.wait_ge(gated, KT)
                sp.dma_start(ya_scr, yT).then_inc(ya_out, 16)
                sp.wait_ge(ya_out, 16)

            @block.tensor
            def _(pe):
                for j in range(KT):
                    if j >= 4:
                        pe.wait_ge(centred, j - 3)
                    nc.tensor.matmul(bank[j % 4][:, :], head_ones[:, :], yT[:, j, :], start=True, stop=True).then_inc(mean_mm, 1)
                for j in range(KT):
                    pe.wait_ge(sq_ok, j + 1)
                    if j >= 4:
                        pe.wait_ge(rstd_ok, j - 3)
                    nc.tensor.matmul(bank[4 + j % 4][:, :], head_ones[:, :], y_sq[:, ts(j)], start=True, stop=True).then_inc(var_mm, 1)

            @block.vector
            def _(dve):
                for j in range(KT):
                    dve.wait_ge(mean_mm, j + 1)
                    nc.vector.scalar_tensor_tensor(out=yf[:, ts(j)], in0=bank[j % 4][:, :], scalar=-1.0 / HD, in1=yf[:, ts(j)],
                                                   op0=ALU.mult, op1=ALU.add).then_inc(centred, 1)
                dve.wait_ge(rstd_ok, KT + 1)
                for j in range(KT):
                    nc.vector.tensor_tensor(yf[:, ts(j)], yf[:, ts(j)], y_rstd[:, ts(j)], ALU.mult).then_inc(scaled, 1)
                dve.wait_ge(og_in, 32)
                for j in range(KT):
                    dve.wait_ge(affine, j + 1)
                    nc.vector.tensor_tensor(yf[:, ts(j)], yf[:, ts(j)], bonus[:, ts(j)], ALU.add).then_inc(with_bonus, 1)
                for j in range(KT):
                    dve.wait_ge(with_bonus, j + 1)
                    nc.vector.tensor_tensor(yf[:, ts(j)], yf[:, ts(j)], og[:, ts(j)], ALU.mult).then_inc(gated, 1)

            @block.scalar
            def _(act):
                for j in range(KT):
                    act.wait_ge(centred, j + 1)
                    nc.scalar.activation(y_sq[:, ts(j)], yf[:, ts(j)], ACT.Square).then_inc(sq_ok, 1)
                for j in range(KT):
                    act.wait_ge(var_mm, j + 1)
                    nc.scalar.activation(y_rstd[:, ts(j)], bank[4 + j % 4][:, :], ACT.Ln, scale=1.0 / HD, bias=eps_col[:, 1:2]).then_inc(rstd_ok, 1)
                act.wait_ge(rstd_ok, KT)
                nc.scalar.activation(y_rstd, y_rstd, ACT.Exp, scale=-0.5).then_inc(rstd_ok, 1)
                for j in range(KT):
                    act.wait_ge(scaled, j + 1)
                    nc.scalar.activation(yf[:, ts(j)], yf[:, ts(j)], ACT.Identity, scale=col("lnx_g", j), bias=col("lnx_b", j)).then_inc(affine, 1)
        wkv.close()

        dense = ExitStack()
        d = Area(dense)
        x2T = d.sb("x2T", [P, KT, T])
        with ExitStack() as s:
            a = Area(s)
            xT = x2T
            ring = a.sb("ring", [P, 2, KT, 512])
            hq = a.sb("hq", [P, KT, T])
            ya = a.sb("ya", [P, KT, T])
            yb = a.sb("yb", [P, KT, T])
            gates = a.sb("gates", [P, 16, T])
            merged = a.sb("merged", [P, KT, T])
            kT = a.sb("kT", [P, KT, MEM])
            vm = a.sb("vm", [P, 2, D])
            memT = a.sb("memT", [P, KT, MEM])
            rstd = a.sb("rstd", [P, T])
            prob = a.sb("prob", [P, 2, MEM])
            pT = a.sb("pT", [P, 2, 2, T])
            small = a.sb("small", [P, 4, 16])
            qT, oT, sq = ya, yb, gates[:, 0:8, :]
            mem_tok = pT[:, :, :, :].rearrange("p a b t -> p (a b t)").rearrange("p (i e) -> p i e", i=2)
            names = ("ya_in yb_in gates_in x_in mem_in tile_mm tile_out mem_T memT_ok sq_ok mean_mm ms_ok std_ok "
                     "rstd_ok mn_ok hq_ok gb_ok br_ok s_mm max_ok nmax_ok exp_ok inv_ok p_ok p_T pT_ok o_mm o_out").split()
            S = {n: a.sem(n) for n in names}
            w_loaded = [a.sem("w_loaded0"), a.sem("w_loaded1")]
            MEMK, MEMV, BRA, BRB, MIX, WQ, WO = 0, 2, 4, 6, 8, 10, 12
            block = s.enter_context(nc.Block())
            mm, outn = S["tile_mm"], S["tile_out"]

            @block.sync
            def _(sp):
                sp.dma_start(mem_tok, mem[0, :, :].rearrange("(i p) e -> p i e", p=P)).then_inc(S["mem_in"], 16)
                sp.sem_inc(mm, 8)

                def load(g, slot, dst, src):
                    sp.wait_ge(mm, 4 * g + 4)
                    sp.dma_start(dst, src).then_inc(w_loaded[slot], 16)

                def pairs_of_groups(base, turns, src):
                    with sp.Fori(0, turns) as i:
                        for u in range(2):
                            load(i * 2 + (base + u), u, ring[:, u, :, :], src(i * 1024 + 512 * u).rearrange("(k p) c -> p k c", p=P))

                pairs_of_groups(MEMK, 1, lambda c: wkv_mem[0, :, bass.ds(c, 512)])
                sp.dma_start(ya[:, :, :], ya_scr).then_inc(S["ya_in"], 16)
                sp.dma_start(yb[:, :, :], yb_scr).then_inc(S["yb_in"], 16)
                sp.dma_start(gates[:, :, :], gates_scr).then_inc(S["gates_in"], 16)
                sp.dma_start(xT[:, :, :], x_scr).then_inc(S["x_in"], 16)
                pairs_of_groups(MEMV, 1, lambda c: wkv_mem[0, :, bass.ds(c + D, 512)])
                for base, wt in ((BRA, w_br_a), (BRB, w_br_b), (MIX, w_mix_out), (WQ, wq_mem), (WO, wo_mem)):
                    pairs_of_groups(base, 1, lambda c: wt[0, :, bass.ds(c, 512)])

            def loaded(g):
                return 16 * (g // 2 + 1)

            def bk(g, q):
                return bank[(g % 2) * 4 + q]

            def transpose_probs(pe, n):
                h, i = divmod(n, TT)
                pe.wait_ge(S["p_ok"], n + 1)
                if i == 0 and h >= 1:
                    pe.wait_ge(S["pT_ok"], 2 * h)
                for m in range(2):
                    last = nc.tensor.transpose(bank[2 + m][:, i * P:(i + 1) * P], prob[:, n % 2, m * P:(m + 1) * P], ident[:, :])
                last.then_inc(S["p_T"], 1)

            def values(pe, h):
                pe.wait_ge(S["pT_ok"], 2 * h + 2)
                for e in range(2):
                    if h >= 2:
                        pe.wait_ge(S["o_out"], 2 * (h - 2) + e + 1)
                    for m in range(2):
                        last = nc.tensor.matmul(bank[4 + 2 * (h % 2) + e][:, :], vm[:, m, h * MHD + e * P:h * MHD + (e + 1) * P],
                                                pT[:, h % 2, m, :], start=(m == 0), stop=(m == 1))
                    last.then_inc(S["o_mm"], 1)

            def squares_mem(act):
                for k in range(KT):
                    act.wait_ge(S["memT_ok"], k + 1)
                    nc.scalar.activation(merged[:, k, 0:MEM], memT[:, k, :], ACT.Square).then_inc(S["sq_ok"], 1)

            def out_copy(act, h):
                for e in range(2):
                    act.wait_ge(S["o_mm"], 2 * h + e + 1)
                    nc.scalar.activation(oT[:, 2 * h + e, :], bank[4 + 2 * (h % 2) + e][:, :], ACT.Copy).then_inc(S["o_out"], 1)

            def probs_copy(dve, h):
                dve.wait_ge(S["p_T"], TT * (h + 1))
                if h >= 2:
                    dve.wait_ge(S["o_mm"], 2 * (h - 1))
                for m in range(2):
                    nc.vector.tensor_copy(pT[:, h % 2, m, :], bank[2 + m][:, :]).then_inc(S["pT_ok"], 1)

            @block.tensor
            def _(pe):
                def group(g, act, n=T):
                    u = g % 2
                    pe.wait_ge(w_loaded[u], loaded(g))
                    pe.wait_ge(outn, 4 * g + 4)
                    for q in range(4):
                        for k in range(KT):
                            last = nc.tensor.matmul(bk(g, q)[:, 0:n], ring[:, u, k, q * P:(q + 1) * P], act[:, k, :],
                                                    start=(k == 0), stop=(k == KT - 1))
                        last.then_inc(mm, 1)

                def mean_square(b, src, n, at):
                    for k in range(KT):
                        pe.wait_ge(S["sq_ok"], at + k + 1)
                        last = nc.tensor.matmul(b[:, 0:n], mean_ones[:, :], src[:, k, 0:n], start=(k == 0), stop=(k == KT - 1))
                    last.then_inc(S["mean_mm"], 1)

                pe.wait_ge(S["mem_in"], 16)
                pe.wait_ge(outn, 4 * MEMK + 8)
                for k in range(KT):
                    for i in range(2):
                        last = nc.tensor.transpose(bank[k // 2][:, (k % 2) * MEM + i * P:(k % 2) * MEM + (i + 1) * P],
                                                   mem_tok[:, i, k * P:(k + 1) * P], ident[:, :])
                    last.then_inc(S["mem_T"], 1)
                mean_square(bank[4], merged, MEM, 0)
                pe.wait_ge(S["mn_ok"], KT)
                for u in range(2):
                    group(MEMK + u, memT, MEM)
                for u in range(2):
                    g = MEMV + u
                    pe.wait_ge(w_loaded[u], loaded(g))
                    pe.wait_ge(outn, 4 * g + 4)
                    for m in range(2):
                        for k in range(KT):
                            last = nc.tensor.matmul(bk(g, m)[:, :], memT[:, k, m * P:(m + 1) * P], ring[:, u, k, :],
                                                    start=(k == 0), stop=(k == KT - 1))
                        last.then_inc(mm, (1, 3)[m])
                pe.wait_ge(S["ya_in"], 16)
                for u in range(2):
                    group(BRA + u, ya)
                pe.wait_ge(S["yb_in"], 16)
                for u in range(2):
                    group(BRB + u, yb)
                pe.wait_ge(S["br_ok"], KT)
                for u in range(2):
                    group(MIX + u, merged)
                pe.wait_ge(outn, 4 * MIX + 16)
                mean_square(bank[0], sq, T, KT)
                pe.wait_ge(S["hq_ok"], KT)
                for u in range(2):
                    group(WQ + u, hq)
                pe.wait_ge(outn, 4 * WQ + 16)
                for h in range(MH):
                    for i in range(TT):
                        n = h * TT + i
                        if n >= 2:
                            pe.wait_ge(S["exp_ok"], n - 1)
                        for k in range(2):
                            last = nc.tensor.matmul(bank[n % 2][:, 0:MEM], qT[:, 2 * h + k, i * P:(i + 1) * P], kT[:, 2 * h + k, :],
                                                    start=(k == 0), stop=(k == 1))
                        last.then_inc(S["s_mm"], 1)
                        if n >= 1:
                            transpose_probs(pe, n - 1)
                        if i == 0 and h >= 1:
                            values(pe, h - 1)
                transpose_probs(pe, MH * TT - 1)
                values(pe, MH - 1)
                pe.wait_ge(S["o_out"], 2 * MH)
                for u in range(2):
                    group(WO + u, oT)

            @block.scalar
            def _(act):
                def squares(src, n, wait):
                    for k in range(KT):
                        act.wait_ge(*wait(k))
                        nc.scalar.activation(sq[:, k, 0:n], src[:, k, 0:n], ACT.Square).then_inc(S["sq_ok"], 1)

                act.sem_inc(outn, 8)
                for k in range(KT):
                    act.wait_ge(S["mem_T"], 2 * (k // 2) + 2)
                    nc.scalar.activation(memT[:, k, :], bank[k // 2][:, (k % 2) * MEM:(k % 2) * MEM + MEM], ACT.Copy).then_inc(S["memT_ok"], 1)
                squares_mem(act)
                act.wait_ge(S["ms_ok"], 1)
                nc.scalar.activation(rstd[:, 0:MEM], rstd[:, 0:MEM], ACT.Sqrt).then_inc(S["std_ok"], 1)
                act.wait_ge(outn, 4 * MEMK + 8)
                for u in range(2):
                    for q in range(4):
                        act.wait_ge(mm, 4 * (MEMK + u) + q + 9)
                        nc.scalar.activation(kT[:, 4 * u + q, :], bank[4 * u + q][:, 0:MEM], ACT.Copy).then_inc(outn, 1)
                for u in range(2):
                    for m in range(2):
                        act.wait_ge(mm, 4 * (MEMV + u) + (9, 12)[m])
                        nc.scalar.activation(vm[:, m, u * 512:(u + 1) * 512], bank[4 * u + m][:, :], ACT.Copy).then_inc(outn, (1, 3)[m])
                squares(x2T, T, lambda k: (outn, 4 * MIX + 9 + k))
                act.wait_ge(S["ms_ok"], 2)
                nc.scalar.activation(rstd[:, :], rstd[:, :], ACT.Sqrt).then_inc(S["std_ok"], 1)
                act.wait_ge(outn, 4 * WQ + 8)
                for u in range(2):
                    for q in range(4):
                        act.wait_ge(mm, 4 * (WQ + u) + q + 9)
                        nc.scalar.activation(qT[:, 4 * u + q, :], bank[4 * u + q][:, :], ACT.Copy).then_inc(outn, 1)
                for h in range(MH):
                    for i in range(TT):
                        n = h * TT + i
                        act.wait_ge(S["nmax_ok"], n + 1)
                        if n >= 2:
                            act.wait_ge(S["p_T"], n - 1)
                        nc.scalar.activation(prob[:, n % 2, :], bank[n % 2][:, 0:MEM], ACT.Exp, bias=small[:, 0, n:n + 1], scale=MHD ** -0.5,
                                             accum_out=small[:, 1, n:n + 1]).then_inc(S["exp_ok"], 1)
                        if i == 2 and h >= 1:
                            out_copy(act, h - 1)
                out_copy(act, MH - 1)

            @block.vector
            def _(dve):
                def rms(at, b, n, g, src, dst, done):
                    dve.wait_ge(S["mean_mm"], at)
                    nc.vector.tensor_scalar(rstd[:, 0:n], b[:, 0:n], RMS_EPS, None, ALU.add).then_inc(S["ms_ok"], 1)
                    dve.wait_ge(S["std_ok"], at)
                    nc.vector.reciprocal(rstd[:, 0:n], rstd[:, 0:n]).then_inc(S["rstd_ok"], 1)
                    dve.wait_ge(S["rstd_ok"], at)
                    for k in range(KT):
                        nc.vector.scalar_tensor_tensor(out=dst[:, k, 0:n], in0=src[:, k, 0:n], scalar=col(g, k), in1=rstd[:, 0:n],
                                                       op0=ALU.mult, op1=ALU.mult).then_inc(done, 1)

                dve.wait_ge(S["sq_ok"], KT)
                rms(1, bank[4], MEM, "norm_memkv", memT, memT, S["mn_ok"])
                dve.wait_ge(S["gates_in"], 16)
                dve.wait_ge(outn, 4 * BRA + 8)
                for u in range(2):
                    for q in range(4):
                        dve.wait_ge(mm, 4 * (BRA + u) + q + 9)
                        nc.vector.tensor_tensor(merged[:, 4 * u + q, :], bank[4 * u + q][:, :], gates[:, 4 * u + q, :], ALU.mult).then_inc(outn, 1)
                for u in range(2):
                    for q in range(4):
                        j = 4 * u + q
                        dve.wait_ge(mm, 4 * (BRB + u) + q + 9)
                        nc.vector.tensor_tensor(gates[:, 8 + j, :], bank[4 * u + q][:, :], gates[:, 8 + j, :], ALU.mult).then_inc(outn, 1)
                        dve.wait_ge(outn, 4 * (BRB + u) + q + 9)
                        nc.vector.tensor_tensor(merged[:, j, :], merged[:, j, :], gates[:, 8 + j, :], ALU.add).then_inc(S["br_ok"], 1)
                dve.wait_ge(S["x_in"], 16)
                for u in range(2):
                    for q in range(4):
                        j = 4 * u + q
                        dve.wait_ge(mm, 4 * (MIX + u) + q + 9)
                        nc.vector.tensor_tensor(xT[:, j, :], xT[:, j, :], bank[4 * u + q][:, :], ALU.add).then_inc(outn, 1)
                rms(2, bank[0], T, "norm_memq", xT, hq, S["hq_ok"])
                for h in range(MH):
                    for i in range(TT):
                        n = h * TT + i
                        dve.wait_ge(S["s_mm"], n + 1)
                        nc.vector.reduce_max(small[:, 3, n:n + 1], bank[n % 2][:, 0:MEM], AX.X).then_inc(S["max_ok"], 1)
                        dve.wait_ge(S["max_ok"], n + 1)
                        nc.vector.tensor_scalar(small[:, 0, n:n + 1], small[:, 3, n:n + 1], -(MHD ** -0.5), None, ALU.mult).then_inc(S["nmax_ok"], 1)
                        dve.wait_ge(S["exp_ok"], n + 1)
                        nc.vector.reciprocal(small[:, 2, n:n + 1], small[:, 1, n:n + 1]).then_inc(S["inv_ok"], 1)
                        dve.wait_ge(S["inv_ok"], n + 1)
                        nc.vector.tensor_scalar(prob[:, n % 2, :], prob[:, n % 2, :], small[:, 2, n:n + 1], None, ALU.mult).then_inc(S["p_ok"], 1)
                        if i == 0 and h >= 1:
                            probs_copy(dve, h - 1)
                probs_copy(dve, MH - 1)
                dve.wait_ge(outn, 4 * WO + 8)
                for u in range(2):
                    for q in range(4):
                        j = 4 * u + q
                        dve.wait_ge(mm, 4 * (WO + u) + q + 9)
                        nc.vector.tensor_tensor(xT[:, j, :], xT[:, j, :], bank[4 * u + q][:, :], ALU.add).then_inc(outn, 1)



        Area.recycle()
        moe = d
        x2_tok = moe.sb("x2_tok", [P, TT, D])
        rows_i = moe.sb("rows_i", [P, TT, 2], I32)
        weight = moe.sb("weight", [P, TT, 2])
        most_i = moe.sb("most_i", [P, 1], I32)
        experts = ExitStack()
        weights = Area(experts)
        wg = [weights.sb(f"wg{u}", [P, KT, DE]) for u in range(2)]
        wu = [weights.sb(f"wu{u}", [P, KT, DE]) for u in range(2)]
        wdn = [weights.sb(f"wd{u}", [P, DE // P, D]) for u in range(2)]
        gu_in = [weights.sem("gu_in0"), weights.sem("gu_in1")]
        dn_in = [weights.sem("dn_in0"), weights.sem("dn_in1")]

        def load_weights(sp, e, u):
            for dst, src in ((wg[u], w_e_gate), (wu[u], w_e_up)):
                sp.dma_start(dst[:, :, :], src[0, bass.ds(e, 1), :, :].rearrange("e (k p) f -> p (e k) f", p=P)).then_inc(gu_in[u], 16)
            sp.dma_start(wdn[u][:, :, :], w_e_down[0, bass.ds(e, 1), :, :].rearrange("e (k p) f -> p (e k) f", p=P)).then_inc(dn_in[u], 16)

        with ExitStack() as s:
            a = Area(s)
            hnT = a.sb("hnT", [P, KT, T])
            hn_tok = a.sb("hn_tok", [P, TT, D])
            sq = a.sb("sq", [P, KT, T])
            rstd = a.sb("rstd", [P, T])
            rw = a.sb("rw", [P, KT, NG + NE])
            rb = a.sb("rb", [P, NG + NE])
            ones = a.sb("ones", [P, P])
            rank = a.sb("rank", [P, EPG])
            base = a.sb("base", [P, NE])
            logit = a.sb("logit", [P, TT, NG + NE])
            t4, fg, f1, f2, el, el2, eg = (a.sb(n, [P, TT, EPG]) for n in ("t4", "fg", "f1", "f2", "el", "el2", "eg"))
            mx, mg, m1, m2, gs, e2, den = (a.sb(n, [P, TT, 1]) for n in ("mx", "mg", "m1", "m2", "gs", "e2", "den"))
            t44 = a.sb("t44", [P, TT, NG, EPG])
            one_hot = a.sb("one_hot", [P, 2, TT, NE])
            chosen = a.sb("chosen", [P, TT, NE])
            place = a.sb("place", [P, TT, NE])
            t16 = a.sb("t16", [P, TT, NE])
            rows_f = a.sb("rows_f", [P, TT, 2])
            entry_f = a.sb("entry_f", [P, TT, 2])
            entry_i = a.sb("entry_i", [P, TT, 2], I32)
            expert_no = a.sb("expert_no", [P, NE])
            most = a.sb("most", [P, 1])
            token = a.sb("token", [P, TT], I32)
            zero_i = a.sb("zero_i", [P, NE * T // P], I32)
            names = ("router_in bias_in sq_ok mean_mm ms_ok std_ok rstd_ok hn_ok x_T hn_T x_tok_ok hn_tok_ok logit_mm small_step exp_in exp_ok chosen_ok place_mm "
                     "rows_ok hn_out zero_ok zeroed token_ok scattered consts pool_step").split()
            S = {n: a.sem(n) for n in names}
            block = s.enter_context(nc.Block())

            @block.sync
            def _(sp):
                sp.dma_start(rw[:, :, 0:NG], router_g[0, :, :].rearrange("(k p) c -> p k c", p=P)).then_inc(S["router_in"], 16)
                sp.dma_start(rw[:, :, NG:NG + NE], router_e[0, :, :].rearrange("(k p) c -> p k c", p=P)).then_inc(S["router_in"], 16)
                sp.dma_start(rb[:, 0:NG], router_g_b[0:1, :].to_broadcast([P, NG])).then_inc(S["bias_in"], 16)
                sp.dma_start(rb[:, NG:NG + NE], router_e_b[0:1, :].to_broadcast([P, NE])).then_inc(S["bias_in"], 16)
                sp.wait_ge(S["zero_ok"], 1)
                sp.dma_start(tok_scr.rearrange("(p n) a -> p (n a)", p=P), zero_i[:, :]).then_inc(S["zeroed"], 16)
                for u in range(2):
                    load_weights(sp, u, u)
                sp.wait_ge(S["hn_tok_ok"], KT)
                sp.dma_start(hn_scr.rearrange("(i p) e -> p i e", p=P), hn_tok[:, :, :]).then_inc(S["hn_out"], 16)
                sp.wait_ge(S["hn_out"], 16)

            @block.gpsimd
            def _(pool):
                step = Steps(pool, S["pool_step"])
                step(nc.gpsimd.memset(zero_i[:, :], 0))
                pool.sem_inc(S["zero_ok"], 1)
                step(nc.gpsimd.iota(token[:, :], pattern=[[P, TT]], base=0, channel_multiplier=1))
                pool.wait_ge(S["zeroed"], 16)
                pool.wait_ge(S["rows_ok"], 1)
                for i in range(TT):
                    for n in range(2):
                        nc.gpsimd.indirect_dma_start(tok_scr, bass.IndirectOffsetOnAxis(ap=entry_i[:, i, n:n + 1], axis=0),
                                                     token[:, i:i + 1], None).then_inc(S["scattered"], 16)
                pool.wait_ge(S["scattered"], 16 * 2 * TT)

            @block.scalar
            def _(act):
                for k in range(KT):
                    nc.scalar.activation(sq[:, k, :], x2T[:, k, :], ACT.Square).then_inc(S["sq_ok"], 1)
                act.wait_ge(S["ms_ok"], 1)
                nc.scalar.activation(rstd[:, :], rstd[:, :], ACT.Sqrt).then_inc(S["std_ok"], 1)
                for k in range(KT):
                    act.wait_ge(S["x_T"], k + 1)
                    nc.scalar.activation(x2_tok[:, :, k * P:(k + 1) * P], bank[k % 4][:, :].rearrange("p (i c) -> p i c", i=TT), ACT.Copy).then_inc(S["x_tok_ok"], 1)
                for k in range(KT):
                    act.wait_ge(S["hn_T"], k + 1)
                    nc.scalar.activation(hn_tok[:, :, k * P:(k + 1) * P], bank[k % 4][:, :].rearrange("p (i c) -> p i c", i=TT), ACT.Copy).then_inc(S["hn_tok_ok"], 1)
                act.wait_ge(S["exp_in"], 1)
                nc.scalar.activation(eg[:, :, :], eg[:, :, :], ACT.Exp).then_inc(S["exp_ok"], 1)
                act.wait_ge(S["exp_in"], 2)
                nc.scalar.activation(e2[:, :, :], e2[:, :, :], ACT.Exp).then_inc(S["exp_ok"], 1)

            @block.tensor
            def _(pe):
                for k in range(KT):
                    pe.wait_ge(S["sq_ok"], k + 1)
                    last = nc.tensor.matmul(bank[4][:, :], mean_ones[:, :], sq[:, k, :], start=(k == 0), stop=(k == KT - 1))
                last.then_inc(S["mean_mm"], 1)
                for k in range(KT):
                    if k >= 4:
                        pe.wait_ge(S["x_tok_ok"], k - 3)
                    for i in range(TT):
                        last = nc.tensor.transpose(bank[k % 4][:, i * P:(i + 1) * P], x2T[:, k, i * P:(i + 1) * P], ident[:, :])
                    last.then_inc(S["x_T"], 1)
                pe.wait_ge(S["hn_ok"], KT)
                pe.wait_ge(S["router_in"], 32)
                for i in range(TT):
                    for k in range(KT):
                        last = nc.tensor.matmul(bank[5][:, i * 32:i * 32 + NG + NE], hnT[:, k, i * P:(i + 1) * P], rw[:, k, :],
                                                start=(k == 0), stop=(k == KT - 1))
                last.then_inc(S["logit_mm"], 1)
                for k in range(KT):
                    if k >= 4:
                        pe.wait_ge(S["hn_tok_ok"], k - 3)
                    else:
                        pe.wait_ge(S["x_tok_ok"], k + 5)
                    for i in range(TT):
                        last = nc.tensor.transpose(bank[k % 4][:, i * P:(i + 1) * P], hnT[:, k, i * P:(i + 1) * P], ident[:, :])
                    last.then_inc(S["hn_T"], 1)
                pe.wait_ge(S["chosen_ok"], 1)
                pe.wait_ge(S["consts"], 1)
                for i in range(TT):
                    for m in range(i):
                        nc.tensor.matmul(bank[6][:, i * NE:(i + 1) * NE], ones[:, :], chosen[:, m, :], start=(m == 0), stop=False)
                    nc.tensor.matmul(bank[6][:, i * NE:(i + 1) * NE], earlier[:, :], chosen[:, i, :], start=(i == 0), stop=True)
                for i in range(TT):
                    last = nc.tensor.matmul(bank[7][:, 0:NE], ones[:, :], chosen[:, i, :], start=(i == 0), stop=(i == TT - 1))
                last.then_inc(S["place_mm"], 1)

            @block.vector
            def _(dve):
                step = Steps(dve, S["small_step"])
                nc.vector.memset(ones[:, :], 1.0)
                for n in range(EPG):
                    nc.vector.memset(rank[:, n:n + 1], float(EPG - n))
                for n in range(NE):
                    nc.vector.memset(expert_no[:, n:n + 1], float(n))
                    last = nc.vector.memset(base[:, n:n + 1], float(n * SLOTS))
                last.then_inc(S["consts"], 1)
                dve.wait_ge(S["consts"], 1)
                dve.wait_ge(S["mean_mm"], 1)
                nc.vector.tensor_scalar(rstd[:, :], bank[4][:, :], RMS_EPS, None, ALU.add).then_inc(S["ms_ok"], 1)
                dve.wait_ge(S["std_ok"], 1)
                nc.vector.reciprocal(rstd[:, :], rstd[:, :]).then_inc(S["rstd_ok"], 1)
                dve.wait_ge(S["rstd_ok"], 1)
                for k in range(KT):
                    nc.vector.scalar_tensor_tensor(out=hnT[:, k, :], in0=x2T[:, k, :], scalar=col("norm_ffn", k), in1=rstd[:, :],
                                                   op0=ALU.mult, op1=ALU.mult).then_inc(S["hn_ok"], 1)
                dve.wait_ge(S["logit_mm"], 1)
                dve.wait_ge(S["bias_in"], 32)
                v = nc.vector

                def over(ap, shape):
                    return ap.to_broadcast(shape)

                four = [P, TT, EPG]
                step(v.tensor_tensor(logit[:, :, :], bank[5][:, 0:TT * 32].rearrange("p (i c) -> p i c", i=TT)[:, :, 0:NG + NE],
                                     rb[:, :].unsqueeze(1).to_broadcast([P, TT, NG + NE]), ALU.add))

                def first_max(values, m, hot):
                    step(v.reduce_max(m[:, :, :], values, AX.X))
                    step(v.tensor_tensor(t4[:, :, :], values, over(m[:, :, :], four), ALU.is_equal))
                    step(v.tensor_tensor(t4[:, :, :], t4[:, :, :], rank[:, :].unsqueeze(1).to_broadcast(four), ALU.mult))
                    step(v.reduce_max(mx[:, :, :], t4[:, :, :], AX.X))
                    step(v.tensor_tensor(hot[:, :, :], t4[:, :, :], over(mx[:, :, :], four), ALU.is_equal))

                lg = logit[:, :, 0:NG]
                first_max(lg, mg, fg)
                v.tensor_tensor(eg[:, :, :], lg, over(mg[:, :, :], four), ALU.subtract).then_inc(S["exp_in"], 1)
                step(v.tensor_tensor(t44[:, :, :, :], logit[:, :, NG:NG + NE].rearrange("p i (g e) -> p i g e", g=NG),
                                     fg[:, :, :].unsqueeze(3).to_broadcast([P, TT, NG, EPG]), ALU.mult))
                step(v.tensor_tensor(t44[:, :, 0:2, :], t44[:, :, 0:2, :], t44[:, :, 2:4, :], ALU.add))
                step(v.tensor_tensor(el[:, :, :].unsqueeze(2), t44[:, :, 0:1, :], t44[:, :, 1:2, :], ALU.add))
                first_max(el[:, :, :], m1, f1)
                step(v.scalar_tensor_tensor(out=el2[:, :, :], in0=f1[:, :, :], scalar=-3.0e38, in1=el[:, :, :], op0=ALU.mult, op1=ALU.add))
                first_max(el2[:, :, :], m2, f2)
                v.tensor_tensor(e2[:, :, :], m2[:, :, :], m1[:, :, :], ALU.subtract).then_inc(S["exp_in"], 1)
                for n, f in ((0, f1), (1, f2)):
                    step(v.tensor_tensor(one_hot[:, n, :, :].rearrange("p i (g e) -> p i g e", g=NG),
                                         fg[:, :, :].unsqueeze(3).to_broadcast([P, TT, NG, EPG]),
                                         f[:, :, :].unsqueeze(2).to_broadcast([P, TT, NG, EPG]), ALU.mult))
                v.tensor_tensor(chosen[:, :, :], one_hot[:, 0, :, :], one_hot[:, 1, :, :], ALU.add).then_inc(S["chosen_ok"], 1)
                dve.wait_ge(S["exp_ok"], 2)
                step(v.reduce_sum(gs[:, :, :], eg[:, :, :], AX.X))
                step(v.tensor_scalar(den[:, :, :], e2[:, :, :], 1.0, None, ALU.add))
                step(v.tensor_tensor(den[:, :, :], den[:, :, :], gs[:, :, :], ALU.mult))
                step(v.reciprocal(weight[:, :, 0:1], den[:, :, :]))
                step(v.tensor_tensor(weight[:, :, 1:2], weight[:, :, 0:1], e2[:, :, :], ALU.mult))
                dve.wait_ge(S["place_mm"], 1)
                counted = bank[6][:, 0:TT * NE].rearrange("p (i c) -> p i c", i=TT)
                step(v.tensor_tensor(place[:, :, :], counted, base[:, :].unsqueeze(1).to_broadcast([P, TT, NE]), ALU.add))
                for c in range(1, T // SLOTS):
                    step(v.tensor_scalar(t16[:, :, :], counted, float(c * SLOTS), float((NE - 1) * SLOTS), ALU.is_ge, ALU.mult))
                    step(v.tensor_tensor(place[:, :, :], place[:, :, :], t16[:, :, :], ALU.add))
                for n in range(2):
                    step(v.tensor_tensor(t16[:, :, :], place[:, :, :], one_hot[:, n, :, :], ALU.mult))
                    step(v.reduce_sum(rows_f[:, :, n:n + 1], t16[:, :, :], AX.X))
                step(v.tensor_scalar(t16[:, :, :], bank[6][:, 0:TT * NE].rearrange("p (i c) -> p i c", i=TT), float(NE), None, ALU.mult))
                step(v.tensor_tensor(place[:, :, :], t16[:, :, :], expert_no[:, :].unsqueeze(1).to_broadcast([P, TT, NE]), ALU.add))
                for n in range(2):
                    step(v.tensor_tensor(t16[:, :, :], place[:, :, :], one_hot[:, n, :, :], ALU.mult))
                    step(v.reduce_sum(entry_f[:, :, n:n + 1], t16[:, :, :], AX.X))
                step(v.tensor_copy(entry_i[:, :, :], entry_f[:, :, :]))
                step(v.reduce_max(most[:, :], bank[7][:, 0:NE], AX.X))
                step(v.tensor_copy(most_i[:, :], most[:, :]))
                v.tensor_copy(rows_i[:, :, :], rows_f[:, :, :]).then_inc(S["rows_ok"], 1)
                dve.wait_ge(S["rows_ok"], 1)

        with ExitStack() as s:
            a = Area(s)
            toks = a.sb("toks", [P, NE], I32)
            xg = [a.sb(f"xg{u}", [P, D]) for u in range(2)]
            xgT = [a.sb(f"xgT{u}", [P, KT, SLOTS]) for u in range(2)]
            silu = a.sb("silu", [P, DE])
            hid = [a.sb(f"hid{u}", [P, DE // P, SLOTS]) for u in range(2)]
            y = [a.sb(f"y{u}", [P, D]) for u in range(2)]
            names = ("toks_in gate_mm up_mm down_mm xg_T xgT_ok silu_ok hid_ok y_ok").split()
            S = {n: a.sem(n) for n in names}
            xg_in = [a.sem("xg_in0"), a.sem("xg_in1")]
            y_out = [a.sem("y_out0"), a.sem("y_out1")]
            FT = DE // P
            first_pieces = ExitStack()
            block = first_pieces.enter_context(nc.Block())

            @block.sync
            def _(sp):
                sp.dma_start(toks[:, :], tok_scr[0:SLOTS * NE, :].rearrange("(s e) a -> s (e a)", e=NE)).then_inc(S["toks_in"], 16)

                def store(e, u):
                    sp.dma_start(y_scr[bass.ds(e * SLOTS, SLOTS), :], y[u][:, :]).then_inc(y_out[u], 16)

                with sp.Fori(0, NE // 2 - 1) as i:
                    for u in range(2):
                        sp.wait_ge(S["down_mm"], i * 4 + (2 * u + 6))
                        load_weights(sp, i * 2 + (u + 2), u)
                        sp.wait_ge(S["y_ok"], i * 4 + (2 * u + 6))
                        store(i * 2 + u, u)
                for u in range(2):
                    sp.wait_ge(S["y_ok"], 2 * (NE - 2 + u) + 6)
                    store(NE - 2 + u, u)
                for u in range(2):
                    sp.wait_ge(y_out[u], 16 * (NE // 2 + 1))

            @block.gpsimd
            def _(pool):
                pool.wait_ge(S["toks_in"], 16)
                for e in range(NE):
                    if e >= 2:
                        pool.wait_ge(S["xg_T"], 2 * (e - 1))
                    nc.gpsimd.indirect_dma_start(xg[e % 2][:, :], None, hn_scr, bass.IndirectOffsetOnAxis(ap=toks[:, e:e + 1], axis=0)).then_inc(xg_in[e % 2], 16)

            @block.tensor
            def _(pe):
                def transpose_tokens(u, loaded_at, n2):
                    pe.wait_ge(xg_in[u], loaded_at)
                    pe.wait_ge(S["xgT_ok"], n2)
                    for half in range(2):
                        for k in range(4):
                            last = nc.tensor.transpose(bank[2 + half][:, k * P:(k + 1) * P], xg[u][:, (4 * half + k) * P:(4 * half + k + 1) * P], ident[:, :])
                        last.then_inc(S["xg_T"], 1)

                def gate_up(u, loaded_at, n2):
                    pe.wait_ge(gu_in[u], loaded_at)
                    pe.wait_ge(S["xgT_ok"], n2)
                    for b, wt, done in ((0, wg[u], S["gate_mm"]), (1, wu[u], S["up_mm"])):
                        for f in range(FT):
                            for k in range(KT):
                                last = nc.tensor.matmul(bank[b][:, f * SLOTS:(f + 1) * SLOTS], wt[:, k, f * P:(f + 1) * P], xgT[u][:, k, :],
                                                        start=(k == 0), stop=(k == KT - 1))
                        last.then_inc(done, 1)

                def down(u, loaded_at, hid_at, y_at):
                    pe.wait_ge(dn_in[u], loaded_at)
                    pe.wait_ge(S["hid_ok"], hid_at)
                    pe.wait_ge(S["y_ok"], y_at)
                    for half in range(2):
                        for f in range(FT):
                            last = nc.tensor.matmul(bank[4 + 2 * u + half][:, :], hid[u][:, f, :], wdn[u][:, f, half * 512:(half + 1) * 512],
                                                    start=(f == 0), stop=(f == FT - 1))
                        last.then_inc(S["down_mm"], 1)

                pe.sem_inc(S["down_mm"], 4)
                transpose_tokens(0, 16, 2)
                with pe.Fori(0, NE // 2 - 1) as i:
                    for u in range(2):
                        gate_up(u, i * 32 + 32, i * 4 + (2 * u + 4))
                        transpose_tokens(1 - u, i * 16 + 16 * (u + 1), i * 4 + (2 * u + 4))
                        down(u, i * 16 + 16, i * 2 + (u + 2), i * 4 + (2 * u + 2))
                n = NE // 2 - 1
                gate_up(0, 32 * n + 32, 4 * n + 4)
                transpose_tokens(1, 16 * n + 16, 4 * n + 4)
                down(0, 16 * n + 16, 2 * n + 2, 4 * n + 2)
                gate_up(1, 32 * n + 32, 4 * n + 6)
                down(1, 16 * n + 16, 2 * n + 3, 4 * n + 4)

            @block.scalar
            def _(act):
                act.sem_inc(S["xgT_ok"], 2)

                def tokens_copy(u, n2):
                    for half in range(2):
                        act.wait_ge(S["xg_T"], n2 + half + 1)
                        nc.scalar.activation(xgT[u][:, 4 * half:4 * half + 4, :], bank[2 + half][:, :].rearrange("p (k s) -> p k s", k=4), ACT.Copy).then_inc(S["xgT_ok"], 1)

                def gated(e1):
                    act.wait_ge(S["gate_mm"], e1)
                    act.wait_ge(S["hid_ok"], e1)
                    nc.scalar.activation(silu[:, :], bank[0][:, :], ACT.Silu).then_inc(S["silu_ok"], 1)

                tokens_copy(0, 0)
                with act.Fori(0, NE // 2 - 1) as i:
                    for u in range(2):
                        gated(i * 2 + (u + 1))
                        tokens_copy(1 - u, i * 4 + (2 * u + 2))
                gated(NE - 1)
                tokens_copy(1, 2 * NE - 2)
                gated(NE)

            @block.vector
            def _(dve):
                dve.sem_inc(S["hid_ok"], 1)
                dve.sem_inc(S["y_ok"], 4)
                for u in range(2):
                    dve.sem_inc(y_out[u], 16)
                with dve.Fori(0, NE // 2) as i:
                    for u in range(2):
                        dve.wait_ge(S["silu_ok"], i * 2 + (u + 1))
                        dve.wait_ge(S["up_mm"], i * 2 + (u + 1))
                        dve.wait_ge(S["down_mm"], i * 4 + (2 * u + 2))
                        nc.vector.tensor_tensor(hid[u][:, :, :].rearrange("p f s -> p (f s)"), silu[:, :], bank[1][:, :], ALU.mult).then_inc(S["hid_ok"], 1)
                        dve.wait_ge(y_out[u], i * 16 + 16)
                        for half in range(2):
                            dve.wait_ge(S["down_mm"], i * 4 + (2 * u + half + 5))
                            nc.vector.tensor_copy(y[u][:, half * 512:(half + 1) * 512], bank[4 + 2 * u + half][:, :]).then_inc(S["y_ok"], 1)

            first_pieces.close()

            rest = ExitStack()
            r_ = Area(rest)
            tok1 = r_.sb("tok1", [P, 1], I32)
            names = "piece_done w_in tok_in x_in x_T xT_ok gate_mm up_mm silu_ok hid_ok down_mm y_ok y_out".split()
            R = {n: r_.sem(n) for n in names}
            MORE = T // SLOTS - 1
            block = rest.enter_context(nc.Block())

            def overfull(eng):
                return eng.value_load(most_i[0:1, 0:1], min_val=0, max_val=T) > SLOTS

            @block.sync
            def _(sp):
                with sp.If(overfull(sp)):
                    with sp.Fori(0, NE) as e:
                        for dst, src in ((wg[0], w_e_gate), (wu[0], w_e_up), (wdn[0], w_e_down)):
                            sp.dma_start(dst[:, :, :], src[0, bass.ds(e, 1), :, :].rearrange("e (k p) f -> p (e k) f", p=P)).then_inc(R["w_in"], 16)
                        for c in range(MORE):
                            sp.dma_start(tok1[:, :], tok_scr.rearrange("(s e) a -> s (e a)", e=NE)[SLOTS * (c + 1):SLOTS * (c + 2), bass.ds(e, 1)],
                                         allow_slow_non_contiguous=True).then_inc(R["tok_in"], 16)
                            sp.wait_ge(R["y_ok"], e * MORE + (c + 1))
                            sp.dma_start(y_scr[bass.ds(e * SLOTS + NE * SLOTS * (c + 1), SLOTS), :], y[0][:, :]).then_inc(R["y_out"], 16)
                            sp.wait_ge(R["y_out"], e * (16 * MORE) + 16 * (c + 1))
                            sp.sem_inc(R["piece_done"], 1)

            @block.gpsimd
            def _(pool):
                with pool.If(overfull(pool)):
                    with pool.Fori(0, NE) as e:
                        for c in range(MORE):
                            pool.wait_ge(R["tok_in"], e * (16 * MORE) + 16 * (c + 1))
                            pool.sem_inc(S["toks_in"], 1)
                            nc.gpsimd.indirect_dma_start(xg[0][:, :], None, hn_scr, bass.IndirectOffsetOnAxis(ap=tok1[:, 0:1], axis=0)).then_inc(R["x_in"], 16)

            @block.tensor
            def _(pe):
                with pe.If(overfull(pe)):
                    with pe.Fori(0, NE) as e:
                        for c in range(MORE):
                            m = e * MORE + (c + 1)
                            pe.wait_ge(R["x_in"], e * (16 * MORE) + 16 * (c + 1))
                            for k in range(KT):
                                last = nc.tensor.transpose(bank[2 + k // 4][:, (k % 4) * P:(k % 4 + 1) * P], xg[0][:, k * P:(k + 1) * P], ident[:, :])
                            last.then_inc(R["x_T"], 1)
                            pe.wait_ge(R["w_in"], e * 48 + 48)
                            pe.wait_ge(R["xT_ok"], m)
                            for b, wt, done in ((0, wg[0], R["gate_mm"]), (1, wu[0], R["up_mm"])):
                                for f in range(FT):
                                    for k in range(KT):
                                        last = nc.tensor.matmul(bank[b][:, f * SLOTS:(f + 1) * SLOTS], wt[:, k, f * P:(f + 1) * P], xgT[0][:, k, :],
                                                                start=(k == 0), stop=(k == KT - 1))
                                last.then_inc(done, 1)
                            pe.wait_ge(R["hid_ok"], m)
                            for half in range(2):
                                for f in range(FT):
                                    last = nc.tensor.matmul(bank[4 + half][:, :], hid[0][:, f, :], wdn[0][:, f, half * 512:(half + 1) * 512],
                                                            start=(f == 0), stop=(f == FT - 1))
                            last.then_inc(R["down_mm"], 1)

            @block.scalar
            def _(act):
                with act.If(overfull(act)):
                    with act.Fori(0, NE) as e:
                        for c in range(MORE):
                            m = e * MORE + (c + 1)
                            act.wait_ge(R["x_T"], m)
                            nc.scalar.activation(xgT[0][:, 0:4, :], bank[2][:, :].rearrange("p (k s) -> p k s", k=4), ACT.Copy)
                            nc.scalar.activation(xgT[0][:, 4:8, :], bank[3][:, :].rearrange("p (k s) -> p k s", k=4), ACT.Copy).then_inc(R["xT_ok"], 1)
                            act.wait_ge(R["gate_mm"], m)
                            nc.scalar.activation(silu[:, :], bank[0][:, :], ACT.Silu).then_inc(R["silu_ok"], 1)

            @block.vector
            def _(dve):
                with dve.If(overfull(dve)):
                    with dve.Fori(0, NE) as e:
                        for c in range(MORE):
                            m = e * MORE + (c + 1)
                            dve.wait_ge(R["silu_ok"], m)
                            dve.wait_ge(R["up_mm"], m)
                            nc.vector.tensor_tensor(hid[0][:, :, :].rearrange("p f s -> p (f s)"), silu[:, :], bank[1][:, :], ALU.mult).then_inc(R["hid_ok"], 1)
                            dve.wait_ge(R["down_mm"], m)
                            nc.vector.tensor_copy(y[0][:, 0:512], bank[4][:, :])
                            nc.vector.tensor_copy(y[0][:, 512:1024], bank[5][:, :]).then_inc(R["y_ok"], 1)
            rest.close()
        experts.close()

        with ExitStack() as s:
            a = Area(s)
            picked = a.sb("picked", [P, TT, 2, D])
            gf = a.sb("gf", [P, D])
            sqf = a.sb("sqf", [P, TT, D])
            ssq = a.sb("ssq", [P, TT])
            res = a.sb("res", [P, TT, D])
            names = "gf_in added ssq_ok mean_ok std_ok rstd_ok res_ok out_ok".split()
            S = {n: a.sem(n) for n in names}
            picked_in = [a.sem(f"picked_in{i}") for i in range(TT)]
            block = s.enter_context(nc.Block())

            @block.gpsimd
            def _(pool):
                def pick(written):
                    for i in range(TT):
                        for n in range(2):
                            nc.gpsimd.indirect_dma_start(picked[:, i, n, :], None, y_scr[0:written, :], bass.IndirectOffsetOnAxis(ap=rows_i[:, i, n:n + 1], axis=0)).then_inc(picked_in[i], 16)

                with pool.If(pool.value_load(most_i[0:1, 0:1], min_val=0, max_val=T) > SLOTS):
                    pick(NE * T)
                with pool.Else():
                    pick(NE * SLOTS)

            @block.vector
            def _(dve):
                for i in range(TT):
                    dve.wait_ge(picked_in[i], 32)
                    for n in range(2):
                        nc.vector.scalar_tensor_tensor(out=x2_tok[:, i, :], in0=picked[:, i, n, :], scalar=weight[:, i, n:n + 1], in1=x2_tok[:, i, :],
                                                       op0=ALU.mult, op1=ALU.add).then_inc(S["added"], 1)
                        dve.wait_ge(S["added"], 2 * i + n + 1)
                for i in range(TT):
                    dve.wait_ge(S["ssq_ok"], i + 1)
                    nc.vector.tensor_scalar(ssq[:, i:i + 1], ssq[:, i:i + 1], 1.0 / D, RMS_EPS, ALU.mult, ALU.add).then_inc(S["mean_ok"], 1)
                dve.wait_ge(S["gf_in"], 16)
                for i in range(TT):
                    dve.wait_ge(S["std_ok"], i + 1)
                    nc.vector.reciprocal(ssq[:, i:i + 1], ssq[:, i:i + 1]).then_inc(S["rstd_ok"], 1)
                    dve.wait_ge(S["rstd_ok"], i + 1)
                    nc.vector.scalar_tensor_tensor(out=res[:, i, :], in0=x2_tok[:, i, :], scalar=ssq[:, i:i + 1], in1=gf[:, :],
                                                   op0=ALU.mult, op1=ALU.mult).then_inc(S["res_ok"], 1)

            @block.scalar
            def _(act):
                for i in range(TT):
                    act.wait_ge(S["added"], 2 * i + 2)
                    nc.scalar.activation(sqf[:, i, :], x2_tok[:, i, :], ACT.Square, accum_out=ssq[:, i:i + 1]).then_inc(S["ssq_ok"], 1)
                for i in range(TT):
                    act.wait_ge(S["mean_ok"], i + 1)
                    nc.scalar.activation(ssq[:, i:i + 1], ssq[:, i:i + 1], ACT.Sqrt).then_inc(S["std_ok"], 1)

            @block.sync
            def _(sp):
                sp.dma_start(gf[:, :], norm_f.unsqueeze(0).to_broadcast([P, D])).then_inc(S["gf_in"], 16)
                for i in range(TT):
                    sp.wait_ge(S["res_ok"], i + 1)
                    sp.dma_start(out[0, i * P:(i + 1) * P, :], res[:, i, :]).then_inc(S["out_ok"], 16)
                sp.wait_ge(S["out_ok"], 16 * TT)
        nc.clear_and_free_semaphores(Area.sems)
        dense.close()


_INS = ("x mem norm_mix w_in mu_in w0 w_decay_up a0 w_aaa_up w_gate_up k_k k_a r_k lnx_g lnx_b conv_w gate_b w_br_a w_br_b "
        "w_mix_out norm_memq norm_memkv wq_mem wkv_mem wo_mem norm_ffn router_g router_g_b router_e router_e_b w_e_gate "
        "w_e_up w_e_down norm_f").split()


def kernel(**inputs):
    import numpy as _np
    import concourse.bacc as _bacc
    from concourse import mybir as _mybir
    from concourse.bass_utils import run_bass_kernel_spmd as _run

    nc = _bacc.Bacc("TRN2", target_bir_lowering=False, num_devices=1)
    arrays, args = {}, []
    for name in _INS:
        a = _np.ascontiguousarray(inputs[name])
        arrays[f"in_{name}"] = a
        args.append(nc.dram_tensor(f"in_{name}", a.shape, _mybir.dt.from_np(a.dtype), kind="ExternalInput").ap())
    args.append(nc.dram_tensor("out", (1, T, D), F32, kind="ExternalOutput").ap())
    build_trunk(nc, *args)
    r = _run(nc, [arrays], core_ids=[0])
    return r.results[0]["out"]
```

```python
import concourse.bass as bass
from concourse import mybir
from contextlib import ExitStack

F32 = mybir.dt.float32
I32 = mybir.dt.int32
F32R = mybir.dt.float32r
ALU = mybir.AluOpType
ACT = mybir.ActivationFunctionType
AX = mybir.AxisListType

P = 128
D = 1024
T = 512
KT = D // P
TT = T // P
HEADS, HD = 16, 64
PAIRS = HEADS // 2
C = 32
NCH = T // C
MEM = 256
MH, MHD = 4, 256
NG, EPG = 4, 4
NE = NG * EPG
DE = 512
SLOTS = P
RMS_EPS, LNX_EPS = 1e-6, 64e-5
EXP_M_HALF = 0.6065306597126334

RW_COLS = 3 * D + 64 + 64 + 160
CONV0 = RW_COLS
GATE0 = RW_COLS + 3 * D


class Steps:

    def __init__(self, eng, sem):
        self.eng, self.sem, self.n, self.i, self.per = eng, sem, 0, None, 0

    def value(self):
        return self.n if self.i is None else self.i * self.per + self.n

    def __call__(self, ins):
        ins.then_inc(self.sem, 1)
        self.n += 1
        self.eng.wait_ge(self.sem, self.value())

    def last(self, ins):
        ins.then_inc(self.sem, 1)
        self.n += 1

    def wait(self):
        self.eng.wait_ge(self.sem, self.value())

    def enter(self, i, per):
        self.i, self.per, self.base = i, per, self.n

    def leave(self, turns):
        assert self.n - self.base == self.per, (self.n - self.base, self.per)
        self.n, self.i = self.base + turns * self.per, None


def build_trunk(nc, x, mem, norm_mix, w_in, mu_in, w0, w_decay_up, a0, w_aaa_up, w_gate_up, k_k, k_a, r_k,
                lnx_g, lnx_b, conv_w, gate_b, w_br_a, w_br_b, w_mix_out, norm_memq, norm_memkv, wq_mem,
                wkv_mem, wo_mem, norm_ffn, router_g, router_g_b, router_e, router_e_b, w_e_gate, w_e_up,
                w_e_down, norm_f, out):
    whole = ExitStack()

    def dram(name, shape, dt=F32):
        return nc.dram_tensor(name, shape, dt).ap()

    x_scr = dram("x_scr", [P, KT, T])
    og_scr = dram("og_scr", [P, KT, T])
    bonus_scr = dram("bonus_scr", [P, KT, T])
    yb_scr = dram("yb_scr", [P, KT, T])
    gates_scr = dram("gates_scr", [P, 2 * KT, T])
    kv_scr = dram("kv_scr", [P, KT * MEM + 2 * D])
    m_scr = dram("m_scr", [PAIRS * NCH, 2, C, C])
    t_scr = dram("t_scr", [PAIRS * NCH, 2, C, C])
    hn_scr = dram("hn_scr", [T, D])
    tok_scr = dram("tok_scr", [NE * T, 1], I32)
    y_scr = dram("y_scr", [NE * T, D])

    with whole:
        class Area:

            parts = 0
            sems = []

            @staticmethod
            def recycle():
                nc.clear_and_free_semaphores(Area.sems)
                nc.all_engine_barrier()
                Area.sems = []

            def __init__(self, stack):
                self.stack = stack
                Area.parts += 1
                self.part = Area.parts

            def sb(self, name, shape, dt=F32):
                return self.stack.enter_context(nc.sbuf_tensor(f"{name}_{self.part}", shape, dt))

            def sem(self, name):
                sem = nc.alloc_semaphore(f"{name}_{self.part}")
                Area.sems.append(sem)
                return sem

        top = Area(whole)
        bank = [whole.enter_context(nc.psum_tensor(f"bank{i}", [P, 512], F32)) for i in range(8)]
        ident = top.sb("ident", [P, P])
        mean_ones = top.sb("mean_ones", [P, P])
        head_ones = top.sb("head_ones", [P, P])
        earlier = top.sb("earlier", [P, P])
        pcol = top.sb("pcol", [P, 256])
        rkv = top.sb("rkv", [P, 24, T])
        eps_col = top.sb("eps_col", [P, 2])
        one_minus_mu = top.sb("one_minus_mu", [P, 27])
        one_minus_ka = top.sb("one_minus_ka", [P, KT])

        rows, where = [], {}

        def param(name, ap, n, tile):
            at = sum(r[2] for r in rows if r[3] == tile)
            rows.append((name, ap, n, tile, at))
            where[name] = tile * P + at

        def flat(ap):
            return ap.rearrange("(j p) -> j p", p=P)

        param("mu", flat(mu_in[0, 0:3328]), 26, 0)
        param("norm_mix", flat(norm_mix[0, :]), 8, 0)
        param("w0", flat(w0[0, :]), 8, 0)
        param("a0", flat(a0[0, :]), 8, 0)
        param("k_k", flat(k_k[0, :]), 8, 0)
        param("k_a", flat(k_a[0, :]), 8, 0)
        param("r_k", r_k[0, :, :].rearrange("(j h) n -> j (h n)", h=2), 8, 0)
        param("lnx_g", flat(lnx_g[0, :]), 8, 0)
        param("lnx_b", flat(lnx_b[0, :]), 8, 0)
        param("conv_w", conv_w[0, :, :].rearrange("c (j p) -> (c j) p", p=P), 24, 0)
        param("norm_ffn", flat(norm_ffn[0, :]), 8, 0)
        param("gate_b", flat(gate_b[0, :]), 16, 1)
        param("norm_memq", flat(norm_memq[0, :]), 8, 1)
        param("norm_memkv", flat(norm_memkv[0, :]), 8, 1)
        where["mu_g1"] = P + 32

        def col(name, j=0, n=1):
            at = where[name]
            return pcol[:, bass.ds(at + j, n)]

        wkv = ExitStack()
        w = Area(wkv)
        aa = w.sb("aa", [P, KT, T])
        w_end = w.sb("w_end", [P, NCH, PAIRS])
        xn = w.sb("xn", [P, KT, T])
        proj = ExitStack()
        pj = Area(proj)
        w_raw = pj.sb("w_raw", [P, KT, 512])
        xn_hi = pj.sb("xn_hi", [P, KT, T], F32R)
        xn_lo = pj.sb("xn_lo", [P, KT, T], F32R)
        w_hi = pj.sb("w_hi", [P, 8, KT, P], F32R)
        w_lo = pj.sb("w_lo", [P, 8, KT, P], F32R)
        w_loaded = pj.sem("w_loaded")
        shift_in = aa[:, 5:8, :]

        def w_cols(c0, n):
            return w_in[0, :, bass.ds(c0, n)].rearrange("(k p) c -> p k c", p=P)

        with ExitStack() as s:
            a = Area(s)
            x_tok = rkv[:, 0:8, :].rearrange("p k t -> p (k t)").rearrange("p (i e) -> p i e", i=TT)
            prow = a.sb("prow", [P, 2, P])
            xT, sq, rstd = rkv[:, 8:16, :], rkv[:, 16:24, :], aa[:, 0, :]
            const_step, consts, prow_clear, prow_in, x_in = map(a.sem, ("const_step", "consts", "prow_clear", "prow_in", "x_in"))
            pcol_T, x_T, x_out, sq_ok, mean_ok, dve_step, xn_ok, stored, std_ok, xn_hi_ok = map(
                a.sem, ("pcol_T", "x_T", "x_out", "sq_ok", "mean_ok", "dve_step", "xn_ok", "stored", "std_ok", "xn_hi_ok"))
            block = s.enter_context(nc.Block())

            @block.gpsimd
            def _(pool):
                step = Steps(pool, const_step)
                step(nc.gpsimd.memset(ident[:, :], 0.0))
                step(nc.gpsimd.affine_select(out=ident[:, :], in_=ident[:, :], compare_op=ALU.not_equal, fill=1.0,
                                             base=0, pattern=[[-1, P]], channel_multiplier=1))
                step(nc.gpsimd.memset(earlier[:, :], 0.0))
                step(nc.gpsimd.affine_select(out=earlier[:, :], in_=earlier[:, :], compare_op=ALU.is_ge, fill=1.0,
                                             base=0, pattern=[[-1, P]], channel_multiplier=1))
                step(nc.gpsimd.memset(mean_ones[:, :], 1.0 / D))
                step(nc.gpsimd.memset(head_ones[:, :], 0.0))
                step(nc.gpsimd.memset(head_ones[0:HD, 0:HD], 1.0))
                nc.gpsimd.memset(head_ones[HD:P, HD:P], 1.0).then_inc(consts, 1)

            @block.sync
            def _(sp):
                sp.dma_start(x_tok[:, :, :], x[0, :, :].rearrange("(i p) d -> p i d", p=P)).then_inc(x_in, 16)
                sp.wait_ge(prow_clear, 1)
                for name, ap, n, tile, at in rows:
                    sp.dma_start(prow[at:at + n, tile, :], ap).then_inc(prow_in, 16)
                sp.dma_start(prow[32:33, 1, 0:32], mu_in[0:1, 3328:3360]).then_inc(prow_in, 16)
                sp.dma_start(w_raw[:, :, :], w_cols(0, 512)).then_inc(w_loaded, 16)
                sp.wait_ge(x_out, KT)
                sp.dma_start(x_scr, xT[:, :, :]).then_inc(stored, 16)
                sp.wait_ge(stored, 16)

            @block.tensor
            def _(pe):
                pe.wait_ge(consts, 1)
                pe.wait_ge(prow_in, 16 * (len(rows) + 1))
                for i in range(2):
                    nc.tensor.transpose(bank[5][:, i * P:(i + 1) * P], prow[:, i, :], ident[:, :]).then_inc(pcol_T, 1)
                pe.wait_ge(x_in, 16)
                for k in range(KT):
                    if k >= 4:
                        pe.wait_ge(x_out, k - 3)
                        pe.wait_ge(sq_ok, k - 3)
                    for i in range(TT):
                        last = nc.tensor.transpose(bank[k % 4][:, i * P:(i + 1) * P],
                                                   x_tok[:, i, k * P:(k + 1) * P], ident[:, :])
                    last.then_inc(x_T, 1)
                for k in range(KT):
                    pe.wait_ge(sq_ok, k + 1)
                    last = nc.tensor.matmul(bank[4][:, :], mean_ones[:, :], sq[:, k, :], start=(k == 0), stop=(k == KT - 1))
                last.then_inc(mean_ok, 1)

            @block.scalar
            def _(act):
                for k in range(KT):
                    act.wait_ge(x_T, k + 1)
                    nc.scalar.activation(xT[:, k, :], bank[k % 4][:, :], ACT.Copy).then_inc(x_out, 1)
                    nc.scalar.activation(sq[:, k, :], bank[k % 4][:, :], ACT.Square).then_inc(sq_ok, 1)
                act.wait_ge(dve_step, 5)
                nc.scalar.activation(rstd[:, :], rstd[:, :], ACT.Sqrt).then_inc(std_ok, 1)
                for k in range(KT):
                    act.wait_ge(xn_ok, k + 1)
                    nc.scalar.activation(xn_hi[:, k, :], xn[:, k, :], ACT.Copy).then_inc(xn_hi_ok, 1)

            @block.vector
            def _(dve):
                step = Steps(dve, dve_step)
                nc.vector.memset(prow[:, :, :], 0.0).then_inc(prow_clear, 1)
                nc.vector.memset(eps_col[:, 0:1], RMS_EPS)
                nc.vector.memset(eps_col[:, 1:2], LNX_EPS)
                dve.wait_ge(pcol_T, 2)
                step(nc.vector.tensor_copy(pcol[:, :], bank[5][:, 0:256]))
                step(nc.vector.tensor_scalar(one_minus_mu[:, 0:26], pcol[:, 0:26], -1.0, 1.0, ALU.mult, ALU.add))
                step(nc.vector.tensor_scalar(one_minus_mu[:, 26:27], col("mu_g1"), -1.0, 1.0, ALU.mult, ALU.add))
                step(nc.vector.tensor_scalar(one_minus_ka[:, :], col("k_a", 0, 8), -1.0, 1.0, ALU.mult, ALU.add))
                dve.wait_ge(mean_ok, 1)
                step(nc.vector.tensor_scalar(rstd[:, :], bank[4][:, :], RMS_EPS, None, ALU.add))
                dve.wait_ge(x_out, KT)
                dve.wait_ge(std_ok, 1)
                step(nc.vector.reciprocal(rstd[:, :], rstd[:, :]))
                for k in range(KT):
                    nc.vector.scalar_tensor_tensor(out=xn[:, k, :], in0=xT[:, k, :], scalar=col("norm_mix", k), in1=rstd[:, :],
                                                   op0=ALU.mult, op1=ALU.mult).then_inc(xn_ok, 1)
                for k in range(KT):
                    dve.wait_ge(xn_hi_ok, k + 1)
                    nc.vector.tensor_tensor(xn_lo[:, k, :], xn[:, k, :], xn_hi[:, k, :].bitcast(F32), ALU.subtract)

        with ExitStack() as s:
            a = Area(s)
            mm_ok, part1, shifted, w_hi_ok, w_lo_ok = map(a.sem, ("mm_ok", "part1", "shifted", "w_hi_ok", "w_lo_ok"))
            block = s.enter_context(nc.Block())
            GROUPS = 3 * D // 512
            WIDTH = (P, P, 32)

            @block.sync
            def _(sp):
                with sp.Fori(0, GROUPS - 1) as i:
                    sp.wait_ge(w_lo_ok, i * 4 + 4)
                    sp.dma_start(w_raw[:, :, :], w_cols(i * 512 + 512, 512)).then_inc(w_loaded, 16)
                sp.wait_ge(w_lo_ok, 4 * GROUPS)
                sp.dma_start(w_raw[:, :, 0:288], w_cols(3 * D, 288)).then_inc(w_loaded, 16)

            @block.tensor
            def _(pe):
                def tile(slot, q, n=P):
                    for k in range(KT):
                        nc.tensor.matmul(bank[q][0:n, :], w_hi[:, slot, k, 0:n], xn_hi[:, k, :], start=(k == 0), stop=False)
                        nc.tensor.matmul(bank[q][0:n, :], w_hi[:, slot, k, 0:n], xn_lo[:, k, :], start=False, stop=False)
                        last = nc.tensor.matmul(bank[q][0:n, :], w_lo[:, slot, k, 0:n], xn_hi[:, k, :], start=False, stop=(k == KT - 1))
                    last.then_inc(mm_ok, 1)

                with pe.Fori(0, GROUPS // 2) as i:
                    for u in range(2):
                        for q in range(4):
                            pe.wait_ge(w_lo_ok, i * 8 + 4 * u + q + 1)
                            pe.wait_ge(shifted, i * 8 + 4 * u + q + 1)
                            tile(4 * u + q, q)
                for q in range(3):
                    pe.wait_ge(w_lo_ok, 24 + q + 1)
                    pe.wait_ge(shifted, 24 + q + 1)
                    tile(q, q, WIDTH[q])

            @block.scalar
            def _(act):
                def high_weights(u, loaded_at, widths=(P, P, P, P)):
                    act.wait_ge(w_loaded, loaded_at)
                    for q, n in enumerate(widths):
                        nc.scalar.activation(w_hi[:, 4 * u + q, :, 0:n], w_raw[:, :, q * P:q * P + n], ACT.Copy).then_inc(w_hi_ok, 1)

                def shift_group(n0):
                    for q in range(4):
                        act.wait_ge(mm_ok, n0 + (q + 1))
                        nc.scalar.activation(rkv[:, bass.ds(n0 + q, 1), :], bank[q][:, :].rearrange("p (a t) -> p a t", a=1), ACT.Copy,
                                             scale=one_minus_mu[:, bass.ds(n0 + q, 1)]).then_inc(part1, 1)

                high_weights(0, 16)
                high_weights(1, 32)
                with act.Fori(0, GROUPS // 2 - 1) as i:
                    for u in range(2):
                        shift_group(i * 8 + 4 * u)
                        high_weights(u, i * 32 + (48 + 16 * u))
                shift_group(16)
                high_weights(0, 16 * (GROUPS + 1), WIDTH)
                shift_group(20)
                for q, n in enumerate(WIDTH):
                    act.wait_ge(mm_ok, 24 + q + 1)
                    nc.scalar.activation(shift_in[0:n, q, :], bank[q][0:n, :], ACT.Copy,
                                         scale=one_minus_mu[0:n, 24 + q:25 + q]).then_inc(part1, 1)

            @block.vector
            def _(dve):
                def low_weights(u, at, widths=(P, P, P, P)):
                    for q, n in enumerate(widths):
                        dve.wait_ge(w_hi_ok, at + (q + 1))
                        nc.vector.tensor_tensor(w_lo[:, 4 * u + q, :, 0:n], w_raw[:, :, q * P:q * P + n],
                                                w_hi[:, 4 * u + q, :, 0:n].bitcast(F32), ALU.subtract).then_inc(w_lo_ok, 1)

                def shift_group(n0):
                    for q in range(4):
                        dve.wait_ge(part1, n0 + (q + 1))
                        later = rkv[:, bass.ds(n0 + q, 1), 1:T]
                        nc.vector.scalar_tensor_tensor(out=later, in0=bank[q][:, 0:T - 1].rearrange("p (a t) -> p a t", a=1),
                                                       scalar=pcol[:, bass.ds(n0 + q, 1)], in1=later,
                                                       op0=ALU.mult, op1=ALU.add).then_inc(shifted, 1)

                dve.sem_inc(shifted, 4)
                low_weights(0, 0)
                low_weights(1, 4)
                with dve.Fori(0, GROUPS // 2 - 1) as i:
                    for u in range(2):
                        shift_group(i * 8 + 4 * u)
                        low_weights(u, i * 8 + (8 + 4 * u))
                shift_group(16)
                low_weights(0, 24, WIDTH)
                shift_group(20)
                for q, n in enumerate(WIDTH):
                    dve.wait_ge(part1, 24 + q + 1)
                    mu = pcol[0:n, 24 + q:25 + q] if q < 2 else pcol[0:n, where["mu_g1"]:where["mu_g1"] + 1]
                    nc.vector.scalar_tensor_tensor(out=shift_in[0:n, q, 1:T], in0=bank[q][0:n, 0:T - 1], scalar=mu,
                                                   in1=shift_in[0:n, q, 1:T], op0=ALU.mult, op1=ALU.add).then_inc(shifted, 1)
        proj.close()

        lq = w.sb("lq", [P, PAIRS, NCH, 2, C])
        sc = w.sb("sc", [P, PAIRS, NCH, 2, C])
        lq_flat = lq[:, :, :, :, :].rearrange("p j c a t -> p (j c a t)")
        sc_flat = sc[:, :, :, :, :].rearrange("p j c a t -> p (j c a t)")
        early = ExitStack()
        decay = early.enter_context(nc.sbuf_tensor("decay", [P, KT, T], F32))

        with ExitStack() as s0:
            with ExitStack() as s:
                a = Area(s)
                lora = sc_flat[:, 0:3 * T].rearrange("p (k t) -> p k t", k=3)
                og = lq_flat[:, 0:KT * T].rearrange("p (k t) -> p k t", k=KT)
                up_da = lq_flat[:, 4096:4096 + D]
                up_g = lq_flat[:, 4096 + D:4096 + 3 * D].rearrange("p (k d) -> p k d", k=2)
                up_in, lora_act, up_ok, up_out, og_out, og_st = map(a.sem, ("up_in", "lora_act", "up_ok", "up_out", "og_out", "og_st"))
                block = s.enter_context(nc.Block())

                @block.sync
                def _(sp):
                    sp.dma_start(up_da[0:64, :], w_decay_up[0, :, :]).then_inc(up_in, 16)
                    sp.dma_start(up_da[64:128, :], w_aaa_up[0, :, :]).then_inc(up_in, 16)
                    sp.dma_start(up_g[:, 0, :], w_gate_up[0, 0:128, :]).then_inc(up_in, 16)
                    sp.dma_start(up_g[0:32, 1, :], w_gate_up[0, 128:160, :]).then_inc(up_in, 16)
                    sp.wait_ge(og_out, KT)
                    sp.dma_start(og_scr, og[:, :, :]).then_inc(og_st, 16)
                    sp.wait_ge(og_st, 16)

                @block.tensor
                def _(pe):
                    pe.wait_ge(up_in, 64)
                    pe.wait_ge(lora_act, 4)
                    for j in range(KT):
                        cs = slice(j * P, (j + 1) * P)
                        for q in range(3):
                            n = 3 * j + q
                            b = bank[4 + n % 4]
                            if n >= 4:
                                pe.wait_ge(up_out, n - 3)
                            if q < 2:
                                rs = slice(64 * q, 64 * q + 64)
                                nc.tensor.matmul(b[:, :], up_da[rs, cs], lora[rs, 0, :], start=True, stop=True).then_inc(up_ok, 1)
                            else:
                                nc.tensor.matmul(b[:, :], up_g[:, 0, cs], lora[:, 1, :], start=True, stop=False)
                                nc.tensor.matmul(b[:, :], up_g[0:32, 1, cs], lora[0:32, 2, :], start=False, stop=True).then_inc(up_ok, 1)

                @block.scalar
                def _(act):
                    nc.scalar.activation(lora[0:64, 0, :], shift_in[0:64, 0, :], ACT.Tanh).then_inc(lora_act, 1)
                    nc.scalar.activation(lora[64:128, 0, :], shift_in[64:128, 0, :], ACT.Copy).then_inc(lora_act, 1)
                    nc.scalar.activation(lora[:, 1, :], shift_in[:, 1, :], ACT.Sigmoid).then_inc(lora_act, 1)
                    nc.scalar.activation(lora[0:32, 2, :], shift_in[0:32, 2, :], ACT.Sigmoid).then_inc(lora_act, 1)
                    for j in range(KT):
                        act.wait_ge(up_ok, 3 * j + 1)
                        nc.scalar.activation(decay[:, j, :], bank[4 + (3 * j) % 4][:, :], ACT.Sigmoid, bias=col("w0", j)).then_inc(up_out, 1)
                        act.wait_ge(up_ok, 3 * j + 2)
                        nc.scalar.activation(aa[:, j, :], bank[4 + (3 * j + 1) % 4][:, :], ACT.Sigmoid, bias=col("a0", j)).then_inc(up_out, 1)
                        act.wait_ge(up_ok, 3 * j + 3)
                        nc.scalar.activation(og[:, j, :], bank[4 + (3 * j + 2) % 4][:, :], ACT.Copy).then_inc(up_out, 1)
                    act.wait_ge(up_out, 3 * KT)
                    nc.scalar.sem_inc(og_out, KT)


            with ExitStack() as s:
                a = Area(s)
                not_first = a.sb("not_first", [P, T])
                causal = a.sb("causal", [P, 2, C])
                kk0, ssq, ka, w_cum, w_inv, rk, w_log, bonus, conv_y = (
                    a.sb(n, [P, T]) for n in ("kk0", "ssq", "ka", "w_cum", "w_inv", "rk", "w_log", "bonus", "conv_y"))
                sq, kb, conv_x = ssq, w_log, conv_y
                conv_u = a.sb("conv_u", [P, T + 2])
                conv_w3 = a.sb("conv_w3", [P, 3, KT, P])
                lb = a.sb("lb", [P, NCH, 2, 2, C])
                bh, kh = aa, rkv[:, 8:16, :]
                cw_in = [a.sem(f"cw_in{q}") for q in range(3)]
                (bonus_out, yb_out, cx_mm, cc_mm, cb_mm, cx_ok, u_ok, c1_ok, c2_ok, c3_ok, yb_ok, yb_free) = map(
                    a.sem, ("bonus_out", "yb_out", "cx_mm", "cc_mm", "cb_mm", "cx_ok", "u_ok", "c1_ok", "c2_ok", "c3_ok", "yb_ok", "yb_free"))
                (cs, masks_ok, lb_clear, kk0_ok, sq_ok, ka_ok, ssq_mm, ssq_ok, norm_ok, wlog_ok, winv_used, wcum_ok, winv_ok,
                 km_ok, kk_ok, rk_ok, rksum_mm, lq_ok, kb_ok, bh_ok, kh_ok, bonus_ok, wend_ok, lb_ok, sc_mm, sc_ok, spread_begun) = map(
                    a.sem, ("cs", "masks_ok", "lb_clear", "kk0_ok", "sq_ok", "ka_ok", "ssq_mm", "ssq_ok", "norm_ok", "wlog_ok",
                            "winv_used", "wcum_ok", "winv_ok", "km_ok", "kk_ok", "rk_ok", "rksum_mm", "lq_ok", "kb_ok", "bh_ok",
                            "kh_ok", "bonus_ok", "wend_ok", "lb_ok", "sc_mm", "sc_ok", "spread_begun"))
                block = s.enter_context(nc.Block())

                def tile(arr, j):
                    return arr[:, bass.ds(j, 1), :].rearrange("p a t -> p (a t)")

                def chunks(ap):
                    return ap.rearrange("p (c t) -> p c t", c=NCH)

                @block.sync
                def _(sp):
                    def conv_weights(j, q):
                        src = (0, 2, 1)[q] * D + CONV0
                        sp.dma_start(conv_w3[:, q, :, :], w_cols(j * P + src, P)).then_inc(cw_in[q], 16)

                    sp.sem_inc(bonus_out, 16)
                    sp.sem_inc(yb_out, 16)
                    for q in range(3):
                        conv_weights(0, q)
                    with sp.Fori(0, PAIRS - 1) as j:
                        for q, used in enumerate((cx_mm, cc_mm, cb_mm)):
                            sp.wait_ge(used, j + 1)
                            conv_weights(j + 1, q)
                        sp.wait_ge(bonus_ok, j + 2)
                        sp.dma_start(bonus_scr[:, bass.ds(j, 1), :], bonus[:, :].unsqueeze(1)).then_inc(bonus_out, 16)
                        sp.wait_ge(yb_ok, j + 1)
                        sp.dma_start(yb_scr[:, bass.ds(j, 1), :], conv_y[:, :].unsqueeze(1)).then_inc(yb_out, 16)
                    sp.wait_ge(bonus_ok, PAIRS + 1)
                    sp.dma_start(bonus_scr[:, PAIRS - 1, :], bonus[:, :]).then_inc(bonus_out, 16)
                    sp.wait_ge(yb_ok, PAIRS)
                    sp.dma_start(yb_scr[:, PAIRS - 1, :], conv_y[:, :]).then_inc(yb_out, 16)
                    sp.wait_ge(bonus_out, 16 * (PAIRS + 1))
                    sp.wait_ge(yb_out, 16 * (PAIRS + 1))

                @block.gpsimd
                def _(pool):
                    step = Steps(pool, cs)
                    step(nc.gpsimd.memset(not_first[:, :], 1.0))
                    step(nc.gpsimd.memset(chunks(not_first[:, :])[:, :, 0:1], 0.0))
                    for q in range(4):
                        qs = slice(C * q, C * q + C)
                        step(nc.gpsimd.tensor_copy(causal[qs, 0, :], earlier[qs, qs]))
                        step(nc.gpsimd.tensor_tensor(causal[qs, 1, :], earlier[qs, qs], ident[qs, qs], ALU.add))
                    nc.gpsimd.memset(lb[:, :, :, :, :], 0.0).then_inc(lb_clear, 1)
                    with pool.Fori(0, PAIRS) as j:
                        pool.wait_ge(norm_ok, 2 * j + 2)
                        nc.gpsimd.tensor_tensor(kk0[:, :], kk0[:, :], ssq[:, :], ALU.mult).then_inc(kk_ok, 1)

                @block.scalar
                def _(act):
                    with act.Fori(0, PAIRS) as j:
                        act.wait_ge(kk_ok, j + 1)
                        act.wait_ge(bh_ok, j + 1)
                        act.wait_ge(lb_clear, 2)
                        nc.scalar.activation(kk0[:, :], tile(rkv, j + 8), ACT.Copy, scale=col("k_k", j)).then_inc(kk0_ok, 1)
                        act.wait_ge(kk0_ok, j + 1)
                        nc.scalar.activation(sq[:, :], kk0[:, :], ACT.Square).then_inc(sq_ok, 1)
                        act.wait_ge(wlog_ok, j + 1)
                        act.wait_ge(lq_ok, 3 * j + 3)
                        act.wait_ge(wend_ok, j + 1)
                        nc.scalar.activation(w_cum[:, :], w_log[:, :], ACT.Exp, scale=-EXP_M_HALF).then_inc(wcum_ok, 1)
                        nc.scalar.activation(w_inv[:, :], w_log[:, :], ACT.Exp, scale=EXP_M_HALF).then_inc(winv_ok, 1)
                        act.wait_ge(winv_ok, j + 1)
                        act.sem_inc(winv_used, 1)
                        act.wait_ge(km_ok, j + 1)
                        act.wait_ge(lb_clear, 2)
                        nc.scalar.activation(ka[:, :], tile(aa, j), ACT.Identity, scale=col("k_a", j),
                                             bias=one_minus_ka[:, bass.ds(j, 1)]).then_inc(ka_ok, 1)
                        act.wait_ge(ssq_ok, j + 2)
                        nc.scalar.activation(ssq[:, :], ssq[:, :], ACT.Ln).then_inc(norm_ok, 1)
                        act.wait_ge(norm_ok, 2 * j + 1)
                        nc.scalar.activation(ssq[:, :], ssq[:, :], ACT.Exp, scale=-0.5).then_inc(norm_ok, 1)
                        act.wait_ge(sc_mm, 2 * j + 2)
                        act.wait_ge(bh_ok, j + 2)
                        act.wait_ge(kh_ok, j + 1)
                        act.sem_inc(spread_begun, 1)
                        for h in range(2):
                            hs = slice(HD * h, HD * h + HD)
                            nc.scalar.activation(lb[hs, :, 0, h, :], chunks(bh[hs, bass.ds(j, 1), :].rearrange("p a t -> p (a t)")), ACT.Copy).then_inc(lb_ok, 1)
                            nc.scalar.activation(lb[hs, :, 1, h, :], chunks(kh[hs, bass.ds(j, 1), :].rearrange("p a t -> p (a t)")), ACT.Copy).then_inc(lb_ok, 1)
                        act.wait_ge(cx_mm, j + 1)
                        act.wait_ge(yb_out, j * 16 + 16)
                        nc.scalar.activation(conv_x[:, :], bank[4][:, :], ACT.Copy).then_inc(cx_ok, 1)
                        act.wait_ge(u_ok, j + 1)
                        nc.scalar.activation(conv_y[:, :], conv_u[:, 2:T + 2], ACT.Copy, scale=col("conv_w", j + 16)).then_inc(c1_ok, 1)

                @block.tensor
                def _(pe):
                    pe.sem_inc(sc_mm, 2)

                    def conv(j, q, done):
                        pe.wait_ge(cw_in[q], j * 16 + 16)
                        for k in range(KT):
                            last = nc.tensor.matmul(bank[4 + q][:, :], conv_w3[:, q, k, :], xn[:, k, :], start=(k == 0), stop=(k == KT - 1))
                        last.then_inc(done, 1)

                    with pe.Fori(0, PAIRS) as j:
                        pe.wait_ge(sq_ok, j + 1)
                        pe.wait_ge(ssq_ok, j + 1)
                        nc.tensor.matmul(bank[0][:, :], head_ones[:, :], sq[:, :], start=True, stop=True).then_inc(ssq_mm, 1)
                        pe.wait_ge(yb_free, j + 1)
                        conv(j, 0, cx_mm)
                        pe.wait_ge(rk_ok, j + 1)
                        pe.wait_ge(bonus_ok, j + 1)
                        nc.tensor.matmul(bank[1][:, :], head_ones[:, :], rk[:, :], start=True, stop=True).then_inc(rksum_mm, 1)
                        conv(j, 1, cc_mm)
                        conv(j, 2, cb_mm)
                        pe.wait_ge(lb_ok, 4 * j + 4)
                        pe.wait_ge(lq_ok, 3 * j + 6)
                        for g in range(2):
                            pe.wait_ge(sc_ok, 2 * j + g + 1)
                            for c in range(8):
                                last = nc.tensor.matmul(bank[2 + g][:, c * 64:(c + 1) * 64], lb[:, 8 * g + c, :, :, :].rearrange("p b h s -> p (b h s)"),
                                                        lq[:, bass.ds(j, 1), 8 * g + c, :, :].rearrange("p j a t -> p (j a t)"),
                                                        start=True, stop=True)
                            last.then_inc(sc_mm, 1)

                @block.vector
                def _(dve):
                    for n, unused in ((3, lq_ok), (1, wend_ok), (1, yb_free)):
                        dve.sem_inc(unused, n)
                    for unused in (kk_ok, bh_ok, km_ok, ssq_ok, bonus_ok, winv_used, sc_ok, sc_ok):
                        dve.sem_inc(unused, 1)
                    nc.vector.memset(conv_u[:, 0:2], 0.0).then_inc(lb_clear, 1)
                    dve.wait_ge(lb_clear, 2)
                    with dve.Fori(0, PAIRS) as j:
                        r, k, v = (tile(rkv, j + n) for n in (0, 8, 16))
                        dve.wait_ge(winv_used, j + 1)
                        dve.wait_ge(bh_ok, j + 1)
                        nc.vector.tensor_tensor_scan(w_log[:, :], not_first[:, :], tile(decay, j), 0.0, ALU.mult, ALU.add).then_inc(wlog_ok, 1)
                        dve.wait_ge(ka_ok, j + 1)
                        nc.vector.tensor_tensor(k, k, ka[:, :], ALU.mult).then_inc(km_ok, 1)
                        dve.wait_ge(ssq_mm, j + 1)
                        dve.wait_ge(kk_ok, j + 1)
                        nc.vector.tensor_scalar(ssq[:, :], bank[0][:, :], 1e-24, None, ALU.max).then_inc(ssq_ok, 1)
                        dve.wait_ge(km_ok, j + 2)
                        nc.vector.scalar_tensor_tensor(out=rk[:, :], in0=r, scalar=col("r_k", j), in1=k, op0=ALU.mult, op1=ALU.mult).then_inc(rk_ok, 1)
                        dve.wait_ge(wcum_ok, j + 1)
                        lqj = lq[:, bass.ds(j, 1), :, :, :]
                        nc.vector.tensor_tensor(lqj[:, :, :, 1, :].rearrange("p j c t -> p (j c) t"), chunks(r), chunks(w_cum[:, :]), ALU.mult).then_inc(lq_ok, 1)
                        dve.wait_ge(kk_ok, j + 2)
                        nc.vector.tensor_tensor(lqj[:, :, :, 0, 1:C].rearrange("p j c t -> p (j c) t"), chunks(kk0[:, :])[:, :, 1:C],
                                                chunks(w_cum[:, :])[:, :, 0:C - 1], ALU.mult).then_inc(lq_ok, 1)
                        nc.vector.tensor_copy(lqj[:, :, :, 0, 0:1].rearrange("p j c t -> p (j c) t"), chunks(kk0[:, :])[:, :, 0:1]).then_inc(lq_ok, 1)
                        dve.wait_ge(winv_ok, j + 1)
                        nc.vector.scalar_tensor_tensor(out=kb[:, :], in0=kk0[:, :], scalar=-1.0, in1=tile(aa, j), op0=ALU.mult, op1=ALU.mult).then_inc(kb_ok, 1)
                        dve.wait_ge(winv_ok, j + 1)
                        nc.vector.tensor_tensor(k, k, w_inv[:, :], ALU.mult).then_inc(kh_ok, 1)
                        dve.wait_ge(kb_ok, j + 1)
                        nc.vector.tensor_tensor(tile(aa, j), kb[:, :], w_inv[:, :], ALU.mult).then_inc(bh_ok, 1)
                        nc.vector.tensor_copy(w_end[:, :, bass.ds(j, 1)], chunks(w_cum[:, :])[:, :, C - 1:C]).then_inc(wend_ok, 1)
                        dve.wait_ge(rksum_mm, j + 1)
                        dve.wait_ge(bonus_out, j * 16 + 16)
                        nc.vector.tensor_tensor(bonus[:, :], bank[1][:, :], v, ALU.mult).then_inc(bonus_ok, 1)
                        dve.wait_ge(cc_mm, j + 1)
                        dve.wait_ge(cx_ok, j + 1)
                        nc.vector.tensor_tensor(conv_u[:, 2:T + 2], bank[5][:, :], conv_x[:, :], ALU.mult).then_inc(u_ok, 1)
                        for g in range(2):
                            dve.wait_ge(sc_mm, 2 * j + g + 3)
                            nc.vector.tensor_tensor(sc[:, bass.ds(j, 1), 8 * g:8 * g + 8, :, :].rearrange("p j c a t -> p (j c) (a t)"),
                                                    bank[2 + g][:, :].rearrange("p (c a) -> p c a", c=8),
                                                    causal[:, :, :].rearrange("p a t -> p (a t)").unsqueeze(1).to_broadcast([P, 8, 2 * C]),
                                                    ALU.mult).then_inc(sc_ok, 1)
                        dve.wait_ge(c1_ok, j + 1)
                        nc.vector.scalar_tensor_tensor(out=conv_y[:, :], in0=conv_u[:, 1:T + 1], scalar=col("conv_w", j + 8), in1=conv_y[:, :],
                                                       op0=ALU.mult, op1=ALU.add).then_inc(c2_ok, 1)
                        dve.wait_ge(c2_ok, j + 1)
                        nc.vector.scalar_tensor_tensor(out=conv_y[:, :], in0=conv_u[:, 0:T], scalar=col("conv_w", j), in1=conv_y[:, :],
                                                       op0=ALU.mult, op1=ALU.add).then_inc(c3_ok, 1)
                        dve.wait_ge(c3_ok, j + 1)
                        dve.wait_ge(cb_mm, j + 1)
                        nc.vector.tensor_tensor(conv_y[:, :], conv_y[:, :], bank[6][:, :], ALU.mult).then_inc(yb_ok, 1)
                        dve.wait_ge(yb_ok, j + 1)
                        dve.sem_inc(yb_free, 1)
        early.close()

        with ExitStack() as s:
            a = Area(s)
            inv = a.sb("inv", [P, 2, C, C])
            prod = a.sb("prod", [P, 2, C * C // 4])
            MG = 256
            mem_w = a.sb("mem_w", [P, 2, KT, MG])
            memT = a.sb("memT", [P, KT, MEM])
            kv = a.sb("kv", [P, KT * MEM + 2 * D])
            mem_rstd = a.sb("mem_rstd", [P, MEM])
            mem_tok = kv[:, 0:2 * D].rearrange("p (i e) -> p i e", i=2)
            mem_sq = kv[:, KT * MEM:2 * KT * MEM].rearrange("p (k t) -> p k t", k=KT)
            m_out, m_in, solve_step, solved, t_out = map(a.sem, ("m_out", "m_in", "solve_step", "solved", "t_out"))
            (mem_in, mem_T, memT_ok, msq_ok, mean_mm, ln_ok, mrstd_ok, mn_ok, kv_mm, kv_out, kv_st) = map(
                a.sem, ("mem_in", "mem_T", "memT_ok", "msq_ok", "mean_mm", "ln_ok", "mrstd_ok", "mn_ok", "kv_mm", "kv_out", "kv_st"))
            mw_in = [a.sem("mw_in0"), a.sem("mw_in1")]
            block = s.enter_context(nc.Block())

            @block.sync
            def _(sp):
                sp.dma_start(mem_tok, mem[0, :, :].rearrange("(i p) e -> p i e", p=P)).then_inc(mem_in, 16)
                for h in range(2):
                    sp.dma_start(m_scr[:, h, :, :].rearrange("u s t -> s u t"),
                                 sc[C * h:C * h + C, :, :, 0, :].rearrange("s j c t -> s (j c) t")).then_inc(m_out, 16)

                def load_mem_w(g):
                    sp.dma_start(mem_w[:, g % 2, :, :], wkv_mem[0, :, g * MG:(g + 1) * MG].rearrange("(k p) c -> p k c", p=P)).then_inc(mw_in[g % 2], 16)

                load_mem_w(0)
                load_mem_w(1)
                sp.wait_ge(m_out, 32)
                sp.dma_start(inv[:, :, :, :], m_scr).then_inc(m_in, 16)
                for g in range(2, 2 * D // MG):
                    sp.wait_ge(kv_mm, 2 * (g - 1))
                    load_mem_w(g)
                sp.wait_ge(solved, 1)
                sp.dma_start(t_scr, inv[:, :, :, :]).then_inc(t_out, 16)
                sp.wait_ge(kv_out, 16)
                sp.dma_start(kv_scr, kv[:, :]).then_inc(kv_st, 16)
                sp.wait_ge(t_out, 16)
                sp.wait_ge(kv_st, 16)

            @block.tensor
            def _(pe):
                pe.wait_ge(mem_in, 16)
                for k in range(KT):
                    for i in range(2):
                        last = nc.tensor.transpose(bank[k // 2][:, (k % 2) * MEM + i * P:(k % 2) * MEM + (i + 1) * P],
                                                   mem_tok[:, i, k * P:(k + 1) * P], ident[:, :])
                    last.then_inc(mem_T, 1)
                for k in range(KT):
                    pe.wait_ge(msq_ok, k + 1)
                    last = nc.tensor.matmul(bank[4][:, 0:MEM], mean_ones[:, :], mem_sq[:, k, :], start=(k == 0), stop=(k == KT - 1))
                last.then_inc(mean_mm, 1)
                pe.wait_ge(mn_ok, KT)
                for g in range(2 * D // MG):
                    pe.wait_ge(mw_in[g % 2], 16 * (g // 2 + 1))
                    for q in range(2):
                        n = 2 * g + q
                        if n >= 8:
                            pe.wait_ge(kv_out, n - 7)
                        for k in range(KT):
                            if g < D // MG:
                                lhs, rhs = mem_w[:, g % 2, k, q * P:(q + 1) * P], memT[:, k, :]
                            else:
                                lhs, rhs = memT[:, k, q * P:(q + 1) * P], mem_w[:, g % 2, k, :]
                            last = nc.tensor.matmul(bank[n % 8][:, 0:MG], lhs, rhs, start=(k == 0), stop=(k == KT - 1))
                        last.then_inc(kv_mm, 1)

            @block.scalar
            def _(act):
                for k in range(KT):
                    act.wait_ge(mem_T, 2 * (k // 2) + 2)
                    half = bank[k // 2][:, (k % 2) * MEM:(k % 2) * MEM + MEM]
                    nc.scalar.activation(mem_sq[:, k, :], half, ACT.Square).then_inc(msq_ok, 1)
                    nc.scalar.activation(memT[:, k, :], half, ACT.Copy, scale=col("norm_memkv", k)).then_inc(memT_ok, 1)
                act.wait_ge(mean_mm, 1)
                nc.scalar.activation(mem_rstd[:, :], bank[4][:, 0:MEM], ACT.Ln, bias=eps_col[:, 0:1]).then_inc(ln_ok, 1)
                act.wait_ge(ln_ok, 1)
                nc.scalar.activation(mem_rstd[:, :], mem_rstd[:, :], ACT.Exp, scale=-0.5).then_inc(mrstd_ok, 1)
                for n in range(16):
                    at = n * MEM if n < KT else KT * MEM + (n % 2) * D + (n - KT) // 2 * MG
                    act.wait_ge(kv_mm, n + 1)
                    nc.scalar.activation(kv[:, at:at + MG], bank[n % 8][:, 0:MG], ACT.Copy).then_inc(kv_out, 1)

            @block.gpsimd
            def _(pool):
                pool.wait_ge(mrstd_ok, 1)
                for k in range(KT):
                    pool.wait_ge(memT_ok, k + 1)
                    nc.gpsimd.tensor_tensor(memT[:, k, :], memT[:, k, :], mem_rstd[:, :], ALU.mult).then_inc(mn_ok, 1)

            @block.vector
            def _(dve):
                step = Steps(dve, solve_step)
                dve.wait_ge(m_in, 16)
                for n in range(1, C - 1):
                    left, later = n, C - 1 - n
                    pr = prod[:, :, 0:left * later].rearrange("p h (j t) -> p h j t", j=left)
                    step(nc.vector.tensor_tensor(pr, inv[:, :, 0:n, n:n + 1].to_broadcast([P, 2, left, later]),
                                                 inv[:, :, n:n + 1, n + 1:C].to_broadcast([P, 2, left, later]), ALU.mult))
                    step(nc.vector.tensor_tensor(inv[:, :, 0:n, n + 1:C], inv[:, :, 0:n, n + 1:C], pr, ALU.add))
                flat_inv = inv[:, :, :, :].rearrange("p h s t -> p h (s t)")
                nc.vector.tensor_scalar(flat_inv[:, :, 0:C * C:C + 1], flat_inv[:, :, 0:C * C:C + 1], 1.0, None, ALU.add).then_inc(solved, 1)

        yT = rkv[:, 0:8, :]
        with ExitStack() as s:
            a = Area(s)
            state = a.sb("state", [P, PAIRS, HD])
            lqx = [a.sb(f"lqx{u}", [P, PAIRS, 2, 2, C]) for u in range(2)]
            scx = [a.sb(f"scx{u}", [P, PAIRS, 2, 2, C]) for u in range(2)]
            lbx = [a.sb(f"lbx{u}", [P, PAIRS, P]) for u in range(2)]
            ttx = [a.sb(f"ttx{u}", [2 * C, PAIRS, 2, C]) for u in range(2)]
            uv = [a.sb(f"uv{u}", [P, PAIRS, HD]) for u in range(2)]
            qs = a.sb("qs", [2 * C, PAIRS, HD])
            gate_w = a.sb("gate_w", [P, 4, KT, P])
            gate = a.sb("gate", [P, 2, T])
            gw_in = [a.sem(f"gw_in{n}") for n in range(4)]
            gate_out = [a.sem(f"gate_out{n}") for n in range(2)]
            g_mm, gate_ok = a.sem("g_mm"), a.sem("gate_ok")
            head_is = a.sb("head_is", [P, 2])
            (clear, spread, turned, tt_in0, tt_in1, q_mm, q_ok, u_mm, u_ok, s_mm, s_added, s_ok, y_mm, y_ok) = map(
                a.sem, ("clear", "spread", "turned", "tt_in0", "tt_in1", "q_mm", "q_ok", "u_mm", "u_ok", "s_mm", "s_added", "s_ok", "y_mm", "y_ok"))
            tt_in = [tt_in0, tt_in1]
            bh, kh, v = aa, rkv[:, 8:16, :], rkv[:, 16:24, :]
            HP = PAIRS // 2
            block = s.enter_context(nc.Block())

            @block.sync
            def _(sp):
                t_of = t_scr.rearrange("(j c) h s t -> c h s j t", c=NCH)
                for n in range(4):
                    sp.dma_start(gate_w[:, n, :, :], w_cols(GATE0 + n * P, P)).then_inc(gw_in[n], 16)
                sp.wait_ge(clear, 2)
                for c in range(NCH):
                    if c >= 2:
                        sp.wait_ge(u_mm, 2 * (c - 1))
                    for h in range(2):
                        sp.dma_start(ttx[c % 2][C * h:C * h + C, :, h, :], t_of[c, h, :, :, :]).then_inc(tt_in[c % 2], 16)
                    if c >= 2:
                        n = c - 2
                        sp.wait_ge(g_mm, n + 1)
                        if n + 4 < NCH:
                            sp.dma_start(gate_w[:, n % 4, :, :], w_cols(GATE0 + (n + 4) * P, P)).then_inc(gw_in[n % 4], 16)
                        sp.wait_ge(gate_ok, n + 1)
                        sp.dma_start(gates_scr[:, n, :], gate[:, n % 2, :]).then_inc(gate_out[n % 2], 16)
                for n in range(NCH - 2, NCH):
                    sp.wait_ge(gate_ok, n + 1)
                    sp.dma_start(gates_scr[:, n, :], gate[:, n % 2, :]).then_inc(gate_out[n % 2], 16)
                for n in range(2):
                    sp.wait_ge(gate_out[n], 16 * NCH // 2)

            @block.gpsimd
            def _(pool):
                for u in range(2):
                    nc.gpsimd.memset(ttx[u][:, :, :, :], 0.0)
                    nc.gpsimd.memset(lqx[u][:, :, :, :, :], 0.0)
                    nc.gpsimd.memset(lbx[u][:, :, :], 0.0)
                nc.gpsimd.memset(state[:, :, :], 0.0).then_inc(clear, 1)

            @block.scalar
            def _(act):
                act.wait_ge(clear, 2)

                def spread_chunk(c):
                    if c >= 2:
                        act.wait_ge(y_mm, 2 * (c - 1))
                    x = c % 2
                    for h in range(2):
                        hs = slice(HD * h, HD * h + HD)
                        nc.scalar.activation(lqx[x][hs, :, :, h, :], lq[hs, :, c, :, :], ACT.Copy).then_inc(spread, 1)
                        nc.scalar.activation(scx[x][:, :, :, h, :], sc[:, :, c, :, :], ACT.Copy,
                                             scale=head_is[:, h:h + 1]).then_inc(spread, 1)

                def gate_sigmoid(n):
                    act.wait_ge(g_mm, n + 1)
                    if n >= 2:
                        act.wait_ge(gate_out[n % 2], 16 * (n // 2))
                    nc.scalar.activation(gate[:, n % 2, :], bank[6 + n % 2][:, :], ACT.Sigmoid, bias=col("gate_b", n)).then_inc(gate_ok, 1)

                spread_chunk(0)
                for c in range(NCH):
                    if c + 1 < NCH:
                        spread_chunk(c + 1)
                    for g in range(2):
                        act.wait_ge(u_mm, 2 * c + g + 1)
                        nc.scalar.activation(uv[c % 2][0:2 * C, HP * g:HP * g + HP, :],
                                             bank[2 + g][0:2 * C, 0:HP * HD].rearrange("p (j v) -> p j v", j=HP), ACT.Copy).then_inc(u_ok, 1)
                    if c >= 1:
                        gate_sigmoid(c - 1)
                gate_sigmoid(NCH - 1)

            @block.vector
            def _(dve):
                for q in range(4):
                    nc.vector.memset(head_is[C * q:C * q + C, q % 2:q % 2 + 1], 1.0)
                    last = nc.vector.memset(head_is[C * q:C * q + C, 1 - q % 2:2 - q % 2], 0.0)
                last.then_inc(clear, 1)
                dve.wait_ge(clear, 2)

                def turn_chunk(c):
                    if c >= 2:
                        dve.wait_ge(y_mm, 2 * (c - 1))
                    cs = slice(C * c, C * c + C)
                    for h in range(2):
                        for half in range(2):
                            src = slice(HD * h + C * half, HD * h + C * half + C)
                            to = slice(HD * h + C * half, HD * h + C * half + C)
                            for kind, arr in ((0, bh), (1, kh)):
                                rs = slice(2 * C * kind + C * h, 2 * C * kind + C * h + C)
                                nc.vector.transpose(lbx[c % 2][rs, :, to], arr[src, :, cs]).then_inc(turned, 1)
                            nc.vector.transpose(uv[c % 2][2 * C + C * h:2 * C + C * h + C, :, C * half:C * half + C],
                                                v[src, :, cs]).then_inc(turned, 1)

                turn_chunk(0)
                for c in range(NCH):
                    for g in range(2):
                        js = slice(HP * g, HP * g + HP)
                        dve.wait_ge(q_mm, 2 * c + g + 1)
                        if c >= 1:
                            dve.wait_ge(u_mm, 2 * c - 1 + g)
                        nc.vector.tensor_copy(qs[:, js, :], bank[g][0:2 * C, 0:HP * HD].rearrange("p (j v) -> p j v", j=HP)).then_inc(q_ok, 1)
                    if c + 1 < NCH:
                        turn_chunk(c + 1)
                    for g in range(2):
                        js = slice(HP * g, HP * g + HP)
                        dve.wait_ge(s_mm, 2 * c + g + 1)
                        nc.vector.tensor_tensor(state[:, js, :], state[:, js, :], bank[4 + g][:, 0:HP * HD].rearrange("p (j v) -> p j v", j=HP),
                                                ALU.add).then_inc(s_added, 1)
                        dve.wait_ge(s_added, 2 * c + g + 1)
                        nc.vector.tensor_tensor(state[:, js, :], state[:, js, :],
                                                w_end[:, c, js].unsqueeze(2).to_broadcast([P, HP, HD]), ALU.mult).then_inc(s_ok, 1)
                    for g in range(2):
                        dve.wait_ge(y_mm, 2 * c + g + 1)
                        for h in range(2):
                            for half in range(2):
                                nc.vector.transpose(yT[HD * h + C * half:HD * h + C * half + C, HP * g:HP * g + HP, C * c:C * c + C],
                                                    bank[g][2 * C + C * h:2 * C + C * h + C, 0:HP * HD].rearrange("p (j v) -> p j v", j=HP)[:, :, C * half:C * half + C]).then_inc(y_ok, 1)

            @block.tensor
            def _(pe):
                pe.wait_ge(clear, 2)

                def gate_part(n, ks):
                    if ks[0] == 0:
                        pe.wait_ge(gw_in[n % 4], 16 * (n // 4 + 1))
                        if n >= 2:
                            pe.wait_ge(gate_ok, n - 1)
                    for k in ks:
                        last = nc.tensor.matmul(bank[6 + n % 2][:, :], gate_w[:, n % 4, k, :], xn[:, k, :], start=(k == 0), stop=(k == KT - 1))
                    if ks[-1] == KT - 1:
                        last.then_inc(g_mm, 1)

                for c in range(NCH):
                    x = c % 2
                    pe.wait_ge(spread, 4 * (c + 1))
                    pe.wait_ge(turned, 12 * (c + 1))
                    for g in range(2):
                        if c >= 1:
                            pe.wait_ge(s_ok, 2 * (c - 1) + g + 1)
                            pe.wait_ge(y_ok, 8 * (c - 1) + 4 * g + 4)
                        for n in range(HP):
                            j = HP * g + n
                            cols = slice(HD * n, HD * n + HD)
                            nc.tensor.matmul(bank[g][:, cols], lqx[x][:, j, :, :, :].rearrange("p a h t -> p (a h t)"), state[:, j, :],
                                             start=(n == 0), stop=False, skip_group_check=True)
                            last = nc.tensor.matmul(bank[g][0:2 * C, cols], scx[x][2 * C:P, j, 0, :, :].rearrange("p h t -> p (h t)"),
                                                    uv[x][2 * C:P, j, :], start=False, stop=False, skip_group_check=True)
                        last.then_inc(q_mm, 1)
                    gate_part(c, (0,))
                    pe.wait_ge(tt_in[x], 32 * (c // 2 + 1))
                    for g in range(2):
                        pe.wait_ge(q_ok, 2 * c + g + 1)
                        if c >= 1:
                            pe.wait_ge(u_ok, 2 * (c - 1) + g + 1)
                        for n in range(HP):
                            j = HP * g + n
                            last = nc.tensor.matmul(bank[2 + g][0:2 * C, HD * n:HD * n + HD], ttx[x][:, j, :, :].rearrange("p h t -> p (h t)"),
                                                    qs[:, j, :], start=True, stop=True)
                        last.then_inc(u_mm, 1)
                    gate_part(c, (1,))
                    for g in range(2):
                        pe.wait_ge(u_ok, 2 * c + g + 1)
                        for n in range(HP):
                            j = HP * g + n
                            last = nc.tensor.matmul(bank[4 + g][:, HD * n:HD * n + HD], lbx[x][:, j, :], uv[x][:, j, :], start=True, stop=True)
                        last.then_inc(s_mm, 1)
                        for n in range(HP):
                            j = HP * g + n
                            last = nc.tensor.matmul(bank[g][2 * C:P, HD * n:HD * n + HD], scx[x][:, j, 1, :, :].rearrange("p h t -> p (h t)"),
                                                    uv[x][:, j, :], start=False, stop=True, skip_group_check=True)
                        last.then_inc(y_mm, 1)
                    gate_part(c, (2, 3, 4, 5, 6, 7))


        with ExitStack() as s:
            a = Area(s)
            y_sq, y_rstd = sc_flat[:, 0:4096], sc_flat[:, 4096:8192]
            og = lq_flat[:, 0:4096]
            bonus = rkv[:, 8:16, :].rearrange("p k t -> p (k t)")
            yf = yT.rearrange("p k t -> p (k t)")
            (og_in, mean_mm, centred, sq_ok, var_mm, rstd_ok, scaled, exp_ok, with_bonus, gated, yb_in) = map(
                a.sem, ("og_in", "mean_mm", "centred", "sq_ok", "var_mm", "rstd_ok", "scaled", "exp_ok", "with_bonus", "gated", "yb_in"))
            block = s.enter_context(nc.Block())

            def ts(j):
                return slice(j * T, j * T + T)

            @block.sync
            def _(sp):
                sp.dma_start(og, og_scr).then_inc(og_in, 16)
                sp.dma_start(bonus, bonus_scr).then_inc(og_in, 16)
                sp.dma_start(rkv[:, 16:24, :], yb_scr).then_inc(yb_in, 16)
                sp.wait_ge(og_in, 32)
                sp.wait_ge(yb_in, 16)

            @block.tensor
            def _(pe):
                for j in range(KT):
                    if j >= 4:
                        pe.wait_ge(centred, j - 3)
                    nc.tensor.matmul(bank[j % 4][:, :], head_ones[:, :], yT[:, j, :], start=True, stop=True).then_inc(mean_mm, 1)
                for j in range(KT):
                    pe.wait_ge(sq_ok, j + 1)
                    if j >= 4:
                        pe.wait_ge(rstd_ok, j - 3)
                    nc.tensor.matmul(bank[4 + j % 4][:, :], head_ones[:, :], y_sq[:, ts(j)], start=True, stop=True).then_inc(var_mm, 1)

            @block.vector
            def _(dve):
                for j in range(KT):
                    dve.wait_ge(mean_mm, j + 1)
                    nc.vector.scalar_tensor_tensor(out=yf[:, ts(j)], in0=bank[j % 4][:, :], scalar=-1.0 / HD, in1=yf[:, ts(j)],
                                                   op0=ALU.mult, op1=ALU.add).then_inc(centred, 1)
                dve.wait_ge(og_in, 32)
                for j in range(KT):
                    dve.wait_ge(exp_ok, j + 1)
                    nc.vector.scalar_tensor_tensor(out=yf[:, ts(j)], in0=yf[:, ts(j)], scalar=col("lnx_g", j), in1=y_rstd[:, ts(j)],
                                                   op0=ALU.mult, op1=ALU.mult).then_inc(scaled, 1)
                    if j >= 1:
                        dve.wait_ge(scaled, j)
                        nc.vector.scalar_tensor_tensor(out=yf[:, ts(j - 1)], in0=yf[:, ts(j - 1)], scalar=col("lnx_b", j - 1), in1=bonus[:, ts(j - 1)],
                                                       op0=ALU.add, op1=ALU.add).then_inc(with_bonus, 1)
                    if j >= 2:
                        dve.wait_ge(with_bonus, j - 1)
                        nc.vector.tensor_tensor(yf[:, ts(j - 2)], yf[:, ts(j - 2)], og[:, ts(j - 2)], ALU.mult).then_inc(gated, 1)
                dve.wait_ge(scaled, KT)
                nc.vector.scalar_tensor_tensor(out=yf[:, ts(KT - 1)], in0=yf[:, ts(KT - 1)], scalar=col("lnx_b", KT - 1), in1=bonus[:, ts(KT - 1)],
                                               op0=ALU.add, op1=ALU.add).then_inc(with_bonus, 1)
                for j in range(KT - 2, KT):
                    dve.wait_ge(with_bonus, j + 1)
                    nc.vector.tensor_tensor(yf[:, ts(j)], yf[:, ts(j)], og[:, ts(j)], ALU.mult).then_inc(gated, 1)

            @block.scalar
            def _(act):
                for j in range(KT):
                    act.wait_ge(centred, j + 1)
                    nc.scalar.activation(y_sq[:, ts(j)], yf[:, ts(j)], ACT.Square).then_inc(sq_ok, 1)
                for j in range(KT):
                    act.wait_ge(var_mm, j + 1)
                    nc.scalar.activation(y_rstd[:, ts(j)], bank[4 + j % 4][:, :], ACT.Ln, scale=1.0 / HD, bias=eps_col[:, 1:2]).then_inc(rstd_ok, 1)
                for j in range(KT):
                    act.wait_ge(rstd_ok, j + 1)
                    nc.scalar.activation(y_rstd[:, ts(j)], y_rstd[:, ts(j)], ACT.Exp, scale=-0.5).then_inc(exp_ok, 1)
        wkv.close()

        dense = ExitStack()
        d = Area(dense)
        x2T = rkv[:, 0:8, :]
        with ExitStack() as s:
            a = Area(s)
            xT = x2T
            SLOT_TILES = 6
            w_raw = a.sb("w_raw", [P, KT, 512])
            w_hi = a.sb("w_hi", [P, SLOT_TILES, KT, P], F32R)
            w_lo = a.sb("w_lo", [P, SLOT_TILES, KT, P], F32R)
            act_hi = a.sb("act_hi", [P, KT, T], F32R)
            act_lo = a.sb("act_lo", [P, KT, T], F32R)
            yb_hi = a.sb("yb_hi", [P, KT, T], F32R)
            yb_lo = a.sb("yb_lo", [P, KT, T], F32R)
            gates = a.sb("gates", [P, KT, T])
            ya, yb, merged = rkv[:, 0:8, :], rkv[:, 16:24, :], rkv[:, 8:16, :]
            pT = a.sb("pT", [P, 2, 2, T])
            rstd = a.sb("rstd", [P, T])
            prob = a.sb("prob", [P, 2, MEM])
            small = a.sb("small", [P, 4, 16])
            hq, qT, sq = merged, merged, gates
            kv = gates[:, :, :].rearrange("p k t -> p (k t)")
            kT = kv[:, 0:KT * MEM].rearrange("p (k t) -> p k t", k=KT)
            vm = kv[:, KT * MEM:KT * MEM + 2 * D].rearrange("p (m e) -> p m e", m=2)
            names = ("gates_in gates_in0 gates_in1 x_in kv_in tile_mm tile_out w_hi_ok w_lo_ok a_hi_ok a_lo_ok sq_ok mean_mm ms_ok std_ok "
                     "rstd_ok hq_ok br_ok s_mm max_ok nmax_ok exp_ok inv_ok p_ok p_T pT_ok o_mm").split()
            S = {n: a.sem(n) for n in names}
            w_loaded = a.sem("w_loaded")
            BRA, BRB, MIX, WQ, WO = 0, 2, 4, 6, 8
            MATRICES = (w_br_a, w_br_b, w_mix_out, wq_mem, wo_mem)
            block = s.enter_context(nc.Block())
            mm, outn = S["tile_mm"], S["tile_out"]

            @block.sync
            def _(sp):
                sp.sem_inc(mm, 8)
                for g in range(10):
                    if g >= 1:
                        sp.wait_ge(S["w_lo_ok"], 4 * g)
                    sp.dma_start(w_raw[:, :, :], MATRICES[g // 2][0, :, (g % 2) * 512:(g % 2) * 512 + 512].rearrange("(k p) c -> p k c", p=P)
                                 ).then_inc(w_loaded, 16)
                    if g == BRA:
                        sp.dma_start(gates[:, :, :], gates_scr[:, 0:KT, :]).then_inc(S["gates_in"], 16)
                    if g == BRB:
                        sp.wait_ge(S["a_lo_ok"], 8)
                        sp.dma_start(xT[:, :, :], x_scr).then_inc(S["x_in"], 16)
                    if g == BRB + 1:
                        for u in range(2):
                            sp.wait_ge(outn, 4 * (BRA + u) + 12)
                            sp.dma_start(gates[:, 4 * u:4 * u + 4, :], gates_scr[:, KT + 4 * u:KT + 4 * u + 4, :]).then_inc(S[f"gates_in{u}"], 16)
                    if g == WQ + 1:
                        sp.wait_ge(S["mean_mm"], 1)
                        sp.dma_start(kv, kv_scr).then_inc(S["kv_in"], 16)

            def bk(g, q):
                return bank[(g % 2) * 4 + q]

            HI_OF = {BRA: act_hi, BRB: yb_hi, MIX: act_hi, WQ: act_hi, WO: act_hi}
            LO_OF = {BRA: act_lo, BRB: yb_lo, MIX: act_lo, WQ: act_lo, WO: act_lo}

            def transpose_probs(pe, n):
                h, i = divmod(n, TT)
                pe.wait_ge(S["p_ok"], n + 1)
                if i == 0 and h >= 1:
                    pe.wait_ge(S["pT_ok"], 2 * h)
                for m in range(2):
                    last = nc.tensor.transpose(bank[2 + m][:, i * P:(i + 1) * P], prob[:, n % 2, m * P:(m + 1) * P], ident[:, :])
                last.then_inc(S["p_T"], 1)

            def values(pe, h):
                pe.wait_ge(S["pT_ok"], 2 * h + 2)
                for e in range(2):
                    if h >= 2:
                        pe.wait_ge(S["a_lo_ok"], 4 * 8 + 2 * (h - 2) + e + 1)
                    for m in range(2):
                        last = nc.tensor.matmul(bank[4 + 2 * (h % 2) + e][:, :], vm[:, m, h * MHD + e * P:h * MHD + (e + 1) * P],
                                                pT[:, h % 2, m, :], start=(m == 0), stop=(m == 1))
                    last.then_inc(S["o_mm"], 1)

            def probs_copy(dve, h):
                dve.wait_ge(S["p_T"], TT * (h + 1))
                if h >= 2:
                    dve.wait_ge(S["o_mm"], 2 * (h - 1))
                for m in range(2):
                    nc.vector.tensor_copy(pT[:, h % 2, m, :], bank[2 + m][:, :]).then_inc(S["pT_ok"], 1)

            @block.tensor
            def _(pe):
                def group(g):
                    hi, lo = HI_OF[g - g % 2], LO_OF[g - g % 2]
                    pe.wait_ge(outn, 4 * g + 4)
                    for q in range(4):
                        pe.wait_ge(S["w_lo_ok"], 4 * g + q + 1)
                        n = (4 * g + q) % SLOT_TILES
                        for k in range(KT):
                            if q == 0:
                                pe.wait_ge(S["a_lo_ok"], 8 * (g // 2) + k + 1)
                            nc.tensor.matmul(bk(g, q)[:, :], w_hi[:, n, k, :], hi[:, k, :], start=(k == 0), stop=False)
                            nc.tensor.matmul(bk(g, q)[:, :], w_hi[:, n, k, :], lo[:, k, :], start=False, stop=False)
                            last = nc.tensor.matmul(bk(g, q)[:, :], w_lo[:, n, k, :], hi[:, k, :], start=False, stop=(k == KT - 1))
                        last.then_inc(mm, 1)

                for g in range(MIX + 2):
                    group(g)
                pe.wait_ge(outn, 4 * MIX + 16)
                for k in range(KT):
                    pe.wait_ge(S["sq_ok"], k + 1)
                    last = nc.tensor.matmul(bank[0][:, :], mean_ones[:, :], sq[:, k, :], start=(k == 0), stop=(k == KT - 1))
                last.then_inc(S["mean_mm"], 1)
                for u in range(2):
                    group(WQ + u)
                pe.wait_ge(outn, 4 * WQ + 16)
                pe.wait_ge(S["kv_in"], 16)
                for h in range(MH):
                    for i in range(TT):
                        n = h * TT + i
                        if n >= 2:
                            pe.wait_ge(S["exp_ok"], n - 1)
                        for k in range(2):
                            last = nc.tensor.matmul(bank[n % 2][:, 0:MEM], qT[:, 2 * h + k, i * P:(i + 1) * P], kT[:, 2 * h + k, :],
                                                    start=(k == 0), stop=(k == 1))
                        last.then_inc(S["s_mm"], 1)
                        if n >= 1:
                            transpose_probs(pe, n - 1)
                        if i == 0 and h >= 1:
                            values(pe, h - 1)
                transpose_probs(pe, MH * TT - 1)
                values(pe, MH - 1)
                pe.wait_ge(S["a_lo_ok"], 5 * 8)
                for u in range(2):
                    group(WO + u)

            @block.scalar
            def _(act):
                def high_weights(g, tiles=range(4)):
                    act.wait_ge(w_loaded, 16 * (g + 1))
                    for q in tiles:
                        n = 4 * g + q
                        if n >= SLOT_TILES:
                            act.wait_ge(mm, 8 + n - SLOT_TILES + 1)
                        nc.scalar.activation(w_hi[:, n % SLOT_TILES, :, :], w_raw[:, :, q * P:(q + 1) * P], ACT.Copy).then_inc(S["w_hi_ok"], 1)

                def high(dst, src, k):
                    nc.scalar.activation(dst[:, k, :], src[:, k, :], ACT.Copy).then_inc(S["a_hi_ok"], 1)

                def high_values(h):
                    for e in range(2):
                        act.wait_ge(S["o_mm"], 2 * h + e + 1)
                        nc.scalar.activation(act_hi[:, 2 * h + e, :], bank[4 + 2 * (h % 2) + e][:, :], ACT.Copy).then_inc(S["a_hi_ok"], 1)

                act.sem_inc(outn, 8)
                for k in range(KT):
                    high(act_hi, ya, k)
                high_weights(BRA)
                high_weights(BRA + 1)
                for k in range(KT):
                    high(yb_hi, yb, k)
                high_weights(BRB)
                high_weights(BRB + 1)
                for u in range(2):
                    for q in range(4):
                        act.wait_ge(S["br_ok"], 4 * u + q + 1)
                        high(act_hi, merged, 4 * u + q)
                    high_weights(MIX + u)
                for u in range(2):
                    for q in range(4):
                        act.wait_ge(outn, 4 * (MIX + u) + q + 9)
                        nc.scalar.activation(sq[:, 4 * u + q, :], x2T[:, 4 * u + q, :], ACT.Square).then_inc(S["sq_ok"], 1)
                    if u == 0:
                        high_weights(WQ)
                act.wait_ge(S["ms_ok"], 1)
                nc.scalar.activation(rstd[:, :], rstd[:, :], ACT.Sqrt).then_inc(S["std_ok"], 1)
                for k in range(KT):
                    act.wait_ge(S["hq_ok"], k + 1)
                    high(act_hi, hq, k)
                high_weights(WQ + 1)
                for u in range(2):
                    for q in range(4):
                        act.wait_ge(mm, 4 * (WQ + u) + q + 9)
                        nc.scalar.activation(qT[:, 4 * u + q, :], bank[4 * u + q][:, :], ACT.Copy).then_inc(outn, 1)
                    if u == 0:
                        high_weights(WO)
                for h in range(MH):
                    for i in range(TT):
                        n = h * TT + i
                        act.wait_ge(S["nmax_ok"], n + 1)
                        if n >= 2:
                            act.wait_ge(S["p_T"], n - 1)
                        nc.scalar.activation(prob[:, n % 2, :], bank[n % 2][:, 0:MEM], ACT.Exp, bias=small[:, 0, n:n + 1], scale=MHD ** -0.5,
                                             accum_out=small[:, 1, n:n + 1]).then_inc(S["exp_ok"], 1)
                        if i == 2 and h >= 1:
                            high_values(h - 1)
                        if i == 3 and h == 1:
                            high_weights(WO + 1, (0, 1))
                high_values(MH - 1)
                high_weights(WO + 1, (2, 3))

            @block.vector
            def _(dve):
                def low_weights(g, tiles=range(4)):
                    for q in tiles:
                        n = 4 * g + q
                        dve.wait_ge(S["w_hi_ok"], n + 1)
                        nc.vector.tensor_tensor(w_lo[:, n % SLOT_TILES, :, :], w_raw[:, :, q * P:(q + 1) * P],
                                                w_hi[:, n % SLOT_TILES, :, :].bitcast(F32), ALU.subtract).then_inc(S["w_lo_ok"], 1)

                def low(phase, dst, src, hi, k):
                    dve.wait_ge(S["a_hi_ok"], 8 * phase + k + 1)
                    nc.vector.tensor_tensor(dst[:, k, :], src, hi[:, k, :].bitcast(F32), ALU.subtract).then_inc(S["a_lo_ok"], 1)

                def low_values(h):
                    for e in range(2):
                        low(4, act_lo, bank[4 + 2 * (h % 2) + e][:, :], act_hi, 2 * h + e)

                for k in range(KT):
                    low(0, act_lo, ya[:, k, :], act_hi, k)
                low_weights(BRA)
                low_weights(BRA + 1)
                for k in range(KT):
                    low(1, yb_lo, yb[:, k, :], yb_hi, k)
                dve.wait_ge(S["gates_in"], 16)
                dve.wait_ge(outn, 8)
                for u in range(2):
                    for q in range(4):
                        dve.wait_ge(mm, 4 * (BRA + u) + q + 9)
                        nc.vector.tensor_tensor(merged[:, 4 * u + q, :], bank[4 * u + q][:, :], gates[:, 4 * u + q, :], ALU.mult).then_inc(outn, 1)
                    low_weights(BRB + u)
                for u in range(2):
                    dve.wait_ge(S[f"gates_in{u}"], 16)
                    for q in range(4):
                        j = 4 * u + q
                        dve.wait_ge(mm, 4 * (BRB + u) + q + 9)
                        nc.vector.tensor_tensor(gates[:, j, :], bank[4 * u + q][:, :], gates[:, j, :], ALU.mult).then_inc(outn, 1)
                        dve.wait_ge(outn, 4 * (BRB + u) + q + 9)
                        nc.vector.tensor_tensor(merged[:, j, :], merged[:, j, :], gates[:, j, :], ALU.add).then_inc(S["br_ok"], 1)
                        low(2, act_lo, merged[:, j, :], act_hi, j)
                    low_weights(MIX + u)
                dve.wait_ge(S["x_in"], 16)
                for u in range(2):
                    for q in range(4):
                        j = 4 * u + q
                        dve.wait_ge(mm, 4 * (MIX + u) + q + 9)
                        nc.vector.tensor_tensor(xT[:, j, :], xT[:, j, :], bank[4 * u + q][:, :], ALU.add).then_inc(outn, 1)
                    if u == 0:
                        low_weights(WQ)
                dve.wait_ge(S["mean_mm"], 1)
                nc.vector.tensor_scalar(rstd[:, :], bank[0][:, :], RMS_EPS, None, ALU.add).then_inc(S["ms_ok"], 1)
                dve.wait_ge(S["std_ok"], 1)
                nc.vector.reciprocal(rstd[:, :], rstd[:, :]).then_inc(S["rstd_ok"], 1)
                dve.wait_ge(S["rstd_ok"], 1)
                for k in range(KT):
                    nc.vector.scalar_tensor_tensor(out=hq[:, k, :], in0=xT[:, k, :], scalar=col("norm_memq", k), in1=rstd[:, :],
                                                   op0=ALU.mult, op1=ALU.mult).then_inc(S["hq_ok"], 1)
                    if k >= 1:
                        low(3, act_lo, hq[:, k - 1, :], act_hi, k - 1)
                low(3, act_lo, hq[:, KT - 1, :], act_hi, KT - 1)
                low_weights(WQ + 1)
                low_weights(WO)
                for h in range(MH):
                    for i in range(TT):
                        n = h * TT + i
                        dve.wait_ge(S["s_mm"], n + 1)
                        nc.vector.reduce_max(small[:, 3, n:n + 1], bank[n % 2][:, 0:MEM], AX.X).then_inc(S["max_ok"], 1)
                        dve.wait_ge(S["max_ok"], n + 1)
                        nc.vector.tensor_scalar(small[:, 0, n:n + 1], small[:, 3, n:n + 1], -(MHD ** -0.5), None, ALU.mult).then_inc(S["nmax_ok"], 1)
                        dve.wait_ge(S["exp_ok"], n + 1)
                        nc.vector.reciprocal(small[:, 2, n:n + 1], small[:, 1, n:n + 1]).then_inc(S["inv_ok"], 1)
                        dve.wait_ge(S["inv_ok"], n + 1)
                        nc.vector.tensor_scalar(prob[:, n % 2, :], prob[:, n % 2, :], small[:, 2, n:n + 1], None, ALU.mult).then_inc(S["p_ok"], 1)
                        if i == 0 and h >= 1:
                            probs_copy(dve, h - 1)
                        if i == 2 and h >= 1:
                            low_values(h - 1)
                        if i == 3 and h == 1:
                            low_weights(WO + 1, (0, 1))
                probs_copy(dve, MH - 1)
                low_values(MH - 1)
                dve.wait_ge(outn, 4 * WO + 8)
                for u in range(2):
                    for q in range(4):
                        if u == 0 and q == 2:
                            low_weights(WO + 1, (2, 3))
                        j = 4 * u + q
                        dve.wait_ge(mm, 4 * (WO + u) + q + 9)
                        nc.vector.tensor_tensor(xT[:, j, :], xT[:, j, :], bank[4 * u + q][:, :], ALU.add).then_inc(outn, 1)



        Area.recycle()
        moe = d
        x2_tok = rkv[:, 8:16, :].rearrange("p k t -> p (k t)").rearrange("p (i e) -> p i e", i=TT)
        rows_i = moe.sb("rows_i", [P, TT, 2], I32)
        weight = moe.sb("weight", [P, TT, 2])
        most_i = moe.sb("most_i", [P, 1], I32)
        experts = ExitStack()
        weights = Area(experts)
        wg = [weights.sb(f"wg{u}", [P, KT, DE]) for u in range(2)]
        wu = [weights.sb(f"wu{u}", [P, KT, DE]) for u in range(2)]
        wdn = [weights.sb(f"wd{u}", [P, DE // P, D]) for u in range(2)]
        gu_in = [weights.sem("gu_in0"), weights.sem("gu_in1")]
        dn_in = [weights.sem("dn_in0"), weights.sem("dn_in1")]

        def load_weights(sp, e, u):
            for dst, src in ((wg[u], w_e_gate), (wu[u], w_e_up)):
                sp.dma_start(dst[:, :, :], src[0, bass.ds(e, 1), :, :].rearrange("e (k p) f -> p (e k) f", p=P)).then_inc(gu_in[u], 16)
            sp.dma_start(wdn[u][:, :, :], w_e_down[0, bass.ds(e, 1), :, :].rearrange("e (k p) f -> p (e k) f", p=P)).then_inc(dn_in[u], 16)

        with ExitStack() as s:
            a = Area(s)
            hnT = a.sb("hnT", [P, KT, T])
            hn_tok = a.sb("hn_tok", [P, TT, D])
            sq = a.sb("sq", [P, KT, T])
            rstd = a.sb("rstd", [P, T])
            rw = a.sb("rw", [P, KT, NG + NE])
            rb = a.sb("rb", [P, NG + NE])
            ones = a.sb("ones", [P, P])
            rank = a.sb("rank", [P, EPG])
            base = a.sb("base", [P, NE])
            logit = a.sb("logit", [P, TT, NG + NE])
            t4, fg, f1, f2, el, el2, eg = (a.sb(n, [P, TT, EPG]) for n in ("t4", "fg", "f1", "f2", "el", "el2", "eg"))
            mx, mg, m1, m2, gs, e2, den = (a.sb(n, [P, TT, 1]) for n in ("mx", "mg", "m1", "m2", "gs", "e2", "den"))
            t44 = a.sb("t44", [P, TT, NG, EPG])
            one_hot = a.sb("one_hot", [P, 2, TT, NE])
            chosen = a.sb("chosen", [P, TT, NE])
            place = a.sb("place", [P, TT, NE])
            t16 = a.sb("t16", [P, TT, NE])
            rows_f = a.sb("rows_f", [P, TT, 2])
            entry_f = a.sb("entry_f", [P, TT, 2])
            entry_i = a.sb("entry_i", [P, TT, 2], I32)
            expert_no = a.sb("expert_no", [P, NE])
            most = a.sb("most", [P, 1])
            token = a.sb("token", [P, TT], I32)
            zero_i = a.sb("zero_i", [P, NE * T // P], I32)
            names = ("router_in bias_in sq_ok mean_mm ms_ok std_ok rstd_ok hn_ok x_T hn_T x_tok_ok hn_tok_ok logit_mm small_step exp_in exp_ok chosen_ok place_mm "
                     "rows_ok hn_out zero_ok zeroed token_ok scattered consts pool_step").split()
            S = {n: a.sem(n) for n in names}
            block = s.enter_context(nc.Block())

            @block.sync
            def _(sp):
                sp.dma_start(rw[:, :, 0:NG], router_g[0, :, :].rearrange("(k p) c -> p k c", p=P)).then_inc(S["router_in"], 16)
                sp.dma_start(rw[:, :, NG:NG + NE], router_e[0, :, :].rearrange("(k p) c -> p k c", p=P)).then_inc(S["router_in"], 16)
                sp.dma_start(rb[:, 0:NG], router_g_b[0:1, :].to_broadcast([P, NG])).then_inc(S["bias_in"], 16)
                sp.dma_start(rb[:, NG:NG + NE], router_e_b[0:1, :].to_broadcast([P, NE])).then_inc(S["bias_in"], 16)
                sp.wait_ge(S["zero_ok"], 1)
                sp.dma_start(tok_scr.rearrange("(p n) a -> p (n a)", p=P), zero_i[:, :]).then_inc(S["zeroed"], 16)
                for u in range(2):
                    load_weights(sp, u, u)
                sp.wait_ge(S["hn_tok_ok"], KT)
                sp.dma_start(hn_scr.rearrange("(i p) e -> p i e", p=P), hn_tok[:, :, :]).then_inc(S["hn_out"], 16)
                sp.wait_ge(S["hn_out"], 16)

            @block.gpsimd
            def _(pool):
                step = Steps(pool, S["pool_step"])
                step(nc.gpsimd.memset(zero_i[:, :], 0))
                pool.sem_inc(S["zero_ok"], 1)
                step(nc.gpsimd.iota(token[:, :], pattern=[[P, TT]], base=0, channel_multiplier=1))
                pool.wait_ge(S["zeroed"], 16)
                pool.wait_ge(S["rows_ok"], 1)
                for i in range(TT):
                    for n in range(2):
                        nc.gpsimd.indirect_dma_start(tok_scr, bass.IndirectOffsetOnAxis(ap=entry_i[:, i, n:n + 1], axis=0),
                                                     token[:, i:i + 1], None).then_inc(S["scattered"], 16)
                pool.wait_ge(S["scattered"], 16 * 2 * TT)

            @block.scalar
            def _(act):
                for k in range(KT):
                    nc.scalar.activation(sq[:, k, :], x2T[:, k, :], ACT.Square).then_inc(S["sq_ok"], 1)
                act.wait_ge(S["ms_ok"], 1)
                nc.scalar.activation(rstd[:, :], rstd[:, :], ACT.Sqrt).then_inc(S["std_ok"], 1)
                for k in range(KT):
                    act.wait_ge(S["x_T"], k + 1)
                    nc.scalar.activation(x2_tok[:, :, k * P:(k + 1) * P], bank[k % 4][:, :].rearrange("p (i c) -> p i c", i=TT), ACT.Copy).then_inc(S["x_tok_ok"], 1)
                for k in range(KT):
                    act.wait_ge(S["hn_T"], k + 1)
                    nc.scalar.activation(hn_tok[:, :, k * P:(k + 1) * P], bank[k % 4][:, :].rearrange("p (i c) -> p i c", i=TT), ACT.Copy).then_inc(S["hn_tok_ok"], 1)
                act.wait_ge(S["exp_in"], 1)
                nc.scalar.activation(eg[:, :, :], eg[:, :, :], ACT.Exp).then_inc(S["exp_ok"], 1)
                act.wait_ge(S["exp_in"], 2)
                nc.scalar.activation(e2[:, :, :], e2[:, :, :], ACT.Exp).then_inc(S["exp_ok"], 1)

            @block.tensor
            def _(pe):
                for k in range(KT):
                    pe.wait_ge(S["sq_ok"], k + 1)
                    last = nc.tensor.matmul(bank[4][:, :], mean_ones[:, :], sq[:, k, :], start=(k == 0), stop=(k == KT - 1))
                last.then_inc(S["mean_mm"], 1)
                for k in range(KT):
                    if k >= 4:
                        pe.wait_ge(S["x_tok_ok"], k - 3)
                    for i in range(TT):
                        last = nc.tensor.transpose(bank[k % 4][:, i * P:(i + 1) * P], x2T[:, k, i * P:(i + 1) * P], ident[:, :])
                    last.then_inc(S["x_T"], 1)
                pe.wait_ge(S["hn_ok"], KT)
                pe.wait_ge(S["router_in"], 32)
                for i in range(TT):
                    for k in range(KT):
                        last = nc.tensor.matmul(bank[5][:, i * 32:i * 32 + NG + NE], hnT[:, k, i * P:(i + 1) * P], rw[:, k, :],
                                                start=(k == 0), stop=(k == KT - 1))
                last.then_inc(S["logit_mm"], 1)
                for k in range(KT):
                    if k >= 4:
                        pe.wait_ge(S["hn_tok_ok"], k - 3)
                    else:
                        pe.wait_ge(S["x_tok_ok"], k + 5)
                    for i in range(TT):
                        last = nc.tensor.transpose(bank[k % 4][:, i * P:(i + 1) * P], hnT[:, k, i * P:(i + 1) * P], ident[:, :])
                    last.then_inc(S["hn_T"], 1)
                pe.wait_ge(S["chosen_ok"], 1)
                pe.wait_ge(S["consts"], 1)
                for i in range(TT):
                    for m in range(i):
                        nc.tensor.matmul(bank[6][:, i * NE:(i + 1) * NE], ones[:, :], chosen[:, m, :], start=(m == 0), stop=False)
                    nc.tensor.matmul(bank[6][:, i * NE:(i + 1) * NE], earlier[:, :], chosen[:, i, :], start=(i == 0), stop=True)
                for i in range(TT):
                    last = nc.tensor.matmul(bank[7][:, 0:NE], ones[:, :], chosen[:, i, :], start=(i == 0), stop=(i == TT - 1))
                last.then_inc(S["place_mm"], 1)

            @block.vector
            def _(dve):
                step = Steps(dve, S["small_step"])
                nc.vector.memset(ones[:, :], 1.0)
                for n in range(EPG):
                    nc.vector.memset(rank[:, n:n + 1], float(EPG - n))
                for n in range(NE):
                    nc.vector.memset(expert_no[:, n:n + 1], float(n))
                    last = nc.vector.memset(base[:, n:n + 1], float(n * SLOTS))
                last.then_inc(S["consts"], 1)
                dve.wait_ge(S["consts"], 1)
                dve.wait_ge(S["mean_mm"], 1)
                nc.vector.tensor_scalar(rstd[:, :], bank[4][:, :], RMS_EPS, None, ALU.add).then_inc(S["ms_ok"], 1)
                dve.wait_ge(S["std_ok"], 1)
                nc.vector.reciprocal(rstd[:, :], rstd[:, :]).then_inc(S["rstd_ok"], 1)
                dve.wait_ge(S["rstd_ok"], 1)
                for k in range(KT):
                    nc.vector.scalar_tensor_tensor(out=hnT[:, k, :], in0=x2T[:, k, :], scalar=col("norm_ffn", k), in1=rstd[:, :],
                                                   op0=ALU.mult, op1=ALU.mult).then_inc(S["hn_ok"], 1)
                dve.wait_ge(S["logit_mm"], 1)
                dve.wait_ge(S["bias_in"], 32)
                v = nc.vector

                def over(ap, shape):
                    return ap.to_broadcast(shape)

                four = [P, TT, EPG]
                step(v.tensor_tensor(logit[:, :, :], bank[5][:, 0:TT * 32].rearrange("p (i c) -> p i c", i=TT)[:, :, 0:NG + NE],
                                     rb[:, :].unsqueeze(1).to_broadcast([P, TT, NG + NE]), ALU.add))

                def first_max(values, m, hot):
                    step(v.reduce_max(m[:, :, :], values, AX.X))
                    step(v.tensor_tensor(t4[:, :, :], values, over(m[:, :, :], four), ALU.is_equal))
                    step(v.tensor_tensor(t4[:, :, :], t4[:, :, :], rank[:, :].unsqueeze(1).to_broadcast(four), ALU.mult))
                    step(v.reduce_max(mx[:, :, :], t4[:, :, :], AX.X))
                    step(v.tensor_tensor(hot[:, :, :], t4[:, :, :], over(mx[:, :, :], four), ALU.is_equal))

                lg = logit[:, :, 0:NG]
                first_max(lg, mg, fg)
                v.tensor_tensor(eg[:, :, :], lg, over(mg[:, :, :], four), ALU.subtract).then_inc(S["exp_in"], 1)
                step(v.tensor_tensor(t44[:, :, :, :], logit[:, :, NG:NG + NE].rearrange("p i (g e) -> p i g e", g=NG),
                                     fg[:, :, :].unsqueeze(3).to_broadcast([P, TT, NG, EPG]), ALU.mult))
                step(v.tensor_tensor(t44[:, :, 0:2, :], t44[:, :, 0:2, :], t44[:, :, 2:4, :], ALU.add))
                step(v.tensor_tensor(el[:, :, :].unsqueeze(2), t44[:, :, 0:1, :], t44[:, :, 1:2, :], ALU.add))
                first_max(el[:, :, :], m1, f1)
                step(v.scalar_tensor_tensor(out=el2[:, :, :], in0=f1[:, :, :], scalar=-3.0e38, in1=el[:, :, :], op0=ALU.mult, op1=ALU.add))
                first_max(el2[:, :, :], m2, f2)
                v.tensor_tensor(e2[:, :, :], m2[:, :, :], m1[:, :, :], ALU.subtract).then_inc(S["exp_in"], 1)
                for n, f in ((0, f1), (1, f2)):
                    step(v.tensor_tensor(one_hot[:, n, :, :].rearrange("p i (g e) -> p i g e", g=NG),
                                         fg[:, :, :].unsqueeze(3).to_broadcast([P, TT, NG, EPG]),
                                         f[:, :, :].unsqueeze(2).to_broadcast([P, TT, NG, EPG]), ALU.mult))
                v.tensor_tensor(chosen[:, :, :], one_hot[:, 0, :, :], one_hot[:, 1, :, :], ALU.add).then_inc(S["chosen_ok"], 1)
                dve.wait_ge(S["exp_ok"], 2)
                step(v.reduce_sum(gs[:, :, :], eg[:, :, :], AX.X))
                step(v.tensor_scalar(den[:, :, :], e2[:, :, :], 1.0, None, ALU.add))
                step(v.tensor_tensor(den[:, :, :], den[:, :, :], gs[:, :, :], ALU.mult))
                step(v.reciprocal(weight[:, :, 0:1], den[:, :, :]))
                step(v.tensor_tensor(weight[:, :, 1:2], weight[:, :, 0:1], e2[:, :, :], ALU.mult))
                dve.wait_ge(S["place_mm"], 1)
                counted = bank[6][:, 0:TT * NE].rearrange("p (i c) -> p i c", i=TT)
                step(v.tensor_tensor(place[:, :, :], counted, base[:, :].unsqueeze(1).to_broadcast([P, TT, NE]), ALU.add))
                for c in range(1, T // SLOTS):
                    step(v.tensor_scalar(t16[:, :, :], counted, float(c * SLOTS), float((NE - 1) * SLOTS), ALU.is_ge, ALU.mult))
                    step(v.tensor_tensor(place[:, :, :], place[:, :, :], t16[:, :, :], ALU.add))
                for n in range(2):
                    step(v.tensor_tensor(t16[:, :, :], place[:, :, :], one_hot[:, n, :, :], ALU.mult))
                    step(v.reduce_sum(rows_f[:, :, n:n + 1], t16[:, :, :], AX.X))
                step(v.tensor_scalar(t16[:, :, :], bank[6][:, 0:TT * NE].rearrange("p (i c) -> p i c", i=TT), float(NE), None, ALU.mult))
                step(v.tensor_tensor(place[:, :, :], t16[:, :, :], expert_no[:, :].unsqueeze(1).to_broadcast([P, TT, NE]), ALU.add))
                for n in range(2):
                    step(v.tensor_tensor(t16[:, :, :], place[:, :, :], one_hot[:, n, :, :], ALU.mult))
                    step(v.reduce_sum(entry_f[:, :, n:n + 1], t16[:, :, :], AX.X))
                step(v.tensor_copy(entry_i[:, :, :], entry_f[:, :, :]))
                step(v.reduce_max(most[:, :], bank[7][:, 0:NE], AX.X))
                step(v.tensor_copy(most_i[:, :], most[:, :]))
                v.tensor_copy(rows_i[:, :, :], rows_f[:, :, :]).then_inc(S["rows_ok"], 1)
                dve.wait_ge(S["rows_ok"], 1)

        with ExitStack() as s:
            a = Area(s)
            toks = a.sb("toks", [P, NE], I32)
            xg = [a.sb(f"xg{u}", [P, D]) for u in range(2)]
            xgT = [a.sb(f"xgT{u}", [P, KT, SLOTS]) for u in range(2)]
            silu = a.sb("silu", [P, DE])
            hid = [a.sb(f"hid{u}", [P, DE // P, SLOTS]) for u in range(2)]
            y = [a.sb(f"y{u}", [P, D]) for u in range(2)]
            names = ("toks_in gate_mm up_mm down_mm xg_T xgT_ok silu_ok hid_ok y_ok").split()
            S = {n: a.sem(n) for n in names}
            xg_in = [a.sem("xg_in0"), a.sem("xg_in1")]
            y_out = [a.sem("y_out0"), a.sem("y_out1")]
            FT = DE // P
            first_pieces = ExitStack()
            block = first_pieces.enter_context(nc.Block())

            @block.sync
            def _(sp):
                sp.dma_start(toks[:, :], tok_scr[0:SLOTS * NE, :].rearrange("(s e) a -> s (e a)", e=NE)).then_inc(S["toks_in"], 16)

                def store(e, u):
                    sp.dma_start(y_scr[bass.ds(e * SLOTS, SLOTS), :], y[u][:, :]).then_inc(y_out[u], 16)

                with sp.Fori(0, NE // 2 - 1) as i:
                    for u in range(2):
                        sp.wait_ge(S["down_mm"], i * 4 + (2 * u + 6))
                        load_weights(sp, i * 2 + (u + 2), u)
                        sp.wait_ge(S["y_ok"], i * 4 + (2 * u + 6))
                        store(i * 2 + u, u)
                for u in range(2):
                    sp.wait_ge(S["y_ok"], 2 * (NE - 2 + u) + 6)
                    store(NE - 2 + u, u)
                for u in range(2):
                    sp.wait_ge(y_out[u], 16 * (NE // 2 + 1))

            @block.gpsimd
            def _(pool):
                pool.wait_ge(S["toks_in"], 16)
                for e in range(NE):
                    if e >= 2:
                        pool.wait_ge(S["xg_T"], 2 * (e - 1))
                    nc.gpsimd.indirect_dma_start(xg[e % 2][:, :], None, hn_scr, bass.IndirectOffsetOnAxis(ap=toks[:, e:e + 1], axis=0)).then_inc(xg_in[e % 2], 16)

            @block.tensor
            def _(pe):
                def transpose_tokens(u, loaded_at, n2):
                    pe.wait_ge(xg_in[u], loaded_at)
                    pe.wait_ge(S["xgT_ok"], n2)
                    for half in range(2):
                        for k in range(4):
                            last = nc.tensor.transpose(bank[2 + half][:, k * P:(k + 1) * P], xg[u][:, (4 * half + k) * P:(4 * half + k + 1) * P], ident[:, :])
                        last.then_inc(S["xg_T"], 1)

                def gate_up(u, loaded_at, n2):
                    pe.wait_ge(gu_in[u], loaded_at)
                    pe.wait_ge(S["xgT_ok"], n2)
                    for b, wt, done in ((0, wg[u], S["gate_mm"]), (1, wu[u], S["up_mm"])):
                        for f in range(FT):
                            for k in range(KT):
                                last = nc.tensor.matmul(bank[b][:, f * SLOTS:(f + 1) * SLOTS], wt[:, k, f * P:(f + 1) * P], xgT[u][:, k, :],
                                                        start=(k == 0), stop=(k == KT - 1))
                        last.then_inc(done, 1)

                def down(u, loaded_at, hid_at, y_at):
                    pe.wait_ge(dn_in[u], loaded_at)
                    pe.wait_ge(S["hid_ok"], hid_at)
                    pe.wait_ge(S["y_ok"], y_at)
                    for half in range(2):
                        for f in range(FT):
                            last = nc.tensor.matmul(bank[4 + 2 * u + half][:, :], hid[u][:, f, :], wdn[u][:, f, half * 512:(half + 1) * 512],
                                                    start=(f == 0), stop=(f == FT - 1))
                        last.then_inc(S["down_mm"], 1)

                pe.sem_inc(S["down_mm"], 4)
                transpose_tokens(0, 16, 2)
                with pe.Fori(0, NE // 2 - 1) as i:
                    for u in range(2):
                        gate_up(u, i * 32 + 32, i * 4 + (2 * u + 4))
                        transpose_tokens(1 - u, i * 16 + 16 * (u + 1), i * 4 + (2 * u + 4))
                        down(u, i * 16 + 16, i * 2 + (u + 2), i * 4 + (2 * u + 2))
                n = NE // 2 - 1
                gate_up(0, 32 * n + 32, 4 * n + 4)
                transpose_tokens(1, 16 * n + 16, 4 * n + 4)
                down(0, 16 * n + 16, 2 * n + 2, 4 * n + 2)
                gate_up(1, 32 * n + 32, 4 * n + 6)
                down(1, 16 * n + 16, 2 * n + 3, 4 * n + 4)

            @block.scalar
            def _(act):
                act.sem_inc(S["xgT_ok"], 2)

                def tokens_copy(u, n2):
                    for half in range(2):
                        act.wait_ge(S["xg_T"], n2 + half + 1)
                        nc.scalar.activation(xgT[u][:, 4 * half:4 * half + 4, :], bank[2 + half][:, :].rearrange("p (k s) -> p k s", k=4), ACT.Copy).then_inc(S["xgT_ok"], 1)

                def gated(e1):
                    act.wait_ge(S["gate_mm"], e1)
                    act.wait_ge(S["hid_ok"], e1)
                    nc.scalar.activation(silu[:, :], bank[0][:, :], ACT.Silu).then_inc(S["silu_ok"], 1)

                tokens_copy(0, 0)
                with act.Fori(0, NE // 2 - 1) as i:
                    for u in range(2):
                        gated(i * 2 + (u + 1))
                        tokens_copy(1 - u, i * 4 + (2 * u + 2))
                gated(NE - 1)
                tokens_copy(1, 2 * NE - 2)
                gated(NE)

            @block.vector
            def _(dve):
                dve.sem_inc(S["hid_ok"], 1)
                dve.sem_inc(S["y_ok"], 4)
                for u in range(2):
                    dve.sem_inc(y_out[u], 16)
                with dve.Fori(0, NE // 2) as i:
                    for u in range(2):
                        dve.wait_ge(S["silu_ok"], i * 2 + (u + 1))
                        dve.wait_ge(S["up_mm"], i * 2 + (u + 1))
                        dve.wait_ge(S["down_mm"], i * 4 + (2 * u + 2))
                        nc.vector.tensor_tensor(hid[u][:, :, :].rearrange("p f s -> p (f s)"), silu[:, :], bank[1][:, :], ALU.mult).then_inc(S["hid_ok"], 1)
                        dve.wait_ge(y_out[u], i * 16 + 16)
                        for half in range(2):
                            dve.wait_ge(S["down_mm"], i * 4 + (2 * u + half + 5))
                            nc.vector.tensor_copy(y[u][:, half * 512:(half + 1) * 512], bank[4 + 2 * u + half][:, :]).then_inc(S["y_ok"], 1)

            first_pieces.close()

            rest = ExitStack()
            r_ = Area(rest)
            tok1 = r_.sb("tok1", [P, 1], I32)
            names = "piece_done w_in tok_in x_in x_T xT_ok gate_mm up_mm silu_ok hid_ok down_mm y_ok y_out".split()
            R = {n: r_.sem(n) for n in names}
            MORE = T // SLOTS - 1
            block = rest.enter_context(nc.Block())

            def overfull(eng):
                return eng.value_load(most_i[0:1, 0:1], min_val=0, max_val=T) > SLOTS

            @block.sync
            def _(sp):
                with sp.If(overfull(sp)):
                    with sp.Fori(0, NE) as e:
                        for dst, src in ((wg[0], w_e_gate), (wu[0], w_e_up), (wdn[0], w_e_down)):
                            sp.dma_start(dst[:, :, :], src[0, bass.ds(e, 1), :, :].rearrange("e (k p) f -> p (e k) f", p=P)).then_inc(R["w_in"], 16)
                        for c in range(MORE):
                            sp.dma_start(tok1[:, :], tok_scr.rearrange("(s e) a -> s (e a)", e=NE)[SLOTS * (c + 1):SLOTS * (c + 2), bass.ds(e, 1)],
                                         allow_slow_non_contiguous=True).then_inc(R["tok_in"], 16)
                            sp.wait_ge(R["y_ok"], e * MORE + (c + 1))
                            sp.dma_start(y_scr[bass.ds(e * SLOTS + NE * SLOTS * (c + 1), SLOTS), :], y[0][:, :]).then_inc(R["y_out"], 16)
                            sp.wait_ge(R["y_out"], e * (16 * MORE) + 16 * (c + 1))
                            sp.sem_inc(R["piece_done"], 1)

            @block.gpsimd
            def _(pool):
                with pool.If(overfull(pool)):
                    with pool.Fori(0, NE) as e:
                        for c in range(MORE):
                            pool.wait_ge(R["tok_in"], e * (16 * MORE) + 16 * (c + 1))
                            pool.sem_inc(S["toks_in"], 1)
                            nc.gpsimd.indirect_dma_start(xg[0][:, :], None, hn_scr, bass.IndirectOffsetOnAxis(ap=tok1[:, 0:1], axis=0)).then_inc(R["x_in"], 16)

            @block.tensor
            def _(pe):
                with pe.If(overfull(pe)):
                    with pe.Fori(0, NE) as e:
                        for c in range(MORE):
                            m = e * MORE + (c + 1)
                            pe.wait_ge(R["x_in"], e * (16 * MORE) + 16 * (c + 1))
                            for k in range(KT):
                                last = nc.tensor.transpose(bank[2 + k // 4][:, (k % 4) * P:(k % 4 + 1) * P], xg[0][:, k * P:(k + 1) * P], ident[:, :])
                            last.then_inc(R["x_T"], 1)
                            pe.wait_ge(R["w_in"], e * 48 + 48)
                            pe.wait_ge(R["xT_ok"], m)
                            for b, wt, done in ((0, wg[0], R["gate_mm"]), (1, wu[0], R["up_mm"])):
                                for f in range(FT):
                                    for k in range(KT):
                                        last = nc.tensor.matmul(bank[b][:, f * SLOTS:(f + 1) * SLOTS], wt[:, k, f * P:(f + 1) * P], xgT[0][:, k, :],
                                                                start=(k == 0), stop=(k == KT - 1))
                                last.then_inc(done, 1)
                            pe.wait_ge(R["hid_ok"], m)
                            for half in range(2):
                                for f in range(FT):
                                    last = nc.tensor.matmul(bank[4 + half][:, :], hid[0][:, f, :], wdn[0][:, f, half * 512:(half + 1) * 512],
                                                            start=(f == 0), stop=(f == FT - 1))
                            last.then_inc(R["down_mm"], 1)

            @block.scalar
            def _(act):
                with act.If(overfull(act)):
                    with act.Fori(0, NE) as e:
                        for c in range(MORE):
                            m = e * MORE + (c + 1)
                            act.wait_ge(R["x_T"], m)
                            nc.scalar.activation(xgT[0][:, 0:4, :], bank[2][:, :].rearrange("p (k s) -> p k s", k=4), ACT.Copy)
                            nc.scalar.activation(xgT[0][:, 4:8, :], bank[3][:, :].rearrange("p (k s) -> p k s", k=4), ACT.Copy).then_inc(R["xT_ok"], 1)
                            act.wait_ge(R["gate_mm"], m)
                            nc.scalar.activation(silu[:, :], bank[0][:, :], ACT.Silu).then_inc(R["silu_ok"], 1)

            @block.vector
            def _(dve):
                with dve.If(overfull(dve)):
                    with dve.Fori(0, NE) as e:
                        for c in range(MORE):
                            m = e * MORE + (c + 1)
                            dve.wait_ge(R["silu_ok"], m)
                            dve.wait_ge(R["up_mm"], m)
                            nc.vector.tensor_tensor(hid[0][:, :, :].rearrange("p f s -> p (f s)"), silu[:, :], bank[1][:, :], ALU.mult).then_inc(R["hid_ok"], 1)
                            dve.wait_ge(R["down_mm"], m)
                            nc.vector.tensor_copy(y[0][:, 0:512], bank[4][:, :])
                            nc.vector.tensor_copy(y[0][:, 512:1024], bank[5][:, :]).then_inc(R["y_ok"], 1)
            rest.close()
        experts.close()

        with ExitStack() as s:
            a = Area(s)
            picked = a.sb("picked", [P, TT, 2, D])
            gf = a.sb("gf", [P, D])
            sqf = a.sb("sqf", [P, TT, D])
            ssq = a.sb("ssq", [P, TT])
            res = a.sb("res", [P, TT, D])
            names = "gf_in added ssq_ok mean_ok std_ok rstd_ok res_ok out_ok".split()
            S = {n: a.sem(n) for n in names}
            picked_in = [a.sem(f"picked_in{i}") for i in range(TT)]
            block = s.enter_context(nc.Block())

            @block.gpsimd
            def _(pool):
                def pick(written):
                    for i in range(TT):
                        for n in range(2):
                            nc.gpsimd.indirect_dma_start(picked[:, i, n, :], None, y_scr[0:written, :], bass.IndirectOffsetOnAxis(ap=rows_i[:, i, n:n + 1], axis=0)).then_inc(picked_in[i], 16)

                with pool.If(pool.value_load(most_i[0:1, 0:1], min_val=0, max_val=T) > SLOTS):
                    pick(NE * T)
                with pool.Else():
                    pick(NE * SLOTS)

            @block.vector
            def _(dve):
                for i in range(TT):
                    dve.wait_ge(picked_in[i], 32)
                    for n in range(2):
                        nc.vector.scalar_tensor_tensor(out=x2_tok[:, i, :], in0=picked[:, i, n, :], scalar=weight[:, i, n:n + 1], in1=x2_tok[:, i, :],
                                                       op0=ALU.mult, op1=ALU.add).then_inc(S["added"], 1)
                        dve.wait_ge(S["added"], 2 * i + n + 1)
                for i in range(TT):
                    dve.wait_ge(S["ssq_ok"], i + 1)
                    nc.vector.tensor_scalar(ssq[:, i:i + 1], ssq[:, i:i + 1], 1.0 / D, RMS_EPS, ALU.mult, ALU.add).then_inc(S["mean_ok"], 1)
                dve.wait_ge(S["gf_in"], 16)
                for i in range(TT):
                    dve.wait_ge(S["std_ok"], i + 1)
                    nc.vector.reciprocal(ssq[:, i:i + 1], ssq[:, i:i + 1]).then_inc(S["rstd_ok"], 1)
                    dve.wait_ge(S["rstd_ok"], i + 1)
                    nc.vector.scalar_tensor_tensor(out=res[:, i, :], in0=x2_tok[:, i, :], scalar=ssq[:, i:i + 1], in1=gf[:, :],
                                                   op0=ALU.mult, op1=ALU.mult).then_inc(S["res_ok"], 1)

            @block.scalar
            def _(act):
                for i in range(TT):
                    act.wait_ge(S["added"], 2 * i + 2)
                    nc.scalar.activation(sqf[:, i, :], x2_tok[:, i, :], ACT.Square, accum_out=ssq[:, i:i + 1]).then_inc(S["ssq_ok"], 1)
                for i in range(TT):
                    act.wait_ge(S["mean_ok"], i + 1)
                    nc.scalar.activation(ssq[:, i:i + 1], ssq[:, i:i + 1], ACT.Sqrt).then_inc(S["std_ok"], 1)

            @block.sync
            def _(sp):
                sp.dma_start(gf[:, :], norm_f.unsqueeze(0).to_broadcast([P, D])).then_inc(S["gf_in"], 16)
                for i in range(TT):
                    sp.wait_ge(S["res_ok"], i + 1)
                    sp.dma_start(out[0, i * P:(i + 1) * P, :], res[:, i, :]).then_inc(S["out_ok"], 16)
                sp.wait_ge(S["out_ok"], 16 * TT)
        nc.clear_and_free_semaphores(Area.sems)
        dense.close()


_INS = ("x mem norm_mix w_in mu_in w0 w_decay_up a0 w_aaa_up w_gate_up k_k k_a r_k lnx_g lnx_b conv_w gate_b w_br_a w_br_b "
        "w_mix_out norm_memq norm_memkv wq_mem wkv_mem wo_mem norm_ffn router_g router_g_b router_e router_e_b w_e_gate "
        "w_e_up w_e_down norm_f").split()


def kernel(**inputs):
    import numpy as _np
    import concourse.bacc as _bacc
    from concourse import mybir as _mybir
    from concourse.bass_utils import run_bass_kernel_spmd as _run

    nc = _bacc.Bacc("TRN2", target_bir_lowering=False, num_devices=1)
    arrays, args = {}, []
    for name in _INS:
        a = _np.ascontiguousarray(inputs[name])
        arrays[f"in_{name}"] = a
        args.append(nc.dram_tensor(f"in_{name}", a.shape, _mybir.dt.from_np(a.dtype), kind="ExternalInput").ap())
    args.append(nc.dram_tensor("out", (1, T, D), F32, kind="ExternalOutput").ap())
    build_trunk(nc, *args)
    r = _run(nc, [arrays], core_ids=[0])
    return r.results[0]["out"]
```
